# Optimizing a Trainium2 kernel written in Bass

```python
import jax, jax.numpy as jnp
from jax import lax
import numpy as np

D_MODEL = 1024
BATCH = 1
SEQ = 512
DEPTH = 2

N_MIXERS = 2
N_A_LAYERS = (DEPTH + 1) // 2
N_B_LAYERS = DEPTH // 2

ATT_HEADS = 16
ATT_KV_HEADS = 4
HEAD_DIM = D_MODEL // ATT_HEADS
GROUP = ATT_HEADS // ATT_KV_HEADS
IDX_HEADS = 8
IDX_DIM = 64
TOPK_MAX = 256
Q_BLOCK = 128
ROPE_THETA = 10000.0
Q_COLS = ATT_HEADS * HEAD_DIM
KV_COLS = ATT_KV_HEADS * HEAD_DIM
IQ_COLS = IDX_HEADS * IDX_DIM
IK_COLS = IDX_DIM
IW_COLS = IDX_HEADS
IN_COLS = Q_COLS + 2 * KV_COLS + IQ_COLS + IK_COLS + IW_COLS

RWKV_HEAD = 64
RWKV_HEADS = D_MODEL // RWKV_HEAD
DECAY_LORA = 64
ICL_LORA = 64
GATE_LORA = 160
LNX_EPS = 64e-5

D_FF = 4 * D_MODEL
NORM_EPS = 1e-6


def rms_norm(x, g):
    xf = x.astype(jnp.float32)
    y = xf * lax.rsqrt(jnp.mean(xf * xf, axis=-1, keepdims=True) + NORM_EPS)
    return (y * g.astype(jnp.float32)).astype(x.dtype)

def rope_tables(length, dim):
    inv = 1.0 / (ROPE_THETA ** (jnp.arange(0, dim, 2, dtype=jnp.float32) / dim))
    ang = jnp.arange(length, dtype=jnp.float32)[:, None] * inv[None, :]
    return jnp.cos(ang), jnp.sin(ang)

def apply_rope(x, cos, sin):
    shape = (1, cos.shape[0]) + (1,) * (x.ndim - 3) + (cos.shape[1],)
    c = cos.reshape(shape)
    s = sin.reshape(shape)
    xf = x.astype(jnp.float32)
    x1, x2 = jnp.split(xf, 2, axis=-1)
    return jnp.concatenate([x1 * c - x2 * s, x2 * c + x1 * s], axis=-1).astype(x.dtype)

def dsa_mixer(h, w_in, w_o):
    B, L, _ = h.shape
    top_k = min(TOPK_MAX, L // 4)
    qb_len = min(Q_BLOCK, L)
    n_blk = L // qb_len
    proj = h @ w_in
    o0 = Q_COLS
    o1 = o0 + KV_COLS
    o2 = o1 + KV_COLS
    o3 = o2 + IQ_COLS
    o4 = o3 + IK_COLS
    q = proj[..., :o0].reshape(B, L, ATT_HEADS, HEAD_DIM)
    k = proj[..., o0:o1].reshape(B, L, ATT_KV_HEADS, HEAD_DIM)
    v = proj[..., o1:o2].reshape(B, L, ATT_KV_HEADS, HEAD_DIM)
    qi = proj[..., o2:o3].reshape(B, L, IDX_HEADS, IDX_DIM)
    ki = proj[..., o3:o4]
    wi = proj[..., o4:] * (IDX_HEADS ** -0.5 * IDX_DIM ** -0.5)
    cos, sin = rope_tables(L, HEAD_DIM)
    q = apply_rope(q, cos, sin)
    k = apply_rope(k, cos, sin)
    cos_i, sin_i = rope_tables(L, IDX_DIM)
    qi = apply_rope(qi, cos_i, sin_i)
    ki = apply_rope(ki, cos_i, sin_i)

    def to_blocks(a):
        return jnp.moveaxis(a.reshape((B, n_blk, qb_len) + a.shape[2:]), 1, 0)

    s_pos = jnp.arange(L, dtype=jnp.int32)

    def block_fn(args):
        q_blk, qi_blk, wi_blk, start = args
        t_pos = start + jnp.arange(qb_len, dtype=jnp.int32)
        rel = jax.nn.relu(jnp.einsum('bthd,bsd->bths', qi_blk, ki).astype(jnp.float32))
        score = jnp.einsum('bths,bth->bts', rel, wi_blk.astype(jnp.float32))
        causal = s_pos[None, :] <= t_pos[:, None]
        score = jnp.where(causal[None], score, -jnp.inf)
        _, sel = lax.top_k(score, top_k)
        valid = sel <= t_pos[None, :, None]
        k_sel = jax.vmap(lambda kb, ib: kb[ib])(k, sel)
        v_sel = jax.vmap(lambda vb, ib: vb[ib])(v, sel)
        qg = q_blk.reshape(B, qb_len, ATT_KV_HEADS, GROUP, HEAD_DIM)
        logits = jnp.einsum('btngd,btknd->btngk', qg, k_sel).astype(jnp.float32) * (HEAD_DIM ** -0.5)
        logits = jnp.where(valid[:, :, None, None, :], logits, -jnp.inf)
        p = jax.nn.softmax(logits, axis=-1).astype(v_sel.dtype)
        o = jnp.einsum('btngk,btknd->btngd', p, v_sel)
        return o.reshape(B, qb_len, ATT_HEADS * HEAD_DIM)

    starts = jnp.arange(n_blk, dtype=jnp.int32) * qb_len
    o = lax.map(block_fn, (to_blocks(q), to_blocks(qi), to_blocks(wi), starts))
    o = jnp.moveaxis(o, 0, 1).reshape(B, L, ATT_HEADS * HEAD_DIM)
    return o @ w_o

def token_shift(x):
    return jnp.pad(x, ((0, 0), (1, 0), (0, 0)))[:, :-1]

def rwkv7_mixer(h, mu, w_rkv, w0, w1, w2, a0, a1, a2, g1, g2, k_k, k_a, r_k, lnx_w, lnx_b, w_o):
    B, L, D = h.shape
    H, N = RWKV_HEADS, RWKV_HEAD
    f32 = jnp.float32
    xx = token_shift(h) - h
    xs = h[None] + xx[None] * mu[:, None, None, :]
    r, k, v = jnp.einsum('cbld,cde->cble', xs[:3], w_rkv)
    xw, xa, xg = xs[3], xs[4], xs[5]
    w_log = -jax.nn.softplus(-(w0 + jnp.tanh(xw @ w1) @ w2).astype(f32)) - 0.5
    decay = jnp.exp(-jnp.exp(w_log))
    a = jax.nn.sigmoid((a0 + (xa @ a1) @ a2).astype(f32))
    g = jax.nn.sigmoid(xg @ g1) @ g2
    kf = k.astype(f32)
    kk = (kf * k_k.astype(f32)).reshape(B, L, H, N)
    kk = kk * lax.rsqrt(jnp.maximum(jnp.sum(kk * kk, axis=-1, keepdims=True), 1e-24))
    kf = kf * (1.0 + (a - 1.0) * k_a.astype(f32))

    def heads(z):
        return z.reshape(B, L, H, N)

    rh, wh, kh, vh, ah = heads(r.astype(f32)), heads(decay), heads(kf), heads(v.astype(f32)), heads(a)
    bh = kk * ah

    def step(state, inp):
        r_t, w_t, k_t, v_t, kk_t, b_t = inp
        sa = jnp.einsum('bhvk,bhk->bhv', state, -kk_t)
        state = (state * w_t[:, :, None, :] + sa[..., None] * b_t[:, :, None, :]
                 + v_t[..., None] * k_t[:, :, None, :])
        y = jnp.einsum('bhvk,bhk->bhv', state, r_t)
        return state, y

    def tm(z):
        return jnp.moveaxis(z, 1, 0)

    state0 = jnp.zeros((B, H, N, N), f32)
    _, y = lax.scan(step, state0, (tm(rh), tm(wh), tm(kh), tm(vh), tm(kk), tm(bh)))
    y = jnp.moveaxis(y, 0, 1)
    mean = jnp.mean(y, axis=-1, keepdims=True)
    var = jnp.mean(jnp.square(y - mean), axis=-1, keepdims=True)
    y = ((y - mean) * lax.rsqrt(var + LNX_EPS) * lnx_w.astype(f32).reshape(H, N)
         + lnx_b.astype(f32).reshape(H, N))
    bonus = jnp.sum(rh * kh * r_k.astype(f32), axis=-1, keepdims=True) * vh
    out = (y + bonus).reshape(B, L, D).astype(h.dtype) * g
    return out @ w_o

def sqrelu_mlp(h, w_up, w_down):
    u = jax.nn.relu(h @ w_up)
    return (u * u) @ w_down

def first_inputs(seed: int = 0) -> dict:
    key = jax.random.key(seed)
    ks = jax.random.split(key, 32)
    D = D_MODEL

    def nrm(k, shape, scale):
        return jax.random.normal(k, shape, jnp.float32) * scale

    nA, nB = N_A_LAYERS, N_B_LAYERS
    return {
        "x": nrm(ks[0], (BATCH, SEQ, D), 1.0),
        "mixer_norm": 1.0 + nrm(ks[1], (DEPTH, D), 0.02),
        "mlp_norm": 1.0 + nrm(ks[2], (DEPTH, D), 0.02),
        "mlp_w_up": nrm(ks[3], (DEPTH, D, D_FF), D ** -0.5),
        "mlp_w_down": nrm(ks[4], (DEPTH, D_FF, D), D_FF ** -0.5),
        "final_norm": 1.0 + nrm(ks[5], (D,), 0.02),
        "dsa_w_in": nrm(ks[6], (nA, D, IN_COLS), D ** -0.5),
        "dsa_w_o": nrm(ks[7], (nA, Q_COLS, D), Q_COLS ** -0.5),
        "rwkv_mu": jax.random.uniform(ks[8], (nB, 6, D), jnp.float32),
        "rwkv_w_rkv": nrm(ks[9], (nB, 3, D, D), D ** -0.5),
        "rwkv_w0": jnp.linspace(-6.0, -1.0, D, dtype=jnp.float32)[None, :] + nrm(ks[10], (nB, D), 0.1),
        "rwkv_w1": nrm(ks[11], (nB, D, DECAY_LORA), D ** -0.5),
        "rwkv_w2": nrm(ks[12], (nB, DECAY_LORA, D), 0.1 * DECAY_LORA ** -0.5),
        "rwkv_a0": nrm(ks[13], (nB, D), 0.1),
        "rwkv_a1": nrm(ks[14], (nB, D, ICL_LORA), D ** -0.5),
        "rwkv_a2": nrm(ks[15], (nB, ICL_LORA, D), 0.1 * ICL_LORA ** -0.5),
        "rwkv_g1": nrm(ks[16], (nB, D, GATE_LORA), D ** -0.5),
        "rwkv_g2": nrm(ks[17], (nB, GATE_LORA, D), GATE_LORA ** -0.5),
        "rwkv_k_k": 0.85 + nrm(ks[18], (nB, D), 0.02),
        "rwkv_k_a": 1.0 + nrm(ks[19], (nB, D), 0.02),
        "rwkv_r_k": -0.04 + nrm(ks[20], (nB, RWKV_HEADS, RWKV_HEAD), 0.02),
        "rwkv_lnx_w": 1.0 + nrm(ks[21], (nB, D), 0.02),
        "rwkv_lnx_b": nrm(ks[22], (nB, D), 0.02),
        "rwkv_w_o": nrm(ks[23], (nB, D, D), D ** -0.5),
    }

def first_block(x, mixer_norm, mlp_norm, mlp_w_up, mlp_w_down, final_norm, dsa_w_in, dsa_w_o,
              rwkv_mu, rwkv_w_rkv, rwkv_w0, rwkv_w1, rwkv_w2, rwkv_a0, rwkv_a1, rwkv_a2,
              rwkv_g1, rwkv_g2, rwkv_k_k, rwkv_k_a, rwkv_r_k, rwkv_lnx_w, rwkv_lnx_b, rwkv_w_o):
    for i in range(DEPTH):
        h = rms_norm(x, mixer_norm[i])
        j = i // N_MIXERS
        if i % N_MIXERS == 0:
            x = x + dsa_mixer(h, dsa_w_in[j], dsa_w_o[j])
        else:
            x = x + rwkv7_mixer(h, rwkv_mu[j], rwkv_w_rkv[j], rwkv_w0[j], rwkv_w1[j], rwkv_w2[j],
                                rwkv_a0[j], rwkv_a1[j], rwkv_a2[j], rwkv_g1[j], rwkv_g2[j],
                                rwkv_k_k[j], rwkv_k_a[j], rwkv_r_k[j], rwkv_lnx_w[j],
                                rwkv_lnx_b[j], rwkv_w_o[j])
        x = x + sqrelu_mlp(rms_norm(x, mlp_norm[i]), mlp_w_up[i], mlp_w_down[i])
    return rms_norm(x, final_norm)


DEPTH_2 = 1

EPS = 1e-6
D_FF_2 = 2816
FFN_RES_WEIGHT = 0.5
CONV_DIM = D_MODEL
CONV_K = 3
GLA_HEADS = 4
GLA_DK = D_MODEL // 2 // GLA_HEADS
GLA_DV = D_MODEL // GLA_HEADS
GLA_QK = GLA_HEADS * GLA_DK
GLA_V = GLA_HEADS * GLA_DV
GATE_RANK = 16
GATE_TAU = 16.0
CHUNK = 64
IN_SIZES = (CONV_DIM, CONV_DIM, CONV_DIM, GLA_QK, GLA_QK, GLA_V, GATE_RANK, GLA_V, D_MODEL, D_MODEL)
IN_COLS_2 = sum(IN_SIZES)
SPLIT_POINTS = tuple(int(s) for s in np.cumsum(IN_SIZES)[:-1])


def rmsnorm(x, g):
    xf = x.astype(jnp.float32)
    y = xf * lax.rsqrt(jnp.mean(xf * xf, axis=-1, keepdims=True) + EPS)
    return (y * g.astype(jnp.float32)).astype(x.dtype)

def swiglu(x, w_gu, w_down):
    g, u = jnp.split(x @ w_gu, 2, axis=-1)
    return (jax.nn.silu(g) * u) @ w_down

def causal_short_conv(u, w):
    S = u.shape[1]
    up = jnp.pad(u, ((0, 0), (CONV_K - 1, 0), (0, 0)))
    out = up[:, 0:S] * w[0]
    for j in range(1, CONV_K):
        out = out + up[:, j:j + S] * w[j]
    return out

def gla_chunked(q, k, v, log_a):
    B, S = q.shape[0], q.shape[1]
    N = S // CHUNK
    f32 = jnp.float32

    def to_chunks(t):
        return t.reshape(B, N, CHUNK, GLA_HEADS, t.shape[-1]).transpose(0, 3, 1, 2, 4).astype(f32)

    qc = to_chunks(q) * (GLA_DK ** -0.5)
    kc, vc, gc = to_chunks(k), to_chunks(v), to_chunks(log_a)
    b = jnp.cumsum(gc, axis=3)
    b_last = b[:, :, :, -1:]
    b_ref = b[:, :, :, CHUNK // 2 - 1:CHUNK // 2]

    q_ref = qc * jnp.exp(b - b_ref)
    k_ref = kc * jnp.exp(b_ref - b)
    scores = jnp.einsum('bhnid,bhnjd->bhnij', q_ref, k_ref)
    causal = jnp.tril(jnp.ones((CHUNK, CHUNK), dtype=bool))
    scores = jnp.where(causal, scores, 0.0)
    o_intra = jnp.einsum('bhnij,bhnjv->bhniv', scores, vc)

    q_inter = q_ref * jnp.exp(b_ref)
    k_state = kc * jnp.exp(b_last - b)
    kv = jnp.einsum('bhncd,bhncv->nbhdv', k_state, vc)
    decay = jnp.exp(b_last[:, :, :, 0]).transpose(2, 0, 1, 3)

    def step(state, inp):
        dec, kv_n = inp
        return state * dec[..., None] + kv_n, state

    init = jnp.zeros((B, GLA_HEADS, GLA_DK, GLA_DV), f32)
    _, states = lax.scan(step, init, (decay, kv))
    o_inter = jnp.einsum('bhncd,nbhdv->bhncv', q_inter, states)
    o = o_intra + o_inter
    return o.transpose(0, 2, 3, 1, 4).reshape(B, S, GLA_HEADS, GLA_DV)

def hybrid_mixer(h, w_in, conv_w, gate_w_up, gate_b, gla_norm_g, w_out_conv, w_out_gla, w_o):
    B, S, _ = h.shape
    z = h @ w_in
    cb, cc, cu, q, k, v, g_lr, r, ga, gb = jnp.split(z, SPLIT_POINTS, axis=-1)

    y_conv = (cb * causal_short_conv(cc * cu, conv_w)) @ w_out_conv

    log_a = jax.nn.log_sigmoid((g_lr @ gate_w_up + gate_b).astype(jnp.float32)) / GATE_TAU
    o = gla_chunked(q.reshape(B, S, GLA_HEADS, GLA_DK),
                    k.reshape(B, S, GLA_HEADS, GLA_DK),
                    v.reshape(B, S, GLA_HEADS, GLA_DV),
                    log_a.reshape(B, S, GLA_HEADS, GLA_DK))
    o = o * lax.rsqrt(jnp.mean(o * o, axis=-1, keepdims=True) + EPS)
    o = o.reshape(B, S, GLA_V) * gla_norm_g.astype(jnp.float32)
    y_gla = (o.astype(h.dtype) * jax.nn.silu(r)) @ w_out_gla

    merged = jax.nn.sigmoid(ga) * y_conv + jax.nn.sigmoid(gb) * y_gla
    return merged @ w_o

def second_inputs(seed: int = 0) -> dict:
    key = jax.random.key(seed)
    ks = jax.random.split(key, 20)
    f32 = jnp.float32

    def nrm(k, shape, fan_in):
        return jax.random.normal(k, shape, f32) * (fan_in ** -0.5)

    def gain(k, shape):
        return 1.0 + 0.02 * jax.random.normal(k, shape, f32)

    L = DEPTH_2
    return {
        'x': jax.random.normal(ks[0], (BATCH, SEQ, D_MODEL), f32),
        'norm_ffn1_g': gain(ks[1], (L, D_MODEL)),
        'ffn1_w_gu': nrm(ks[2], (L, D_MODEL, 2 * D_FF_2), D_MODEL),
        'ffn1_w_down': nrm(ks[3], (L, D_FF_2, D_MODEL), D_FF_2),
        'norm_mix_g': gain(ks[4], (L, D_MODEL)),
        'w_in': nrm(ks[5], (L, D_MODEL, IN_COLS_2), D_MODEL),
        'conv_w': nrm(ks[6], (L, CONV_K, CONV_DIM), CONV_K),
        'gate_w_up': nrm(ks[7], (L, GATE_RANK, GLA_QK), GATE_RANK),
        'gate_b': 0.1 * jax.random.normal(ks[8], (L, GLA_QK), f32),
        'gla_norm_g': gain(ks[9], (L, GLA_V)),
        'w_out_conv': nrm(ks[10], (L, CONV_DIM, D_MODEL), CONV_DIM),
        'w_out_gla': nrm(ks[11], (L, GLA_V, D_MODEL), GLA_V),
        'w_o': nrm(ks[12], (L, D_MODEL, D_MODEL), D_MODEL),
        'norm_ffn2_g': gain(ks[13], (L, D_MODEL)),
        'ffn2_w_gu': nrm(ks[14], (L, D_MODEL, 2 * D_FF_2), D_MODEL),
        'ffn2_w_down': nrm(ks[15], (L, D_FF_2, D_MODEL), D_FF_2),
        'final_norm_g': gain(ks[16], (D_MODEL,)),
    }

def second_block(x, norm_ffn1_g, ffn1_w_gu, ffn1_w_down, norm_mix_g, w_in, conv_w, gate_w_up, gate_b,
              gla_norm_g, w_out_conv, w_out_gla, w_o, norm_ffn2_g, ffn2_w_gu, ffn2_w_down, final_norm_g):
    for l in range(DEPTH_2):
        x = x + FFN_RES_WEIGHT * swiglu(rmsnorm(x, norm_ffn1_g[l]), ffn1_w_gu[l], ffn1_w_down[l])
        x = x + hybrid_mixer(rmsnorm(x, norm_mix_g[l]), w_in[l], conv_w[l], gate_w_up[l], gate_b[l],
                             gla_norm_g[l], w_out_conv[l], w_out_gla[l], w_o[l])
        x = x + FFN_RES_WEIGHT * swiglu(rmsnorm(x, norm_ffn2_g[l]), ffn2_w_gu[l], ffn2_w_down[l])
    return rmsnorm(x, final_norm_g)


def setup_inputs(seed=0):
    out = dict(first_inputs(seed))
    for name, value in second_inputs(seed + 1).items():
        if name != "x":
            out[name + "_2"] = value
    return out


def reference(
    x, mixer_norm, mlp_norm, mlp_w_up, mlp_w_down, final_norm, dsa_w_in, dsa_w_o, rwkv_mu,
    rwkv_w_rkv, rwkv_w0, rwkv_w1, rwkv_w2, rwkv_a0, rwkv_a1, rwkv_a2, rwkv_g1, rwkv_g2,
    rwkv_k_k, rwkv_k_a, rwkv_r_k, rwkv_lnx_w, rwkv_lnx_b, rwkv_w_o, norm_ffn1_g_2, ffn1_w_gu_2,
    ffn1_w_down_2, norm_mix_g_2, w_in_2, conv_w_2, gate_w_up_2, gate_b_2, gla_norm_g_2,
    w_out_conv_2, w_out_gla_2, w_o_2, norm_ffn2_g_2, ffn2_w_gu_2, ffn2_w_down_2, final_norm_g_2,
):
    x = first_block(
        x, mixer_norm, mlp_norm, mlp_w_up, mlp_w_down, final_norm, dsa_w_in, dsa_w_o, rwkv_mu,
        rwkv_w_rkv, rwkv_w0, rwkv_w1, rwkv_w2, rwkv_a0, rwkv_a1, rwkv_a2, rwkv_g1, rwkv_g2,
        rwkv_k_k, rwkv_k_a, rwkv_r_k, rwkv_lnx_w, rwkv_lnx_b, rwkv_w_o,
    )
    return second_block(
        x, norm_ffn1_g_2, ffn1_w_gu_2, ffn1_w_down_2, norm_mix_g_2, w_in_2, conv_w_2,
        gate_w_up_2, gate_b_2, gla_norm_g_2, w_out_conv_2, w_out_gla_2, w_o_2, norm_ffn2_g_2,
        ffn2_w_gu_2, ffn2_w_down_2, final_norm_g_2,
    )


_drawn_inputs = setup_inputs


def setup_inputs(seed=0):
    import zlib

    import numpy as np

    out = dict(_drawn_inputs(seed))
    spreads = {}
    factors = {'rwkv_w1': 8.0,
     'rwkv_w2': 8.0,
     'rwkv_a1': 2.861,
     'rwkv_a2': 2.946,
     'rwkv_k_k': 3.187,
     'rwkv_k_a': 3.209,
     'rwkv_r_k': 2.749,
     'rwkv_lnx_w': 5.834,
     'rwkv_lnx_b': 5.689,
     'norm_ffn1_g_2': 5.168,
     'norm_mix_g_2': 2.869,
     'gate_b_2': 3.333,
     'gla_norm_g_2': 94.091,
     'norm_ffn2_g_2': 35.304,
     'final_norm_g_2': 20.28}
    for name, (base, spread) in spreads.items():
        noise = np.random.default_rng([zlib.crc32(name.encode()), seed]).standard_normal(out[name].shape)
        drawn = base * np.exp(spread * noise) if base else spread * noise
        out[name] = __import__('jax').numpy.asarray(drawn.astype(out[name].dtype))
    for name, factor in factors.items():
        out[name] = (out[name] * factor).astype(out[name].dtype)
    return out
```

```python
from contextlib import ExitStack

import numpy as np

import concourse.bass as bass
from concourse import mybir

F32 = mybir.dt.float32
F32R = mybir.dt.float32r
I32 = mybir.dt.int32
ALU = mybir.AluOpType
ACT = mybir.ActivationFunctionType
AX = mybir.AxisListType

P = 128
T = 512
D = 1024
KT = D // P
NT = T // P
UNIT = 1024
SPLITS = 4
PAIRS = 2
AHEAD = 3

N_DSA_IN = 18
N_PROJ = 8
N_MLP = 64
N_RWKV_IN = 28
FFN_CHUNKS = (8, 8, 6)
N_FFN = sum(2 * c + 8 for c in FFN_CHUNKS)
N_MIX_IN = 24 + 24 + 2 + 8 + 8 + 8

U_DSA = 0
U_DSA_O = U_DSA + N_DSA_IN
U_MLP0 = U_DSA_O + N_PROJ
U_RWKV = U_MLP0 + N_MLP
U_RWKV_O = U_RWKV + N_RWKV_IN
U_MLP1 = U_RWKV_O + N_PROJ
U_FFN1 = U_MLP1 + N_MLP
U_MIX = U_FFN1 + N_FFN
U_GLA_O = U_MIX + N_MIX_IN
U_MIX_O = U_GLA_O + N_PROJ
U_FFN2 = U_MIX_O + N_PROJ
U_END = U_FFN2 + N_FFN

F_DSA, F_DSA_O = 0, 17
F_MLP0 = F_DSA_O + 8
F_RWKV = F_MLP0 + 64
F_RWKV_O = F_RWKV + 4
F_MLP1 = F_RWKV_O + 8
F_FFN1 = F_MLP1 + 64
F_MIX = F_FFN1 + N_FFN
F_GLA_O = F_MIX + 24 + 1 + 24
F_MIX_O = F_GLA_O + 8
F_FFN2 = F_MIX_O + 8

(V_MIX0, V_MIX1, V_MLP0, V_MLP1, V_FINAL, V_FFN1, V_MIXG, V_FFN2, V_OUT) = range(9)
V_MU, V_CONV, N_VEC = 9, 15, 18

LEVELS = (1, 2, 4, 8, 16, 32)
CHUNK = 64
EPS = 1e-6
LNX_EPS = 64e-5
NEG = -1.0e30
SCORE_OUT = -3.0e38
SCORE_TAKEN = -3.4e38
TOPK = 128
E_HALF = float(np.exp(-0.5))


class Tally:

    def __init__(self, eng, sem):
        self.eng, self.sem, self.n, self.reg = eng, sem, 0, 0

    def mark(self, inst):
        inst.then_inc(self.sem, 1)
        self.n += 1
        return self.n + self.reg

    def wait(self, label=None):
        self.eng.wait_ge(self.sem, self.n + self.reg if label is None else label)

    def loop(self, trips, per):
        return _TallyLoop(self, trips, per)


class _TallyLoop:
    def __init__(self, tally, trips, per):
        self.t, self.trips, self.per = tally, trips, per

    def __enter__(self):
        self.n0, self.reg0 = self.t.n, self.t.reg
        return self

    def at(self, i):
        self.t.reg = self.reg0 + i * self.per

    def __exit__(self, kind, *rest):
        if kind is None:
            assert self.t.n - self.n0 == self.per, ("marks in the loop's body", self.t.n - self.n0)
            self.t.n, self.t.reg = self.n0 + self.per * self.trips, self.reg0


def bcast(ap, n, inner):
    return ap.rearrange("p (o i) -> p o i", o=1).to_broadcast([ap.shape[0], n, inner])


def over(ap, inner):
    return ap.rearrange("p (n o) -> p n o", o=1).to_broadcast([ap.shape[0], ap.shape[1], inner])


class Steps:

    def __init__(self, *names):
        self.names = [n for group in names for n in group.split()]

    def value(self, name, rnd):
        return self.names.index(name) + 1 + rnd * len(self.names)


PE_CORE = Steps("decay chunk_decay turn_ar turn_bk m1 m2 a bv",
                " ".join(f"w{v} tw{v} wt{v}" if v < 5 else f"w{v} wt{v}" for v in range(1, 6)),
                "u0 ta", "u_c0 y_c0 s_c0 u_c1 y_c1 s_c1", "yh turn_o")
ACT_CORE = Steps("ex_in ex_before ex_neg pc ar bk bv", " ".join(f"w{v}" for v in range(1, 6)), "ta yh0 yh1 o_hi")
DVE_CORE = Steps("kkr sq ss ssm t kf rkf rkr bs kk b al rho be ka m1_0 m1_1 m2_0 m2_1 t0_0 t0_1 tt0_0 tt0_1",
                 " ".join(f"t{v} tt{v}" if v < 5 else f"tt{v}" for v in range(1, 6)),
                 "u0_0 u0_1 u_c0 sx_c0 s0_c0 s1_c0 u_c1 sx_c1 s0_c1 s1_c1",
                 "y sm mean yc ysq vs ve yn yw yb bonus yv o o_lo")
POOL_CORE = Steps("eye_t eye_tt rn ri")

(KKR, SQ, KK, TA, KF, BB, AL, BE, KA, RHO, RKF, YY, YC, OUT, BON) = range(15)
(H_SS, H_SSM, H_RN, H_BS, H_SM, H_MEAN, H_VS, H_VE, H_RI, H_HALF) = range(10)

PE_GLA = Steps("decay turn scores kv0 kv1 o0 o1 turn_o")
ACT_GLA = Steps("ex ex_neg chunk gT osq o_hi")
DVE_GLA = Steps("qr kr qi ks mask st0 st1 mean on out o_lo")
POOL_GLA = Steps("ri")
GLA_SCALE = 128 ** -0.5
F_GATES = F_MIX + 25
H_MLP0, H_MLP1, H_FFN1, H_CONV, H_MERGED, H_FFN2 = 0, 32, 64, 86, 94, 102


def build(nc, io, out):
    with ExitStack() as ctx:
        def sb(name, shape, dt=F32, at=ctx):
            return at.enter_context(nc.sbuf_tensor(name, shape, dt))

        def sem(name):
            return ctx.enter_context(nc.semaphore(name))

        x = sb("x_res", [P, KT, T])
        gate = sb("gate", [P, 15])
        raw = sb("raw", [P, PAIRS, 2 * UNIT])
        w_hi = sb("w_hi", [P, SPLITS, UNIT], F32R)
        w_lo = sb("w_lo", [P, SPLITS, UNIT], F32R)
        a_hi = sb("a_hi", [P, KT, T], F32R)
        a_lo = sb("a_lo", [P, KT, T], F32R)
        rstd = sb("rstd", [P, T])
        h32 = sb("h32", [P, 3, T])
        ep = sb("ep", [P, 4, T])
        vec = sb("vec", [P, N_VEC, KT])
        ident = sb("ident", [P, P])
        ones = sb("ones", [P, P])
        tri = sb("tri", [P, 6, P])
        strict_incl = sb("strict_incl", [P, 2, P])
        chunk_sum = sb("chunk_sum", [P, 2, 2])
        imask = sb("imask", [P, 14, P], I32)
        pair_mask = sb("pair_mask", [P, P])

        with ExitStack() as attn:
            cos = sb("cos", [P, T], at=attn)
            sin = sb("sin", [P, T], at=attn)
            qT = sb("qT", [P, 8, T], at=attn)
            kd = sb("kd", [P, 4, T], at=attn)
            vT = sb("vT", [P, 2, T], at=attn)
            v_tm = sb("v_tm", [P, NT, 256], at=attn)
            qiT = sb("qiT", [P, 4, T], at=attn)
            kiwi = sb("kiwi", [P, T], at=attn)
            kid = sb("kid", [P, T], at=attn)
            wi = sb("wi", [P, NT, 8], at=attn)
            swap = sb("swap", [P, 2, T], at=attn)
            rope1 = sb("rope1", [P, T], at=attn)
            score = sb("score", [P, T], at=attn)
            top8 = sb("top8", [P, 8], at=attn)
            fill = sb("fill", [P, P], at=attn)
            causal = sb("causal", [P, P], at=attn)
            amask = sb("amask", [P, NT, T], at=attn)
            prob = sb("prob", [P, 3, T], at=attn)
            probT = sb("probT", [P, 2, T], at=attn)
            stat = sb("stat", [P, 4, 64], at=attn)
        with ExitStack() as gla:
            gin = sb("gin", [P, 2, 896], at=gla)
            gex = sb("gex", [P, 4, P], at=gla)
            gdc = sb("gdc", [P, 2], at=gla)
            gqk = sb("gqk", [P, 4, P], at=gla)
            gT = sb("gT", [P, 3, P], at=gla)
            scT = sb("scT", [P, P], at=gla)
            St = sb("St", [P, 256], at=gla)
            gsq = sb("gsq", [P, 256], at=gla)
            gst = sb("gst", [P, 4], at=gla)
            on = sb("on", [P, 256], at=gla)
            gout = sb("gout", [P, 256], at=gla)
            gla_g = sb("gla_g", [P, D], at=gla)
        u_scope = ExitStack()
        u_hi = sb("u_hi", [P, KT, T], F32R, at=u_scope)
        u_lo = sb("u_lo", [P, KT, T], F32R, at=u_scope)
        with ExitStack() as shift:
            h_pad = sb("h_pad", [P, KT, T + 2], at=shift)
            mu1 = sb("mu1", [P, 6, KT], at=shift)
            lora = sb("lora", [P, 4, T], at=shift)
            lora2 = sb("lora2", [P, 4, D], at=shift)
        with ExitStack() as conv:
            uc = sb("uc", [P, 2, T + 2], at=conv)
            uc2 = sb("uc2", [P, 2, T], at=conv)
            merged = sb("merged", [P, KT, T], at=conv)
            sig_b = sb("sig_b", [P, KT, T], at=conv)
            glr = sb("glr", [P, T], at=conv)
            gate_up = sb("gate_up", [P, 512], at=conv)
        u_scope.close()
        with ExitStack() as core:
            rin = sb("rin", [P, 2, 6, 256], at=core)
            prm = sb("prm", [P, 5, D], at=core)
            rt = sb("rt", [P, 16, 256], at=core)
            ex = sb("ex", [P, 3, 256], at=core)
            hst = sb("hst", [P, 10, 4], at=core)
            pc = sb("pc", [P, 2, 2], at=core)
            arT = sb("arT", [P, 2, 2, P], at=core)
            bkT = sb("bkT", [P, 2, 2, P], at=core)
            m1 = sb("m1", [P, 2, 2, 2, P], at=core)
            m2 = sb("m2", [P, 2, 2, 2, P], at=core)
            Tm = sb("Tm", [P, 2, 2, P], at=core)
            TT = sb("TT", [P, 2, 2, P], at=core)
            Wm = sb("Wm", [P, 4, P], at=core)
            bv = sb("bv", [P, 4, P], at=core)
            u0 = sb("u0", [P, 2, 2, 64], at=core)
            taT = sb("taT", [P, 2, P], at=core)
            U = sb("U", [P, 2, P], at=core)
            S = sb("S", [P, 2, P], at=core)
            yh = sb("yh", [P, 2, 2, 64], at=core)
        ps = ctx.enter_context(nc.psum_tensor("ps", [P, 8, T], F32))

        rk_dram = nc.dram_tensor("rwkv_scratch", (4, NT, P, 6, 256), F32).ap()

        gla_dram = nc.dram_tensor("gla_scratch", (4, NT, P, 896), F32).ap()

        raw_in = [sem("raw_in0"), sem("raw_in1")]
        hi_ready = sem("hi_ready")
        split_ready = sem("split_ready")
        unit_done = sem("unit_done")
        bank_free = sem("bank_free")
        tm_free = sem("tm_free")
        const_in = sem("const_in")
        x_in = sem("x_in")
        squared = sem("squared")
        summed = sem("summed")
        rooted = sem("rooted")
        normed = sem("normed")
        a_hi_ready = sem("a_hi_ready")
        a_ready = sem("a_ready")
        ep_act = sem("ep_act")
        ep_dve = sem("ep_dve")
        u_hi_ready = sem("u_hi_ready")
        u_ready = sem("u_ready")
        dve_chain = sem("dve_chain")
        act_chain = sem("act_chain")
        pool_chain = sem("pool_chain")
        pe_step = sem("pe_step")
        act_step = sem("act_step")
        dve_step = sem("dve_step")
        pool_step = sem("pool_step")
        spilled = sem("spilled")
        rin_in = [sem("rin_in0"), sem("rin_in1")]
        prm_in = sem("prm_in")
        swap_ready = sem("swap_ready")
        roped = sem("roped")
        kiwi_ready = sem("kiwi_ready")
        vt_ps = sem("vt_ps")
        v_read = sem("v_read")
        wi_read = sem("wi_read")
        idx_ps = sem("idx_ps")
        idx_relu = sem("idx_relu")
        idx_added = sem("idx_added")
        lg_ps = sem("lg_ps")
        lg_read = sem("lg_read")
        lg_bias = sem("lg_bias")
        exp_ready = sem("exp_ready")
        prob_ready = sem("prob_ready")
        tr_ps = sem("tr_ps")
        probT_ready = sem("probT_ready")
        o_ps = sem("o_ps")
        o_hi = sem("o_hi")
        o_ready = sem("o_ready")
        out_done = sem("out_done")
        late_in = sem("late_in")
        xs32 = sem("xs32")
        xs_hi = sem("xs_hi")
        xs_ready = sem("xs_ready")
        lora_in = sem("lora_in")
        lora_act = sem("lora_act")
        lora_ready = sem("lora_ready")
        lora_ps = sem("lora_ps")
        lora_read = sem("lora_read")
        spill = [sem(f"spill{i}") for i in range(4)]
        pe_core, act_core, dve_core, pool_core = (sem(n) for n in ("pe_core", "act_core", "dve_core", "pool_core"))
        state_zero = sem("state_zero")
        x_scaled = sem("x_scaled")
        gated = sem("gated")
        silu_ready = sem("silu_ready")
        la_act = sem("la_act")
        la_ps = sem("la_ps")
        la_ready = sem("la_ready")
        gate_in = sem("gate_in")
        gla_in = sem("gla_in")
        gin_in = [sem("gin_in0"), sem("gin_in1")]
        st_zero = sem("st_zero")
        pe_gla, act_gla, dve_gla, pool_gla = (sem(n) for n in ("pe_gla", "act_gla", "dve_gla", "pool_gla"))
        merged_ready = sem("merged_ready")
        pool_gla_const = sem("pool_gla_const")
        block = ctx.enter_context(nc.Block())

        @block.sync
        def _(sp):
            for dst, name in ((x, "x"), (vec, "vec"), (ident, "ident"), (ones, "ones"), (tri, "tri"),
                              (strict_incl, "strict_incl"), (chunk_sum, "chunk_sum"), (imask, "imask"),
                              (pair_mask, "pair_mask"), (cos, "cos"), (sin, "sin"), (causal, "causal"),
                              (fill, "fill")):
                sp.dma_start(dst[:], io[name]).then_inc(x_in, 16)
            pairs = U_END // 2
            for s in range(PAIRS):
                sp.dma_start(raw[:, s], io["weights"][s]).then_inc(raw_in[s], 16)
            with sp.Fori(1, pairs // PAIRS) as i:
                for s in range(PAIRS):
                    sp.wait_ge(split_ready, 2 * PAIRS * i + 2 * s - 2 * PAIRS + 2)
                    sp.dma_start(raw[:, s], io["weights"][bass.ds(PAIRS * i + s, 1)].rearrange("o p n -> p (o n)"))\
                        .then_inc(raw_in[s], 16)
            for k in range(KT):
                sp.wait_ge(x_scaled, KT + k + 1)
                sp.dma_start(out[:, k], x[:, k]).then_inc(out_done, 16)
            sp.wait_ge(out_done, 16 * KT)

        @block.tensor
        def _(pe):
            def fm_unit(m, f, hi, lo, off=0, foff=0, k0=0, nk=KT, first=True, last=True, ready=None):
                bank = ps[:, f % 4]
                pe.wait_ge(split_ready, m + 1 + off)
                if first and f >= 4:
                    pe.wait_ge(bank_free, f - 3 + foff)
                for k in range(nk):
                    if ready is not None:
                        pe.wait_ge(ready[0], ready[1] + k + 1 + ready[2])
                    wh = w_hi[:, m % SPLITS, k * P:(k + 1) * P]
                    wl = w_lo[:, m % SPLITS, k * P:(k + 1) * P]
                    nc.tensor.matmul(bank, wh, hi[:, k0 + k], start=first and k == 0, stop=False)
                    nc.tensor.matmul(bank, wh, lo[:, k0 + k], start=False, stop=False)
                    mm = nc.tensor.matmul(bank, wl, hi[:, k0 + k], start=False, stop=last and k == nk - 1)
                mm.then_inc(unit_done, 1)

            def tm_unit(m, g, hi, lo, q, ready=None):
                pe.wait_ge(split_ready, m + 1)
                for k in (2 * q, 2 * q + 1):
                    if ready is not None:
                        pe.wait_ge(ready[0], ready[1] + k + 1)
                    wk = slice((k % 2) * T, (k % 2 + 1) * T)
                    for t in range(NT):
                        if k == 0 and g >= 2:
                            pe.wait_ge(tm_free, 4 * (g - 2) + t + 1)
                        bank = ps[:, 4 * (g % 2) + t]
                        at = slice(t * P, (t + 1) * P)
                        nc.tensor.matmul(bank, hi[:, k, at], w_hi[:, m % SPLITS, wk], start=k == 0, stop=False)
                        nc.tensor.matmul(bank, hi[:, k, at], w_lo[:, m % SPLITS, wk], start=False, stop=False)
                        mm = nc.tensor.matmul(bank, lo[:, k, at], w_hi[:, m % SPLITS, wk], start=False, stop=k == KT - 1)
                mm.then_inc(unit_done, 1)

            def norm_sum(n):
                for k in range(KT):
                    pe.wait_ge(squared, KT * n + k + 1)
                    nc.tensor.matmul(ps[:, 7], ones[:], ep[:, k % 4], start=k == 0, stop=k == KT - 1)\
                        .then_inc(summed, 1)

            def proj(u, f, ready, hi=a_hi, lo=a_lo):
                for j in range(N_PROJ):
                    fm_unit(u + j, f + j, hi, lo, ready=ready if j == 0 else None)

            def mlp(u, f, h, n):
                with pe.Fori(0, 4) as i:
                    off, hoff = 16 * i, 8 * i
                    for j in range(8):
                        fm_unit(u + j, f + j, a_hi, a_lo, off, off,
                                ready=(a_ready, KT * n, 0) if j == 0 else None)
                    for j in range(8):
                        fm_unit(u + 8 + j, f + 8 + j, u_hi, u_lo, off, off,
                                ready=(u_ready, h, hoff) if j == 0 else None)

            def ffn(u, f, h, n):
                def chunk(size, u, f, h, off, hoff, first):
                    for j in range(2 * size):
                        fm_unit(u + j, f + j, a_hi, a_lo, off, off,
                                ready=(a_ready, KT * n, 0) if j == 0 and first else None)
                    for j in range(8):
                        fm_unit(u + 2 * size + j, f + 2 * size + j, u_hi, u_lo, off, off, nk=size,
                                ready=(u_ready, h, hoff) if j == 0 else None)

                with pe.Fori(0, 2) as i:
                    chunk(8, u, f, h, 24 * i, 8 * i, True)
                chunk(6, u + 48, f + 48, h + 16, 0, 0, False)

            pe.wait_ge(x_in, 16 * 13)
            norm_sum(0)
            for j in range(16):
                fm_unit(U_DSA + j, F_DSA + j, a_hi, a_lo, ready=(a_ready, 0, 0) if j == 0 else None)
            fm_unit(U_DSA + 16, F_DSA + 16, a_hi, a_lo, nk=4, last=False)
            fm_unit(U_DSA + 17, F_DSA + 16, a_hi, a_lo, nk=4, k0=4, first=False)
            pe.wait_ge(bank_free, 12)
            for t in range(NT):
                for j in range(2):
                    tr = nc.tensor.transpose(ps[:, 4 + t // 2, (t % 2) * 256 + j * P:(t % 2) * 256 + (j + 1) * P],
                                             vT[:, j, t * P:(t + 1) * P], ident[:])
            tr.then_inc(vt_ps, 1)
            pe.wait_ge(kiwi_ready, 1)
            for t in range(NT):
                tr = nc.tensor.transpose(ps[:, 6, t * P:t * P + 72], kiwi[0:72, t * P:(t + 1) * P], ident[0:72, 0:72])
            tr.then_inc(vt_ps, 1)
            pe.wait_ge(roped, 16)
            pe.wait_ge(v_read, 2)
            pe.wait_ge(wi_read, 1)
            for i in range(24):
                qb, h = 1 + i // 8, i % 8
                n, e = (qb + 1) * P, 64 * (h % 2)
                if i >= 2:
                    pe.wait_ge(idx_relu, i - 1)
                nc.tensor.matmul(ps[:, 4 + i % 2, 0:n], qiT[e:e + 64, h // 2, qb * P:(qb + 1) * P],
                                 kid[e:e + 64, 0:n], start=True, stop=True).then_inc(idx_ps, 1)
            pe.wait_ge(idx_relu, 24)

            def logits(n):
                qb, h = n // 16, n % 16
                e = 64 * (h % 2)
                if n >= 2:
                    pe.wait_ge(lg_read, n - 1)
                nc.tensor.matmul(ps[:, 4 + n % 2, 0:(qb + 1) * P], qT[e:e + 64, h // 2, qb * P:(qb + 1) * P],
                                 kd[e:e + 64, h // 4, 0:(qb + 1) * P], start=True, stop=True).then_inc(lg_ps, 1)

            def turn(n):
                pe.wait_ge(prob_ready, n + 1)
                if n >= 2:
                    pe.wait_ge(probT_ready, n - 1)
                for b in range(n // 16 + 1):
                    tr = nc.tensor.transpose(ps[:, 6 + n % 2, b * P:(b + 1) * P], prob[:, n % 3, b * P:(b + 1) * P], ident[:])
                tr.then_inc(tr_ps, 1)

            def weigh(n):
                qb, h = n // 16, n % 16
                e = 64 * (h % 2)
                pe.wait_ge(probT_ready, n + 1)
                if n % 8 == 0 and n >= 16:
                    pe.wait_ge(o_ready, n // 8 - 1)
                o = ps[e:e + 64, (n // 8) % 2, (h % 8 // 2) * P:(h % 8 // 2 + 1) * P]
                for b in range(qb + 1):
                    mm = nc.tensor.matmul(o, v_tm[:, b, (h // 4) * 64:(h // 4 + 1) * 64],
                                          probT[:, n % 2, b * P:(b + 1) * P], start=b == 0, stop=b == qb)
                mm.then_inc(o_ps, 1)

            pe.wait_ge(bank_free, F_DSA_O)
            for n in range(66):
                if n < 64:
                    logits(n)
                if 1 <= n < 65:
                    turn(n - 1)
                if n >= 2:
                    weigh(n - 2)
            pe.wait_ge(o_ready, 8)
            proj(U_DSA_O, F_DSA_O, None)
            norm_sum(1)
            mlp(U_MLP0, F_MLP0, 0, 1)
            norm_sum(2)
            pe.wait_ge(bank_free, F_RWKV)
            for g in range(6):
                c = g // 2
                hi, lo = (u_hi, u_lo) if c % 2 else (a_hi, a_lo)
                for q in range(4):
                    tm_unit(U_RWKV + 4 * g + q, g, hi, lo, q, ready=(xs_ready, 8 * c) if g % 2 == 0 else None)
            pe.wait_ge(tm_free, 20)
            for j, c in enumerate((3, 4, 5, 5)):
                hi, lo = (u_hi, u_lo) if c % 2 else (a_hi, a_lo)
                fm_unit(U_RWKV + 24 + j, F_RWKV + j, hi, lo, ready=(xs_ready, 8 * c, 0) if j < 3 else None)
            pe.wait_ge(tm_free, 24)
            pe.wait_ge(lora_in, 16)
            for i in range(24):
                kind, t, half = i // 8, i % 8 // 2, i % 2
                if i % 8 == 0:
                    pe.wait_ge(lora_act, (1, 1, 3)[kind])
                    pe.wait_ge(bank_free, F_RWKV + (1, 2, 4)[kind])
                if i >= 4:
                    pe.wait_ge(lora_read, i - 3)
                cols, at = slice(half * T, half * T + T), slice(t * P, t * P + P)
                if kind < 2:
                    mm = nc.tensor.matmul(ps[:, 4 + i % 4], lora[0:65, kind, at], lora2[0:65, kind, cols], start=True, stop=True)
                else:
                    nc.tensor.matmul(ps[:, 4 + i % 4], lora[:, 2, at], lora2[:, 2, cols], start=True, stop=False)
                    mm = nc.tensor.matmul(ps[:, 4 + i % 4], lora[0:32, 3, at], lora2[0:32, 3, cols], start=False, stop=True)
                mm.then_inc(lora_ps, 1)
            pe.wait_ge(lora_read, 24)
            pe.wait_ge(bank_free, F_RWKV + 4)
            with pe.Fori(0, 4) as hg:
                with pe.Fori(0, 2) as tp:
                    for s in range(2):
                        n = 4 * hg + 2 * tp + s
                        r_, k_, v_, sg, a_, g_ = (rin[:, s, c] for c in range(6))
                        heads = [(e, p) for e in range(2) for p in range(2)]

                        def after(sem_, steps, name):
                            pe.wait_ge(sem_, steps.value(name, n))

                        pe.wait_ge(rin_in[s], 32 * hg + 16 * tp + 16)
                        nc.tensor.matmul(ps[:, 0, 0:256], tri[:, 0], sg, start=True, stop=True)
                        nc.tensor.matmul(ps[:, 0, 256:512], tri[:, 1], sg, start=True, stop=True).then_inc(pe_core, 1)
                        for p in range(2):
                            mm = nc.tensor.matmul(ps[:, 1, 2 * p:2 * p + 2], sg[:, p * P:(p + 1) * P], chunk_sum[:, 0], start=True, stop=True)
                        mm.then_inc(pe_core, 1)
                        after(dve_core, DVE_CORE, "rho")
                        for p in range(2):
                            for w, src in enumerate((AL, RHO)):
                                tr = nc.tensor.transpose(ps[:, 2, (2 * p + w) * P:(2 * p + w + 1) * P], rt[:, src, p * P:(p + 1) * P], ident[:])
                        tr.then_inc(pe_core, 1)
                        after(dve_core, DVE_CORE, "ka")
                        for w, src in enumerate((BE, KA)):
                            for p in range(2):
                                tr = nc.tensor.transpose(ps[:, 3, (2 * w + p) * P:(2 * w + p + 1) * P], rt[:, src, p * P:(p + 1) * P], ident[:])
                        tr.then_inc(pe_core, 1)
                        after(act_core, ACT_CORE, "bk")
                        for e, p in heads:
                            rows = slice(64 * e, 64 * e + 64)
                            mm = nc.tensor.matmul(ps[:, e, 256 * p:256 * p + 256], bkT[rows, 0, p], arT[rows, p], start=True, stop=True)
                        mm.then_inc(pe_core, 1)
                        for e, p in heads:
                            rows = slice(64 * e, 64 * e + 64)
                            mm = nc.tensor.matmul(ps[:, 2 + e, 256 * p:256 * p + 256], bkT[rows, 1, p], arT[rows, p], start=True, stop=True)
                        mm.then_inc(pe_core, 1)
                        for e, p in heads:
                            rows = slice(64 * e, 64 * e + 64)
                            mm = nc.tensor.matmul(ps[:, 4 + e, P * p:P * p + P], arT[rows, p, 0], bkT[rows, 0, p], start=True, stop=True)
                        mm.then_inc(pe_core, 1)
                        after(dve_core, DVE_CORE, "m2_1")
                        for e, p in heads:
                            mm = nc.tensor.matmul(ps[:, 6, (2 * e + p) * P:(2 * e + p + 1) * P], m2[:, e, p, 0], v_[:, p * P:(p + 1) * P], start=True, stop=True)
                        mm.then_inc(pe_core, 1)
                        after(act_core, ACT_CORE, "bv")
                        for lv in range(1, 6):
                            after(dve_core, DVE_CORE, f"tt{lv - 1}" if lv > 1 else "tt0_1")
                            for e, p in heads:
                                mm = nc.tensor.matmul(ps[:, 6, (2 * e + p) * P:(2 * e + p + 1) * P], m1[:, e, p, 0], Tm[:, e, p], start=True, stop=True)
                            mm.then_inc(pe_core, 1)
                            after(act_core, ACT_CORE, f"w{lv}")
                            if lv < 5:
                                for e, p in heads:
                                    mm = nc.tensor.matmul(ps[:, 7, (2 * e + p) * P:(2 * e + p + 1) * P], TT[:, e, p], Wm[:, 2 * e + p], start=True, stop=True)
                                mm.then_inc(pe_core, 1)
                            for e, p in heads:
                                mm = nc.tensor.matmul(ps[:, 4, (2 * e + p) * P:(2 * e + p + 1) * P], Wm[:, 2 * e + p], TT[:, e, p], start=True, stop=True)
                            mm.then_inc(pe_core, 1)
                        after(dve_core, DVE_CORE, "tt5")
                        for e, p in heads:
                            mm = nc.tensor.matmul(ps[:, 1, (2 * e + p) * P:(2 * e + p + 1) * P], TT[:, e, p], bv[:, 2 * e + p], start=True, stop=True)
                        mm.then_inc(pe_core, 1)
                        for e, p in heads:
                            mm = nc.tensor.matmul(ps[64 * e:64 * e + 64, 2, P * p:P * p + P], rt[:, AL, P * p + 64 * e:P * p + 64 * e + 64], TT[:, e, p],
                                                  start=True, stop=True)
                        mm.then_inc(pe_core, 1)
                        after(act_core, ACT_CORE, "ta")
                        if s == 0:
                            pe.wait_ge(state_zero, hg + 1)
                        for c in range(2):
                            rows = slice(64 * c, 64 * c + 64)
                            if c:
                                after(dve_core, DVE_CORE, "s1_c0")
                            for p in range(2):
                                mm = nc.tensor.matmul(ps[rows, 5, P * p:P * p + P], taT[:, p, rows], S[:, p], start=True, stop=True)
                            mm.then_inc(pe_core, 1)
                            for p in range(2):
                                mm = nc.tensor.matmul(ps[rows, 3, P * p:P * p + P], arT[:, p, 1, rows], S[:, p], start=True, stop=True)
                            mm.then_inc(pe_core, 1)
                            after(dve_core, DVE_CORE, f"u_c{c}")
                            for p in range(2):
                                nc.tensor.matmul(ps[:, 6 + c, P * p:P * p + P], rt[rows, BE, P * p:P * p + P], U[rows, p], start=True, stop=False)
                                mm = nc.tensor.matmul(ps[:, 6 + c, P * p:P * p + P], rt[rows, KA, P * p:P * p + P], v_[rows, P * p:P * p + P],
                                                      start=False, stop=True)
                            mm.then_inc(pe_core, 1)
                        for e, p in heads:
                            o = ps[:, 0, (2 * e + p) * P:(2 * e + p + 1) * P]
                            nc.tensor.matmul(o, m2[:, e, p, 1], v_[:, P * p:P * p + P], start=True, stop=False)
                            mm = nc.tensor.matmul(o, m1[:, e, p, 1], U[:, p], start=False, stop=True)
                        mm.then_inc(pe_core, 1)
                        after(dve_core, DVE_CORE, "o")
                        for p in range(2):
                            tr = nc.tensor.transpose(ps[:, 1, P * p:P * p + P], rt[:, OUT, P * p:P * p + P], ident[:])
                        tr.then_inc(pe_core, 1)
                        after(dve_core, DVE_CORE, "o_lo")
            proj(U_RWKV_O, F_RWKV_O, None)
            norm_sum(3)
            mlp(U_MLP1, F_MLP1, 32, 3 - 1)
            norm_sum(4)
            norm_sum(5)
            ffn(U_FFN1, F_FFN1, H_FFN1, 3)
            norm_sum(6)
            with pe.Fori(0, 2) as i:
                for j in range(12):
                    fm_unit(U_MIX + j, F_MIX + j, a_hi, a_lo, 12 * i, 12 * i, ready=(a_ready, KT * 4, 0) if j == 0 else None)
            pe.wait_ge(bank_free, F_MIX + 24)
            for g in range(6, 12):
                for q in range(4):
                    tm_unit(U_MIX + 24 + 4 * (g - 6) + q, g, a_hi, a_lo, q)
            pe.wait_ge(silu_ready, 4)
            fm_unit(U_MIX + 48, F_MIX + 24, a_hi, a_lo, nk=4, last=False)
            fm_unit(U_MIX + 49, F_MIX + 24, a_hi, a_lo, nk=4, k0=4, first=False)
            pe.wait_ge(silu_ready, 8)
            pe.wait_ge(gate_in, 16)
            pe.wait_ge(bank_free, F_MIX + 25)
            for t in range(NT):
                nc.tensor.matmul(ps[:, 4 + t], glr[0:33, t * P:(t + 1) * P], gate_up[0:33], start=True, stop=True).then_inc(la_ps, 1)
            for j in range(16):
                fm_unit(U_MIX + 50 + j, F_GATES + j, a_hi, a_lo)
            for j in range(8):
                fm_unit(U_MIX + 66 + j, F_GATES + 16 + j, u_hi, u_lo, ready=(u_ready, H_CONV, 0) if j == 0 else None)
            pe.wait_ge(bank_free, F_GLA_O)
            pe.wait_ge(la_ready, 4)
            with pe.Fori(0, 4) as h:
                with pe.Fori(0, 2) as tp:
                    for s in range(2):
                        n = 4 * h + 2 * tp + s

                        def after(sem_, steps, name):
                            pe.wait_ge(sem_, steps.value(name, n))

                        v_, la = gin[:, s, 256:512], gin[:, s, 768:896]
                        pe.wait_ge(gin_in[s], 32 * h + 16 * tp + 16)
                        for w in range(3):
                            nc.tensor.matmul(ps[:, 0, w * P:(w + 1) * P], tri[:, 2 + w], la, start=True, stop=True)
                        nc.tensor.matmul(ps[:, 0, 384:386], la, chunk_sum[:, 1], start=True, stop=True).then_inc(pe_gla, 1)
                        after(dve_gla, DVE_GLA, "qi")
                        for w in range(3):
                            tr = nc.tensor.transpose(ps[:, 1, w * P:(w + 1) * P], gqk[:, w], ident[:])
                        tr.then_inc(pe_gla, 1)
                        after(act_gla, ACT_GLA, "gT")
                        nc.tensor.matmul(ps[:, 2, 0:P], gT[:, 1], gT[:, 0], start=True, stop=True).then_inc(pe_gla, 1)
                        after(dve_gla, DVE_GLA, "ks")
                        for c in range(2):
                            rows = slice(64 * c, 64 * c + 64)
                            nc.tensor.matmul(ps[:, 4 + c, 0:256], gqk[rows, 3], v_[rows], start=True, stop=True).then_inc(pe_gla, 1)
                        after(dve_gla, DVE_GLA, "mask")
                        if s == 0:
                            pe.wait_ge(st_zero, h + 1)
                        for c in range(2):
                            rows = slice(64 * c, 64 * c + 64)
                            if c:
                                after(dve_gla, DVE_GLA, "st0")
                            nc.tensor.matmul(ps[rows, 3, 0:256], gT[:, 2, rows], St[:], start=True, stop=False)
                            nc.tensor.matmul(ps[rows, 3, 0:256], scT[:, rows], v_, start=False, stop=True).then_inc(pe_gla, 1)
                        after(dve_gla, DVE_GLA, "out")
                        for p in range(2):
                            tr = nc.tensor.transpose(ps[:, 6, P * p:P * p + P], gout[:, P * p:P * p + P], ident[:])
                        tr.then_inc(pe_gla, 1)
                        after(dve_gla, DVE_GLA, "o_lo")
            proj(U_GLA_O, F_GLA_O, None)
            proj(U_MIX_O, F_MIX_O, (u_ready, H_MERGED, 0), u_hi, u_lo)
            norm_sum(7)
            ffn(U_FFN2, F_FFN2, H_FFN2, 5)
            norm_sum(8)

        @block.scalar
        def _(act):
            def split_hi(m, off=0):
                if isinstance(off, int) and m + off >= U_END:
                    return
                act.wait_ge(raw_in[(m // 2) % 2], 16 * (m // 4 + 1) + 4 * off)
                if m >= SPLITS:
                    act.wait_ge(unit_done, m - 3 + off)
                nc.scalar.copy(w_hi[:, m % SPLITS], raw[:, (m // 2) % 2, (m % 2) * UNIT:(m % 2 + 1) * UNIT])\
                    .then_inc(hi_ready, 1)

            def norm(n, f):
                if f:
                    act.wait_ge(bank_free, f)
                else:
                    act.wait_ge(x_in, 16 * 13)
                for k in range(KT):
                    if k >= 4:
                        act.wait_ge(summed, KT * n + k - 3)
                    nc.scalar.activation(ep[:, k % 4], x[:, k], ACT.Square).then_inc(squared, 1)
                act.wait_ge(summed, KT * (n + 1))
                nc.scalar.activation(rstd[:], ps[:, 7], ACT.Sqrt, bias=EPS, scale=1.0 / D).then_inc(rooted, 1)

            def norm_hi(na, u):
                if u:
                    act.wait_ge(unit_done, u)
                for k in range(KT):
                    act.wait_ge(normed, KT * na + k + 1)
                    nc.scalar.copy(a_hi[:, k], h32[:, k % 3]).then_inc(a_hi_ready, 1)

            def hidden_hi(m, f, j, off=0, foff=0):
                act.wait_ge(bank_free, f + 1 + foff)
                nc.scalar.copy(u_hi[:, j], ep[:, 2 + j % 2]).then_inc(u_hi_ready, 1)

            def mlp(u, f):
                with act.Fori(0, 4) as i:
                    off = 16 * i
                    for j in range(8):
                        split_hi(u + j + AHEAD, off)
                        act.wait_ge(unit_done, u + j + 1 + off)
                        nc.scalar.activation(ep[:, j % 2], ps[:, (f + j) % 4], ACT.Relu).then_inc(ep_act, 1)
                        hidden_hi(u + j, f + j, j, off, off)
                    for j in range(8):
                        split_hi(u + 8 + j + AHEAD, off)

            def ffn(u, f):
                def chunk(size, u, f, off):
                    for q in range(0, 2 * size, 4):
                        for e in range(2):
                            split_hi(u + q + e + AHEAD, off)
                            act.wait_ge(unit_done, u + q + e + 1 + off)
                            nc.scalar.activation(ep[:, e], ps[:, (f + q + e) % 4], ACT.Sigmoid).then_inc(ep_act, 1)
                        for e in range(2):
                            split_hi(u + q + 2 + e + AHEAD, off)
                            hidden_hi(u + q + 2 + e, f + q + 2 + e, q // 2 + e, off, off)
                    for j in range(8):
                        split_hi(u + 2 * size + j + AHEAD, off)

                with act.Fori(0, 2) as i:
                    chunk(8, u, f, 24 * i)
                chunk(6, u + 48, f + 48, 0)

            for m in range(AHEAD):
                split_hi(m)
            norm(0, 0)
            norm_hi(0, 0)

            def swap_halves(j, r, rows):
                act.wait_ge(unit_done, j + 1)
                if r >= 2:
                    act.wait_ge(roped, r - 1)
                for q in range(0, rows, 32):
                    nc.scalar.copy(swap[q ^ 32:(q ^ 32) + 32, r % 2], ps[q:q + 32, (F_DSA + j) % 4 if j < 16 else F_DSA % 4])\
                        .then_inc(swap_ready, 1)

            r = 0
            for j in range(16):
                split_hi(j + AHEAD)
                if j in (10, 11):
                    continue
                else:
                    swap_halves(j, r, P)
                    r += 1
            split_hi(16 + AHEAD)
            split_hi(17 + AHEAD)
            swap_halves(17, r, 64)
            for j in range(2):
                act.wait_ge(vt_ps, 1)
                nc.scalar.copy(v_tm[:, 2 * j:2 * j + 2], ps[:, 4 + j].rearrange("p (t n) -> p t n", t=2)).then_inc(v_read, 1)
            for i in range(24):
                n = (2 + i // 8) * P
                act.wait_ge(idx_ps, i + 1)
                if i >= 2:
                    act.wait_ge(idx_added, i - 1)
                nc.scalar.activation(ep[:, i % 2, 0:n], ps[:, 4 + i % 2, 0:n], ACT.Relu).then_inc(idx_relu, 1)

            def probs(n):
                w = (n // 16 + 1) * P
                act.wait_ge(lg_bias, n + 1)
                nc.scalar.activation(prob[:, n % 3, 0:w], prob[:, n % 3, 0:w], ACT.Exp, bias=stat[:, 1, n:n + 1],
                                     scale=0.125, accum_out=stat[:, 2, n:n + 1]).then_inc(exp_ready, 1)

            def turned(n):
                w = (n // 16 + 1) * P
                act.wait_ge(tr_ps, n + 1)
                if n >= 2:
                    act.wait_ge(o_ps, n - 1)
                nc.scalar.copy(probT[:, n % 2, 0:w], ps[:, 6 + n % 2, 0:w]).then_inc(probT_ready, 1)

            def out_hi(g):
                act.wait_ge(o_ps, 8 * g + 8)
                nc.scalar.copy(a_hi[:, 4 * (g % 2):4 * (g % 2) + 4, (g // 2) * P:(g // 2 + 1) * P],
                               ps[:, g % 2].rearrange("p (j t) -> p j t", j=4)).then_inc(o_hi, 1)

            for n in range(66):
                if n < 64:
                    probs(n)
                if 1 <= n < 65:
                    turned(n - 1)
                if n >= 10 and (n - 10) % 8 == 0:
                    out_hi((n - 10) // 8)
            out_hi(7)
            for j in range(N_PROJ):
                split_hi(U_DSA_O + j + AHEAD)
            norm(1, F_MLP0)
            norm_hi(1, U_MLP0)
            mlp(U_MLP0, F_MLP0)
            norm(2, F_RWKV)

            def mixed_hi(c, k):
                if k == 0:
                    act.wait_ge(unit_done, U_RWKV + (0, 0, 8, 16, 24, 25)[c])
                act.wait_ge(xs32, 8 * c + k + 1)
                nc.scalar.copy((u_hi if c % 2 else a_hi)[:, k], h32[:, (8 * c + k) % 3]).then_inc(xs_hi, 1)

            for k in range(KT):
                mixed_hi(0, k)
            for g in range(6):
                for q in range(4):
                    split_hi(U_RWKV + 4 * g + q + AHEAD)
                    mixed_hi(g // 2 + 1, (4 * g + q) % 8)
                act.wait_ge(unit_done, U_RWKV + 4 * g + 4)
                for t in range(NT):
                    if g:
                        act.wait_ge(spill[t], 16 * g)
                    nc.scalar.copy(ep[:, t], ps[:, 4 * (g % 2) + t]).then_inc(tm_free, 1)
            split_hi(U_RWKV + 24 + AHEAD)
            for k in range(KT):
                mixed_hi(4, k)
            split_hi(U_RWKV + 25 + AHEAD)
            for k in range(KT):
                mixed_hi(5, k)
            split_hi(U_RWKV + 26 + AHEAD)
            split_hi(U_RWKV + 27 + AHEAD)
            act.wait_ge(bank_free, F_RWKV + 1)
            nc.scalar.activation(lora[0:64, 0], lora[0:64, 0], ACT.Tanh).then_inc(lora_act, 1)
            act.wait_ge(bank_free, F_RWKV + 3)
            nc.scalar.activation(lora[:, 2], lora[:, 2], ACT.Sigmoid).then_inc(lora_act, 1)
            act.wait_ge(bank_free, F_RWKV + 4)
            nc.scalar.activation(lora[0:32, 3], lora[0:32, 3], ACT.Sigmoid).then_inc(lora_act, 1)
            for i in range(24):
                act.wait_ge(lora_ps, i + 1)
                act.wait_ge(spill[i % 4], 16 * (6 + i // 4))
                nc.scalar.activation(ep[:, i % 4], ps[:, 4 + i % 4], ACT.Sigmoid if i < 16 else ACT.Copy).then_inc(lora_read, 1)
            with act.Fori(0, 4) as hg:
                with act.Fori(0, 2) as tp:
                    for s in range(2):
                        n = 4 * hg + 2 * tp + s

                        def after(name, sem_=None, steps=None):
                            act.wait_ge(pe_core if sem_ is None else sem_, (steps or PE_CORE).value(name, n))

                        after("decay")
                        nc.scalar.activation(ex[:, 0], ps[:, 0, 0:256], ACT.Exp).then_inc(act_core, 1)
                        nc.scalar.activation(ex[:, 1], ps[:, 0, 256:512], ACT.Exp).then_inc(act_core, 1)
                        nc.scalar.activation(ex[:, 2], ps[:, 0, 0:256], ACT.Exp, scale=-1.0).then_inc(act_core, 1)
                        after("chunk_decay")
                        nc.scalar.activation(pc[:].rearrange("p a b -> p (a b)"), ps[:, 1, 0:4], ACT.Exp).then_inc(act_core, 1)
                        after("turn_ar")
                        nc.scalar.copy(arT[:].rearrange("p a b c -> p (a b c)"), ps[:, 2]).then_inc(act_core, 1)
                        after("turn_bk")
                        nc.scalar.copy(bkT[:].rearrange("p a b c -> p (a b c)"), ps[:, 3]).then_inc(act_core, 1)
                        after("bv")
                        nc.scalar.copy(bv[:].rearrange("p a b -> p (a b)"), ps[:, 6]).then_inc(act_core, 1)
                        for lv in range(1, 6):
                            after(f"w{lv}")
                            nc.scalar.copy(Wm[:].rearrange("p a b -> p (a b)"), ps[:, 6]).then_inc(act_core, 1)
                        after("ta")
                        nc.scalar.copy(taT[:].rearrange("p a b -> p (a b)"), ps[:, 2, 0:256]).then_inc(act_core, 1)
                        after("yh")
                        for e in range(2):
                            nc.scalar.copy(yh[:, :, e], ps[:, 0, 256 * e:256 * e + 256].rearrange("p (a b) -> p a b", a=2)[:, :, 64 * e:64 * e + 64])\
                                .then_inc(act_core, 1)
                        after("turn_o")
                        nc.scalar.copy(a_hi[:, bass.ds(2 * hg, 2), bass.ds(2 * P * tp + P * s, P)],
                                       ps[:, 1, 0:256].rearrange("p (a b) -> p a b", a=2)).then_inc(act_core, 1)
            for j in range(N_PROJ):
                split_hi(U_RWKV_O + j + AHEAD)
            norm(3, F_MLP1)
            norm_hi(2, U_MLP1)
            mlp(U_MLP1, F_MLP1)
            norm(4, F_FFN1)
            act.wait_ge(x_scaled, KT)
            norm(5, F_FFN1)
            norm_hi(3, U_FFN1)
            ffn(U_FFN1, F_FFN1)
            norm(6, F_MIX)
            norm_hi(4, U_MIX)
            with act.Fori(0, 2) as i:
                for j in range(12):
                    split_hi(U_MIX + j + AHEAD, 12 * i)
                    if j % 6 >= 4:
                        tile = 2 * (j // 6) + j % 2
                        act.wait_ge(bank_free, F_MIX + j + 1 + 12 * i)
                        nc.scalar.copy(u_hi[:, bass.ds(4 * i + tile, 1)].rearrange("p o t -> p (o t)"), ep[:, 2 + j % 2]).then_inc(u_hi_ready, 1)
            for g in range(6, 12):
                for q in range(4):
                    split_hi(U_MIX + 4 * g + q + AHEAD)
                act.wait_ge(unit_done, U_MIX + 4 * g + 4)
                for t in range(NT):
                    if g > 6:
                        act.wait_ge(spill[t], 16 * (6 + g))
                    if g < 10:
                        nc.scalar.copy(ep[:, t], ps[:, 4 * (g % 2) + t]).then_inc(tm_free, 1)
                    else:
                        nc.scalar.activation(ep[:, t], ps[:, 4 * (g % 2) + t], ACT.Sigmoid).then_inc(tm_free, 1)
            split_hi(U_MIX + 48 + AHEAD)
            split_hi(U_MIX + 49 + AHEAD)
            for t in range(NT):
                act.wait_ge(la_ps, t + 1)
                act.wait_ge(spill[t], 16 * 18)
                nc.scalar.activation(ep[:, t], ps[:, 4 + t], ACT.Abs).then_inc(la_act, 1)
            for t in range(NT):
                act.wait_ge(la_act, t + 1)
                nc.scalar.activation(ep[:, t], ep[:, t], ACT.Exp, scale=-1.0).then_inc(la_act, 1)
            act.wait_ge(la_act, 8)
            for t in range(NT):
                nc.scalar.activation(ep[:, t], ep[:, t], ACT.Ln, bias=1.0).then_inc(la_act, 1)
            for j in range(16):
                split_hi(U_MIX + 50 + j + AHEAD)
                gate = (merged if j < 8 else sig_b)[:, j % 8]
                act.wait_ge(bank_free, F_GATES + j + 1)
                nc.scalar.activation(gate, gate, ACT.Sigmoid).then_inc(gated, 1)
            for j in range(8):
                split_hi(U_MIX + 66 + j + AHEAD)
            with act.Fori(0, 4) as h:
                with act.Fori(0, 2) as tp:
                    for s in range(2):
                        n = 4 * h + 2 * tp + s

                        def after(name):
                            act.wait_ge(pe_gla, PE_GLA.value(name, n))

                        after("decay")
                        nc.scalar.activation(gex[:, 0:3].rearrange("p a b -> p (a b)"), ps[:, 0, 0:384], ACT.Exp).then_inc(act_gla, 1)
                        nc.scalar.activation(gex[:, 3], ps[:, 0, 0:P], ACT.Exp, scale=-1.0).then_inc(act_gla, 1)
                        nc.scalar.activation(gdc[:], ps[:, 0, 384:386], ACT.Exp).then_inc(act_gla, 1)
                        after("turn")
                        nc.scalar.copy(gT[:].rearrange("p a b -> p (a b)"), ps[:, 1, 0:384]).then_inc(act_gla, 1)
                        after("o1")
                        nc.scalar.activation(gsq[:], ps[:, 3, 0:256], ACT.Square, accum_out=gst[:, 0:1]).then_inc(act_gla, 1)
                        after("turn_o")
                        nc.scalar.copy(a_hi[:, bass.ds(2 * h, 2), bass.ds(2 * P * tp + P * s, P)],
                                       ps[:, 6, 0:256].rearrange("p (a b) -> p a b", a=2)).then_inc(act_gla, 1)
            for j in range(8):
                split_hi(U_GLA_O + j + AHEAD)
                act.wait_ge(merged_ready, j + 1)
                nc.scalar.copy(u_hi[:, j], merged[:, j]).then_inc(u_hi_ready, 1)
            for j in range(8):
                split_hi(U_MIX_O + j + AHEAD)
            norm(7, F_FFN2)
            norm_hi(5, U_FFN2)
            ffn(U_FFN2, F_FFN2)
            norm(8, F_FFN2 + N_FFN)

        @block.vector
        def _(dve):
            chain = Tally(dve, dve_chain)

            def split_lo(m, off=0):
                if isinstance(off, int) and m + off >= U_END:
                    return
                dve.wait_ge(hi_ready, m + 1 + off)
                nc.vector.tensor_tensor(w_lo[:, m % SPLITS], raw[:, (m // 2) % 2, (m % 2) * UNIT:(m % 2 + 1) * UNIT],
                                        w_hi[:, m % SPLITS], ALU.subtract).then_inc(split_ready, 1)

            def norm_lo(n, na, col):
                dve.wait_ge(rooted, n + 1)
                chain.mark(nc.vector.reciprocal(rstd[:], rstd[:]))
                chain.wait()

                def low(k):
                    dve.wait_ge(a_hi_ready, KT * na + k + 1)
                    nc.vector.tensor_tensor(a_lo[:, k], h32[:, k % 3], a_hi[:, k], ALU.subtract).then_inc(a_ready, 1)

                for k in range(KT):
                    if k >= 3:
                        dve.wait_ge(a_ready, KT * na + k - 2)
                    nc.vector.scalar_tensor_tensor(h32[:, k % 3], x[:, k], vec[:, col, k:k + 1], rstd[:],
                                                   ALU.mult, ALU.mult).then_inc(normed, 1)
                    if k:
                        low(k - 1)
                low(KT - 1)

            def scale_x(n, col, count):
                dve.wait_ge(rooted, n + 1)
                chain.mark(nc.vector.reciprocal(rstd[:], rstd[:]))
                chain.wait()
                for k in range(KT):
                    nc.vector.scalar_tensor_tensor(x[:, k], x[:, k], vec[:, col, k:k + 1], rstd[:], ALU.mult, ALU.mult)\
                        .then_inc(x_scaled, 1)
                dve.wait_ge(x_scaled, count)

            def add_x(m, f, j, off=0, foff=0, scale=None):
                dve.wait_ge(unit_done, m + 1 + off)
                if scale is None:
                    nc.vector.tensor_tensor(x[:, j], ps[:, f % 4], x[:, j], ALU.add).then_inc(bank_free, 1)
                else:
                    nc.vector.scalar_tensor_tensor(x[:, j], ps[:, f % 4], scale, x[:, j], ALU.mult, ALU.add)\
                        .then_inc(bank_free, 1)

            def hidden_lo(h, j, hoff=0):
                dve.wait_ge(u_hi_ready, h + j + 1 + hoff)
                nc.vector.tensor_tensor(u_lo[:, j], ep[:, 2 + j % 2], u_hi[:, j], ALU.subtract).then_inc(u_ready, 1)

            def proj(u, f):
                for j in range(N_PROJ):
                    split_lo(u + j + AHEAD)
                    add_x(u + j, f + j, j)

            def mlp(u, f, h, e):
                with dve.Fori(0, 4) as i:
                    off, hoff = 16 * i, 8 * i
                    for j in range(8):
                        split_lo(u + j + AHEAD, off)
                        dve.wait_ge(ep_act, e + j + 1 + hoff)
                        nc.vector.tensor_tensor(ep[:, 2 + j % 2], ep[:, j % 2], ps[:, (f + j) % 4], ALU.mult)\
                            .then_inc(bank_free, 1)
                        hidden_lo(h, j, hoff)
                    for j in range(8):
                        split_lo(u + 8 + j + AHEAD, off)
                        add_x(u + 8 + j, f + 8 + j, j, off, off)

            def ffn(u, f, h, e):
                def chunk(size, u, f, h, e, off, hoff):
                    for q in range(0, 2 * size, 4):
                        for s in range(2):
                            split_lo(u + q + s + AHEAD, off)
                            dve.wait_ge(ep_act, e + q // 2 + s + 1 + hoff)
                            if q:
                                dve.wait_ge(u_ready, h + q // 2 + s - 1 + hoff)
                            nc.vector.tensor_tensor(ep[:, 2 + s], ep[:, s], ps[:, (f + q + s) % 4], ALU.mult)\
                                .then_inc(bank_free, 1)
                        for s in range(2):
                            split_lo(u + q + 2 + s + AHEAD, off)
                            dve.wait_ge(unit_done, u + q + 3 + s + off)
                            dve.wait_ge(bank_free, f + q + s + 1 + off)
                            nc.vector.tensor_tensor(ep[:, 2 + s], ep[:, 2 + s], ps[:, (f + q + 2 + s) % 4], ALU.mult)\
                                .then_inc(bank_free, 1)
                            hidden_lo(h, q // 2 + s, hoff)
                    for j in range(8):
                        split_lo(u + 2 * size + j + AHEAD, off)
                        add_x(u + 2 * size + j, f + 2 * size + j, j, off, off, 0.5)

                with dve.Fori(0, 2) as i:
                    chunk(8, u, f, h, e, 24 * i, 8 * i)
                chunk(6, u + 48, f + 48, h + 16, e + 16, 0, 0)

            for m in range(AHEAD):
                split_lo(m)
            dve.wait_ge(x_in, 16 * 13)
            norm_lo(0, 0, V_MIX0)

            def rope(j, r, rows, swaps):
                dve.wait_ge(swap_ready, swaps)
                if r:
                    dve.wait_ge(roped, r)
                chain.mark(nc.vector.tensor_tensor(swap[0:rows, r % 2], swap[0:rows, r % 2], sin[0:rows], ALU.mult))
                if rows == 64:
                    nc.vector.tensor_copy(kiwi[0:72], ps[0:72, 0]).then_inc(kiwi_ready, 1)
                nc.vector.tensor_tensor(rope1[0:rows], ps[0:rows, j % 4], cos[0:rows], ALU.mult).then_inc(bank_free, 1)
                chain.wait()

            r = 0
            for j in range(16):
                split_lo(j + AHEAD)
                if j in (10, 11):
                    dve.wait_ge(unit_done, j + 1)
                    nc.vector.tensor_copy(vT[:, j - 10], ps[:, j % 4]).then_inc(bank_free, 1)
                    continue
                rope(j, r, P, 4 * (r + 1))
                dve.wait_ge(bank_free, j + 1)
                if j < 8 or j >= 12:
                    dst = qT[:, j] if j < 8 else qiT[:, j - 12]
                    nc.vector.tensor_tensor(dst, rope1[:], swap[:, r % 2], ALU.add).then_inc(roped, 1)
                else:
                    for s in range(2):
                        rows, other = slice(64 * s, 64 * s + 64), slice(64 - 64 * s, 128 - 64 * s)
                        chain.mark(nc.vector.tensor_tensor(kd[rows, 2 * (j - 8) + s], rope1[rows], swap[rows, r % 2], ALU.add))
                    chain.wait()
                    for s in range(2):
                        rows, other = slice(64 * s, 64 * s + 64), slice(64 - 64 * s, 128 - 64 * s)
                        cp = nc.vector.tensor_copy(kd[other, 2 * (j - 8) + s], kd[rows, 2 * (j - 8) + s])
                        if s == 0:
                            chain.mark(cp)
                        else:
                            cp.then_inc(roped, 1)
                    chain.wait()
                r += 1
            split_lo(16 + AHEAD)
            split_lo(17 + AHEAD)
            rope(16, r, 64, 4 * 14 + 2)
            dve.wait_ge(bank_free, 17)
            nc.vector.tensor_tensor(kid[0:64], rope1[0:64], swap[0:64, r % 2], ALU.add).then_inc(roped, 1)
            dve.wait_ge(roped, 15)
            nc.vector.tensor_copy(kid[64:128], kid[0:64]).then_inc(roped, 1)
            dve.wait_ge(vt_ps, 2)
            nc.vector.tensor_scalar(wi[:], ps[:, 6].rearrange("p (t n) -> p t n", t=4)[:, :, 64:72],
                                    float(512 ** -0.5), None, ALU.mult).then_inc(wi_read, 1)
            dve.wait_ge(wi_read, 1)
            chain.mark(nc.vector.tensor_copy(amask[:, 0, 0:P], causal[:]))
            for i in range(24):
                qb, h = 1 + i // 8, i % 8
                n = (qb + 1) * P
                dve.wait_ge(idx_relu, i + 1)
                if i:
                    dve.wait_ge(idx_added, i)
                if h == 0:
                    nc.vector.tensor_scalar(score[:, 0:n], ep[:, i % 2, 0:n], wi[:, qb, 0:1], None, ALU.mult).then_inc(idx_added, 1)
                else:
                    nc.vector.scalar_tensor_tensor(score[:, 0:n], ep[:, i % 2, 0:n], wi[:, qb, h:h + 1], score[:, 0:n],
                                                   ALU.mult, ALU.add).then_inc(idx_added, 1)
                if h < 7:
                    continue
                dve.wait_ge(idx_added, i + 1)
                chain.mark(nc.vector.copy_predicated(score[:, n - P:n], imask[:, 12], fill[:]))
                chain.wait()
                for rnd in range(TOPK // 8):
                    chain.mark(nc.vector.max(top8[:], score[:, 0:n]))
                    chain.wait()
                    chain.mark(nc.vector.match_replace(score[:, 0:n], top8[:], score[:, 0:n], SCORE_TAKEN))
                    chain.wait()
                chain.mark(nc.vector.tensor_scalar(amask[:, qb, 0:n], score[:, 0:n], -3.2e38, NEG, ALU.is_gt, ALU.mult))
                chain.wait()

            def peak(n):
                w = (n // 16 + 1) * P
                dve.wait_ge(lg_ps, n + 1)
                if n >= 3:
                    dve.wait_ge(tr_ps, n - 2)
                nc.vector.tensor_tensor_reduce(prob[:, n % 3, 0:w], ps[:, 4 + n % 2, 0:w], amask[:, n // 16, 0:w], 1.0, -3.0e38,
                                               ALU.add, ALU.max, stat[:, 0, n:n + 1]).then_inc(lg_read, 1)
                dve.wait_ge(lg_read, n + 1)
                nc.vector.tensor_scalar(stat[:, 1, n:n + 1], stat[:, 0, n:n + 1], -0.125, None, ALU.mult).then_inc(lg_bias, 1)

            def normalise(n):
                w = (n // 16 + 1) * P
                dve.wait_ge(exp_ready, n + 1)
                chain.mark(nc.vector.reciprocal(stat[:, 3, n:n + 1], stat[:, 2, n:n + 1]))
                chain.wait()
                nc.vector.tensor_scalar(prob[:, n % 3, 0:w], prob[:, n % 3, 0:w], stat[:, 3, n:n + 1], None, ALU.mult)\
                    .then_inc(prob_ready, 1)

            def out_lo(g):
                dve.wait_ge(o_hi, g + 1)
                at = (slice(None), slice(4 * (g % 2), 4 * (g % 2) + 4), slice((g // 2) * P, (g // 2 + 1) * P))
                nc.vector.tensor_tensor(a_lo[at], ps[:, g % 2].rearrange("p (j t) -> p j t", j=4), a_hi[at], ALU.subtract)\
                    .then_inc(o_ready, 1)

            for n in range(66):
                if n < 64:
                    peak(n)
                if 1 <= n < 65:
                    normalise(n - 1)
                if n >= 11 and (n - 11) % 8 == 0:
                    out_lo((n - 11) // 8)
            out_lo(7)
            proj(U_DSA_O, F_DSA_O)
            norm_lo(1, 1, V_MLP0)
            mlp(U_MLP0, F_MLP0, 0, 0)
            dve.wait_ge(unit_done, U_RWKV)
            chain.mark(nc.vector.memset(h_pad[:, :, 0:2], 0.0))
            chain.mark(nc.vector.memset(lora[64:65, 0:2], 1.0))
            chain.mark(nc.vector.tensor_scalar(mu1[:], vec[:, V_MU:V_MU + 6], -1.0, 1.0, ALU.mult, ALU.add))
            dve.wait_ge(rooted, 3)
            chain.mark(nc.vector.reciprocal(rstd[:], rstd[:]))
            chain.wait()
            for k in range(KT):
                chain.mark(nc.vector.scalar_tensor_tensor(h_pad[:, k, 2:T + 2], x[:, k], vec[:, V_MIX1, k:k + 1], rstd[:], ALU.mult, ALU.mult))
            chain.wait()

            def mixed(c, k):
                i = 8 * c + k
                if i >= 3:
                    dve.wait_ge(xs_ready, i - 2)
                chain.mark(nc.vector.tensor_scalar(h32[:, (8 * c + k) % 3], h_pad[:, k, 2:T + 2], mu1[:, c, k:k + 1], None, ALU.mult))
                chain.wait()
                nc.vector.scalar_tensor_tensor(h32[:, (8 * c + k) % 3], h_pad[:, k, 1:T + 1], vec[:, V_MU + c, k:k + 1], h32[:, (8 * c + k) % 3],
                                               ALU.mult, ALU.add).then_inc(xs32, 1)

            def mixed_lo(c, k):
                dve.wait_ge(xs_hi, 8 * c + k + 1)
                nc.vector.tensor_tensor((u_lo if c % 2 else a_lo)[:, k], h32[:, (8 * c + k) % 3], (u_hi if c % 2 else a_hi)[:, k],
                                        ALU.subtract).then_inc(xs_ready, 1)

            def mixed_all(c):
                for k in range(KT):
                    mixed(c, k)
                    if k:
                        mixed_lo(c, k - 1)
                mixed_lo(c, KT - 1)

            mixed_all(0)
            for m in range(24):
                split_lo(U_RWKV + m + AHEAD)
                mixed(m // 8 + 1, m % 8)
                mixed_lo(m // 8 + 1, m % 8)
            split_lo(U_RWKV + 24 + AHEAD)
            mixed_all(4)
            dve.wait_ge(unit_done, U_RWKV + 25)
            nc.vector.tensor_copy(lora[0:64, 0], ps[0:64, F_RWKV % 4]).then_inc(bank_free, 1)
            split_lo(U_RWKV + 25 + AHEAD)
            mixed_all(5)
            for j, (rows, slot) in enumerate(((64, 1), (P, 2), (32, 3))):
                if j:
                    split_lo(U_RWKV + 25 + j + AHEAD)
                dve.wait_ge(unit_done, U_RWKV + 26 + j)
                nc.vector.tensor_copy(lora[0:rows, slot], ps[0:rows, (F_RWKV + 1 + j) % 4]).then_inc(bank_free, 1)
            dve.wait_ge(pool_step, 1)
            with dve.Fori(0, 4) as hg:
                nc.vector.memset(S[:], 0.0).then_inc(state_zero, 1)
                with dve.Fori(0, 2) as tp:
                    for s in range(2):
                        n = 4 * hg + 2 * tp + s
                        r_, k_, v_, sg, a_, g_ = (rin[:, s, c] for c in range(6))
                        todo = list(DVE_CORE.names)

                        def step(name, inst):
                            assert todo.pop(0) == name, name
                            inst.then_inc(dve_core, 1)

                        def own(name):
                            dve.wait_ge(dve_core, DVE_CORE.value(name, n))

                        def pe_(name):
                            dve.wait_ge(pe_core, PE_CORE.value(name, n))

                        def act_(name):
                            dve.wait_ge(act_core, ACT_CORE.value(name, n))

                        def predicated(cell, dst, mask, src):
                            nc.vector.memset(gate[:, cell:cell + 1], 0.0)
                            return nc.vector.copy_predicated(dst, mask, src)

                        def tt(dst, a, b, op=ALU.mult):
                            return nc.vector.tensor_tensor(dst, a, b, op)

                        def stt(dst, a, sc, b, op0, op1):
                            return nc.vector.scalar_tensor_tensor(dst, a, sc, b, op0, op1)

                        def by_head(ap):
                            return ap.rearrange("p (h d) -> p h d", h=4)

                        def prm_(j):
                            return prm[:, j, bass.ds(256 * hg, 256)]

                        X = [rt[:, i] for i in range(16)]
                        dve.wait_ge(rin_in[s], 32 * hg + 16 * tp + 16)
                        step("kkr", tt(X[KKR], k_, prm_(0)))
                        own("kkr")
                        step("sq", tt(X[SQ], X[KKR], X[KKR]))
                        own("sq")
                        step("ss", nc.vector.tensor_reduce(hst[:, H_SS], by_head(X[SQ]), AX.X, ALU.add))
                        own("ss")
                        step("ssm", nc.vector.tensor_scalar(hst[:, H_SSM], hst[:, H_SS], 1e-24, None, ALU.max))
                        step("t", stt(X[TA], a_, -1.0, prm_(1), ALU.add, ALU.mult))
                        own("t")
                        step("kf", stt(X[KF], X[TA], 1.0, k_, ALU.add, ALU.mult))
                        own("kf")
                        step("rkf", tt(X[RKF], r_, X[KF]))
                        own("rkf")
                        step("rkr", tt(X[RKF], X[RKF], prm_(2)))
                        own("rkr")
                        step("bs", nc.vector.tensor_reduce(hst[:, H_BS], by_head(X[RKF]), AX.X, ALU.add))
                        dve.wait_ge(pool_core, POOL_CORE.value("rn", n))
                        step("kk", tt(by_head(X[KK]), by_head(X[KKR]), over(hst[:, H_RN], 64)))
                        own("kk")
                        step("b", tt(X[BB], X[KK], a_))
                        act_("ex_neg")
                        step("al", stt(X[AL], X[KK], -1.0, ex[:, 1], ALU.mult, ALU.mult))
                        step("rho", tt(X[RHO], r_, ex[:, 0]))
                        own("b")
                        step("be", tt(X[BE], X[BB], ex[:, 2]))
                        step("ka", tt(X[KA], X[KF], ex[:, 2]))
                        both = strict_incl[:].rearrange("p (o a) b -> p o a b", o=1).to_broadcast([P, 2, 2, P])
                        pe_("m1")
                        for e in range(2):
                            step(f"m1_{e}", tt(m1[:, e], ps[:, e].rearrange("p (a b c) -> p a b c", a=2, b=2), both))
                        pe_("m2")
                        for e in range(2):
                            step(f"m2_{e}", tt(m2[:, e], ps[:, 2 + e].rearrange("p (a b c) -> p a b c", a=2, b=2), both))
                        dve.wait_ge(pool_core, POOL_CORE.value("eye_tt", n))
                        pe_("a")
                        for e in range(2):
                            step(f"t0_{e}", predicated(
                                e, Tm[:, e], bcast(imask[:, 0], 2, P), ps[:, 4 + e, 0:256].rearrange("p (a b) -> p a b", a=2)))
                        for e in range(2):
                            step(f"tt0_{e}", predicated(
                                2 + e, TT[:, e], bcast(imask[:, 6], 2, P), ps[:, e].rearrange("p (a b c) -> p a b c", a=2, b=2)[:, :, 0]))
                        for lv in range(1, 6):
                            if lv < 5:
                                pe_(f"tw{lv}")
                                step(f"t{lv}", predicated(
                                    3 + lv, Tm[:].rearrange("p a b c -> p (a b) c"), bcast(imask[:, lv], 4, P), ps[:, 7].rearrange("p (a b) -> p a b", a=4)))
                            pe_(f"wt{lv}")
                            own("tt0_1" if lv == 1 else f"tt{lv - 1}")
                            step(f"tt{lv}", predicated(
                                8 + lv, TT[:].rearrange("p a b c -> p (a b) c"), bcast(imask[:, 6 + lv], 4, P), ps[:, 4].rearrange("p (a b) -> p a b", a=4)))
                        pe_("u0")
                        for e in range(2):
                            step(f"u0_{e}", nc.vector.tensor_copy(
                                u0[:, :, e], ps[:, 1, 256 * e:256 * e + 256].rearrange("p (a b) -> p a b", a=2)[:, :, 64 * e:64 * e + 64]))
                        own("u0_1")
                        if s == 0:
                            dve.wait_ge(state_zero, hg + 1)
                        for c in range(2):
                            rows = slice(64 * c, 64 * c + 64)
                            pe_(f"u_c{c}")
                            step(f"u_c{c}", tt(U[rows], ps[rows, 5, 0:256].rearrange("p (a b) -> p a b", a=2),
                                               u0[rows].rearrange("p a b c -> p a (b c)"), ALU.add))
                            pe_(f"s_c{c}")
                            own(f"u_c{c}")
                            step(f"sx_c{c}", tt(S[:], ps[:, 6 + c, 0:256].rearrange("p (a b) -> p a b", a=2), S[:], ALU.add))
                            own(f"sx_c{c}")
                            for p in range(2):
                                step(f"s{p}_c{c}", stt(S[:, p], S[:, p], pc[:, p, c:c + 1], pair_mask[:], ALU.mult, ALU.mult))
                            own(f"s1_c{c}")
                        act_("yh1")
                        step("y", tt(X[YY], ps[:, 3, 0:256], yh[:].rearrange("p a b c -> p (a b c)"), ALU.add))
                        own("y")
                        step("sm", nc.vector.tensor_reduce(hst[:, H_SM], by_head(X[YY]), AX.X, ALU.add))
                        own("sm")
                        step("mean", nc.vector.tensor_scalar(hst[:, H_MEAN], hst[:, H_SM], 1.0 / 64, None, ALU.mult))
                        own("mean")
                        step("yc", tt(by_head(X[YC]), by_head(X[YY]), over(hst[:, H_MEAN], 64), ALU.subtract))
                        own("yc")
                        step("ysq", tt(X[SQ], X[YC], X[YC]))
                        own("ysq")
                        step("vs", nc.vector.tensor_reduce(hst[:, H_VS], by_head(X[SQ]), AX.X, ALU.add))
                        own("vs")
                        step("ve", nc.vector.tensor_scalar(hst[:, H_VE], hst[:, H_VS], 1.0 / 64, LNX_EPS, ALU.mult, ALU.add))
                        dve.wait_ge(pool_core, POOL_CORE.value("ri", n))
                        step("yn", tt(by_head(X[YC]), by_head(X[YC]), over(hst[:, H_RI], 64)))
                        own("yn")
                        step("yw", tt(X[YC], X[YC], prm_(3)))
                        own("yw")
                        step("yb", tt(X[YC], X[YC], prm_(4), ALU.add))
                        step("bonus", tt(by_head(X[BON]), by_head(v_), over(hst[:, H_BS], 64)))
                        own("bonus")
                        step("yv", tt(X[YC], X[YC], X[BON], ALU.add))
                        own("yv")
                        step("o", tt(X[OUT], X[YC], g_))
                        act_("o_hi")
                        at = (slice(None), bass.ds(2 * hg, 2), bass.ds(2 * P * tp + P * s, P))
                        step("o_lo", tt(a_lo[at], ps[:, 1, 0:256].rearrange("p (a b) -> p a b", a=2), a_hi[at], ALU.subtract))
                        own("o_lo")
                        assert not todo
            proj(U_RWKV_O, F_RWKV_O)
            norm_lo(3, 2, V_MLP1)
            mlp(U_MLP1, F_MLP1, 32, 32)
            scale_x(4, V_FINAL, KT)
            norm_lo(5, 3, V_FFN1)
            ffn(U_FFN1, F_FFN1, H_FFN1, 64)
            dve.wait_ge(unit_done, U_MIX)
            chain.mark(nc.vector.memset(uc[:, :, 0:2], 0.0))
            norm_lo(6, 4, V_MIXG)
            with chain.loop(2, 4 * 3) as lp:
                with dve.Fori(0, 2) as i:
                    lp.at(i)
                    for jj in range(0, 12, 6):
                        def done(q):
                            dve.wait_ge(unit_done, U_MIX + jj + q + 1 + 12 * i)

                        for e in range(2):
                            split_lo(U_MIX + jj + e + AHEAD, 12 * i)
                            done(e)
                            dve.wait_ge(u_ready, H_CONV + 2 * (jj // 6) + e - 1 + 4 * i)
                            nc.vector.tensor_copy(ep[:, 2 + e], ps[:, (F_MIX + jj + e) % 4]).then_inc(bank_free, 1)
                        for e in range(2):
                            split_lo(U_MIX + jj + 2 + e + AHEAD, 12 * i)
                            done(2 + e)
                            dve.wait_ge(bank_free, F_MIX + jj + e + 1 + 12 * i)
                            nc.vector.tensor_tensor(uc[:, e, 2:T + 2], ep[:, 2 + e], ps[:, (F_MIX + jj + 2 + e) % 4], ALU.mult)\
                                .then_inc(bank_free, 1)
                            dve.wait_ge(bank_free, F_MIX + jj + 2 + e + 1 + 12 * i)
                            tile = 2 * (jj // 6) + e
                            for w in range(3):
                                tap = vec[:, V_CONV + w, bass.ds(4 * i + tile, 1)]
                                if w == 0:
                                    chain.mark(nc.vector.tensor_scalar(uc2[:, e], uc[:, e, 0:T], tap, None, ALU.mult))
                                else:
                                    chain.wait()
                                    chain.mark(nc.vector.scalar_tensor_tensor(uc2[:, e], uc[:, e, w:T + w], tap, uc2[:, e], ALU.mult, ALU.add))
                            chain.wait()
                        for e in range(2):
                            split_lo(U_MIX + jj + 4 + e + AHEAD, 12 * i)
                            done(4 + e)
                            nc.vector.tensor_tensor(ep[:, 2 + e], uc2[:, e], ps[:, (F_MIX + jj + 4 + e) % 4], ALU.mult).then_inc(bank_free, 1)
                            tile = 2 * (jj // 6) + e
                            dve.wait_ge(u_hi_ready, H_CONV + tile + 1 + 4 * i)
                            nc.vector.tensor_tensor(u_lo[:, bass.ds(4 * i + tile, 1)].rearrange("p o t -> p (o t)"), ep[:, 2 + e],
                                                    u_hi[:, bass.ds(4 * i + tile, 1)].rearrange("p o t -> p (o t)"), ALU.subtract).then_inc(u_ready, 1)
            for g in range(6, 12):
                for q in range(4):
                    split_lo(U_MIX + 4 * g + q + AHEAD)
                if g >= 10:
                    for t in range(NT):
                        dve.wait_ge(tm_free, 4 * g + t + 1)
                        nc.vector.tensor_tensor(ep[:, t], ep[:, t], ps[:, 4 * (g % 2) + t], ALU.mult).then_inc(silu_ready, 1)
            chain.mark(nc.vector.memset(glr[:], 0.0))
            chain.wait()
            chain.mark(nc.vector.memset(glr[32:33], 1.0))
            split_lo(U_MIX + 48 + AHEAD)
            split_lo(U_MIX + 49 + AHEAD)
            dve.wait_ge(unit_done, U_MIX + 50)
            chain.wait()
            nc.vector.tensor_copy(glr[0:16], ps[0:16, (F_MIX + 24) % 4]).then_inc(bank_free, 1)
            for t in range(NT):
                dve.wait_ge(la_act, 9 + t)
                nc.vector.scalar_tensor_tensor(ep[:, t], ps[:, 4 + t], 0.0, ep[:, t], ALU.min, ALU.subtract).then_inc(la_ready, 1)
            for j in range(16):
                split_lo(U_MIX + 50 + j + AHEAD)
                dve.wait_ge(unit_done, U_MIX + 51 + j)
                nc.vector.tensor_copy((merged if j < 8 else sig_b)[:, j % 8], ps[:, (F_GATES + j) % 4]).then_inc(bank_free, 1)
            for j in range(8):
                split_lo(U_MIX + 66 + j + AHEAD)
                dve.wait_ge(unit_done, U_MIX + 67 + j)
                dve.wait_ge(gated, j + 1)
                nc.vector.tensor_tensor(merged[:, j], merged[:, j], ps[:, (F_GATES + 16 + j) % 4], ALU.mult).then_inc(bank_free, 1)
            chain.mark(nc.vector.memset(scT[:], 0.0))
            dve.wait_ge(gla_in, 16)
            chain.wait()
            with dve.Fori(0, 4) as h:
                nc.vector.memset(St[:], 0.0).then_inc(st_zero, 1)
                with dve.Fori(0, 2) as tp:
                    for s in range(2):
                        n = 4 * h + 2 * tp + s
                        todo = list(DVE_GLA.names)

                        def step(name, inst):
                            assert todo.pop(0) == name, name
                            inst.then_inc(dve_gla, 1)

                        def own(name):
                            dve.wait_ge(dve_gla, DVE_GLA.value(name, n))

                        def pe_(name):
                            dve.wait_ge(pe_gla, PE_GLA.value(name, n))

                        def act_(name):
                            dve.wait_ge(act_gla, ACT_GLA.value(name, n))

                        def stt(dst, a, sc, b, op0, op1):
                            return nc.vector.scalar_tensor_tensor(dst, a, sc, b, op0, op1)

                        q_, k_ = gin[:, s, 0:P], gin[:, s, P:2 * P]
                        dve.wait_ge(gin_in[s], 32 * h + 16 * tp + 16)
                        act_("ex_neg")
                        step("qr", stt(gqk[:, 0], q_, GLA_SCALE, gex[:, 0], ALU.mult, ALU.mult))
                        step("kr", nc.vector.tensor_tensor(gqk[:, 1], k_, gex[:, 3], ALU.mult))
                        step("qi", stt(gqk[:, 2], q_, GLA_SCALE, gex[:, 1], ALU.mult, ALU.mult))
                        step("ks", nc.vector.tensor_tensor(gqk[:, 3], k_, gex[:, 2], ALU.mult))
                        pe_("scores")
                        nc.vector.memset(gate[:, 14:15], 0.0)
                        step("mask", nc.vector.copy_predicated(scT[:], imask[:, 13], ps[:, 2, 0:P]))
                        act_("chunk")
                        if s == 0:
                            dve.wait_ge(st_zero, h + 1)
                        for c in range(2):
                            pe_(f"o{c}")
                            step(f"st{c}", stt(St[:], St[:], gdc[:, c:c + 1], ps[:, 4 + c, 0:256], ALU.mult, ALU.add))
                            own(f"st{c}")
                        act_("osq")
                        step("mean", nc.vector.tensor_scalar(gst[:, 1:2], gst[:, 0:1], 1.0 / 256, EPS, ALU.mult, ALU.add))
                        dve.wait_ge(pool_gla, POOL_GLA.value("ri", n))
                        step("on", stt(on[:], ps[:, 3, 0:256], gst[:, 2:3], gla_g[:, bass.ds(256 * h, 256)], ALU.mult, ALU.mult))
                        own("on")
                        step("out", nc.vector.tensor_tensor(gout[:], on[:], gin[:, s, 512:768], ALU.mult))
                        act_("o_hi")
                        at = (slice(None), bass.ds(2 * h, 2), bass.ds(2 * P * tp + P * s, P))
                        step("o_lo", nc.vector.tensor_tensor(a_lo[at], ps[:, 6, 0:256].rearrange("p (a b) -> p a b", a=2), a_hi[at], ALU.subtract))
                        own("o_lo")
                        assert not todo
            for j in range(8):
                split_lo(U_GLA_O + j + AHEAD)
                dve.wait_ge(unit_done, U_GLA_O + j + 1)
                dve.wait_ge(gated, 9 + j)
                nc.vector.tensor_tensor(sig_b[:, j], sig_b[:, j], ps[:, (F_GLA_O + j) % 4], ALU.mult).then_inc(bank_free, 1)
                dve.wait_ge(bank_free, F_GLA_O + j + 1)
                nc.vector.tensor_tensor(merged[:, j], merged[:, j], sig_b[:, j], ALU.add).then_inc(merged_ready, 1)
                dve.wait_ge(u_hi_ready, H_MERGED + j + 1)
                nc.vector.tensor_tensor(u_lo[:, j], merged[:, j], u_hi[:, j], ALU.subtract).then_inc(u_ready, 1)
            proj(U_MIX_O, F_MIX_O)
            norm_lo(7, 5, V_FFN2)
            ffn(U_FFN2, F_FFN2, H_FFN2, 86)
            scale_x(8, V_OUT, 2 * KT)

        @block.gpsimd
        def _(pool):
            def spill_out(slot, c, t, half):
                pool.dma_start(rk_dram[2 * half:2 * half + 2, t, :, c].rearrange("g p n -> p g n"),
                               ep[:, slot].rearrange("p (g n) -> p g n", g=2)).then_inc(spill[slot], 16)

            pool.wait_ge(unit_done, U_RWKV)
            pool.dma_start(lora2[:], io["lora2"]).then_inc(lora_in, 16)
            for g in range(6):
                for t in range(NT):
                    pool.wait_ge(tm_free, 4 * g + t + 1)
                    spill_out(t, g // 2, t, g % 2)
            for i in range(24):
                pool.wait_ge(lora_read, i + 1)
                spill_out(i % 4, (3, 4, 5)[i // 8], i % 8 // 2, i % 2)
            pool.wait_ge(bank_free, F_RWKV + 4)
            nc.gpsimd.memset(hst[:, H_HALF], -0.5).then_inc(pool_step, 1)
            pool.dma_start(prm[:], io["prm"].rearrange("(o j) n -> o j n", o=1).to_broadcast([P, 5, D])).then_inc(prm_in, 16)
            for s in range(4):
                pool.wait_ge(spill[s], 16 * 12)
            rounds = rk_dram.rearrange("g t p c n -> (g t) p (c n)")
            for s in range(2):
                pool.dma_start(rin[:, s].rearrange("p c n -> p (c n)"), rounds[s]).then_inc(rin_in[s], 16)
            pool.wait_ge(pool_step, 1)
            eye = bcast(ident[:], 4, P)

            def round_(n, s, more):
                nc.gpsimd.tensor_copy(Tm[:].rearrange("p a b c -> p (a b) c"), eye).then_inc(pool_core, 1)
                nc.gpsimd.tensor_copy(TT[:].rearrange("p a b c -> p (a b) c"), eye).then_inc(pool_core, 1)
                pool.wait_ge(dve_core, DVE_CORE.value("ssm", n))
                nc.gpsimd.tensor_tensor(hst[:, H_RN], hst[:, H_SSM], hst[:, H_HALF], ALU.pow).then_inc(pool_core, 1)
                pool.wait_ge(dve_core, DVE_CORE.value("ve", n))
                nc.gpsimd.tensor_tensor(hst[:, H_RI], hst[:, H_VE], hst[:, H_HALF], ALU.pow).then_inc(pool_core, 1)
                pool.wait_ge(pe_core, PE_CORE.value("turn_o", n))
                if more:
                    pool.dma_start(rin[:, s].rearrange("p c n -> p (c n)"),
                                   rounds[bass.ds(n + 2, 1)].rearrange("o p n -> p (o n)")).then_inc(rin_in[s], 16)

            with pool.Fori(0, 7) as i:
                for s in range(2):
                    round_(2 * i + s, s, True)
            for s in range(2):
                round_(14 + s, s, False)
            def spill_gla(slot, t, heads, cols):
                dst = gla_dram[heads, t, :, cols].rearrange("g p n -> p g n")
                n = dst.shape[1]
                pool.dma_start(dst, ep[:, slot].rearrange("p (g n) -> p g n", g=n)).then_inc(spill[slot], 16)

            pool.wait_ge(unit_done, U_MIX)
            pool.dma_start(gate_up[:], io["gate_up"]).then_inc(gate_in, 16)
            for g in range(6, 12):
                for t in range(NT):
                    if g < 10:
                        pool.wait_ge(tm_free, 4 * g + t + 1)
                    else:
                        pool.wait_ge(silu_ready, 4 * (g - 10) + t + 1)
                    if g < 8:
                        spill_gla(t, t, slice(0, 4), slice(P * (g - 6), P * (g - 5)))
                    else:
                        half = 2 * (g % 2)
                        spill_gla(t, t, slice(half, half + 2), slice(256, 512) if g < 10 else slice(512, 768))
            for t in range(NT):
                pool.wait_ge(la_ready, t + 1)
                spill_gla(t, t, slice(0, 4), slice(768, 896))
            for t in range(NT):
                pool.wait_ge(spill[t], 16 * 19)
            pool.wait_ge(unit_done, U_GLA_O)
            pool.dma_start(gla_g[:], io["gla_g"].to_broadcast([P, D])).then_inc(gla_in, 16)
            nc.gpsimd.memset(gst[:, 3:4], -0.5).then_inc(pool_gla_const, 1)
            rounds = gla_dram.rearrange("h t p n -> (h t) p n")
            for s in range(2):
                pool.dma_start(gin[:, s], rounds[s]).then_inc(gin_in[s], 16)
            pool.wait_ge(pool_gla_const, 1)

            def round_(n, s, more):
                pool.wait_ge(dve_gla, DVE_GLA.value("mean", n))
                nc.gpsimd.tensor_tensor(gst[:, 2:3], gst[:, 1:2], gst[:, 3:4], ALU.pow).then_inc(pool_gla, 1)
                pool.wait_ge(pe_gla, PE_GLA.value("turn_o", n))
                if more:
                    pool.dma_start(gin[:, s], rounds[bass.ds(n + 2, 1)].rearrange("o p n -> p (o n)")).then_inc(gin_in[s], 16)

            with pool.Fori(0, 7) as i:
                for s in range(2):
                    round_(2 * i + s, s, True)
            for s in range(2):
                round_(14 + s, s, False)


def constants():
    t = np.arange(T, dtype=np.float32)
    inv = (1.0 / (np.float32(10000.0) ** (np.arange(0, 64, 2, dtype=np.float32) / np.float32(64)))).astype(np.float32)
    ang = (inv[:, None] * t[None, :]).astype(np.float32)
    cos, sin = np.cos(ang), np.sin(ang)
    j, i = np.arange(P)[:, None], np.arange(P)[None, :]
    same = j // CHUNK == i // CHUNK
    upto, before = same & (j <= i), same & (j < i)
    ref = i // CHUNK * CHUNK + CHUNK // 2 - 1
    tri = np.stack([upto * -E_HALF, before * -E_HALF,
                    (upto * 1.0 - (same & (j <= ref))) / 16, upto / 16.0, (same & (j > i)) / 16.0, 0.0 * upto], 1)
    chunk = (np.arange(P)[:, None] // CHUNK == np.arange(2)[None, :]).astype(np.float32)
    levels = [((j // s) % 2 == 1) & ((i // s) % 2 == 0) & (j // (2 * s) == i // (2 * s)) for s in LEVELS]
    imask = np.stack(levels + [m.T for m in levels] + [i > j, upto], 1)
    out = dict(
        cos=np.tile(cos, (4, 1)), sin=np.concatenate([-sin, sin, -sin, sin]), ident=np.eye(P), ones=np.ones((P, P)),
        tri=tri, strict_incl=np.stack([before, upto], 1), chunk_sum=np.stack([chunk * -E_HALF, chunk / 16], 1),
        pair_mask=same, causal=np.where(i > j, NEG, 0.0), fill=np.full((P, P), SCORE_OUT),
    )
    out = {k: np.ascontiguousarray(v, np.float32) for k, v in out.items()}
    out["imask"] = np.ascontiguousarray(imask, np.int32)
    return out


def fm(w, col, rows=range(KT)):
    u = np.zeros((P, KT, P), np.float32)
    for n, k in enumerate(rows):
        part = w[k * P:(k + 1) * P, col:col + P]
        u[:, n, :part.shape[1]] = part
    return u.reshape(P, UNIT)


def tm(w, col):
    return [np.ascontiguousarray(w[2 * q * P:(2 * q + 2) * P, col:col + T].reshape(2, P, T).transpose(1, 0, 2)).reshape(P, UNIT)
            for q in range(4)]


def stream(a):
    s = []
    w = a["dsa_w_in"][0]
    s += [fm(w, P * j) for j in range(16)] + [fm(w, 2048, range(4)), fm(w, 2048, range(4, 8))]
    s += [fm(a["dsa_w_o"][0], P * j) for j in range(8)]

    def mlp(n):
        for c in range(4):
            yield from (fm(a["mlp_w_up"][n], D * c + P * j) for j in range(8))
            yield from (fm(a["mlp_w_down"][n], P * j, range(8 * c, 8 * c + 8)) for j in range(8))

    def ffn(gu, down):
        at = 0
        for size in FFN_CHUNKS:
            for j in range(at, at + size, 2):
                yield from (fm(gu, P * j), fm(gu, P * j + P), fm(gu, 2816 + P * j), fm(gu, 2816 + P * j + P))
            yield from (fm(down, P * j, range(at, at + size)) for j in range(8))
            at += size

    s += mlp(0)
    for c in range(3):
        s += tm(a["rwkv_w_rkv"][0, c], 0) + tm(a["rwkv_w_rkv"][0, c], 512)
    s += [fm(a["rwkv_w1"][0], 0), fm(a["rwkv_a1"][0], 0), fm(a["rwkv_g1"][0], 0), fm(a["rwkv_g1"][0], P)]
    s += [fm(a["rwkv_w_o"][0], P * j) for j in range(8)]
    s += mlp(1)
    s += ffn(a["ffn1_w_gu_2"][0], a["ffn1_w_down_2"][0])
    w = a["w_in_2"][0]
    for j in range(0, 8, 2):
        s += [fm(w, D * c + P * (j + e)) for c in (1, 2, 0) for e in (0, 1)]
    for col in (3072, 3584, 4096, 4608, 5136, 5648):
        s += tm(w, col)
    s += [fm(w[:, 5120:5136], 0, range(4)), fm(w[:, 5120:5136], 0, range(4, 8))]
    s += [fm(w, 6160 + P * j) for j in range(16)]
    for name in ("w_out_conv_2", "w_out_gla_2", "w_o_2"):
        s += [fm(a[name][0], P * j) for j in range(8)]
    s += ffn(a["ffn2_w_gu_2"][0], a["ffn2_w_down_2"][0])
    assert len(s) == U_END
    return np.stack(s).reshape(U_END // 2, 2, P, UNIT).transpose(0, 2, 1, 3).reshape(U_END // 2, P, 2 * UNIT)


def arrays_of(inputs):
    a = {k: np.asarray(v) for k, v in inputs.items()}
    v = [a["mixer_norm"], a["mlp_norm"], a["final_norm"][None], a["norm_ffn1_g_2"], a["norm_mix_g_2"], a["norm_ffn2_g_2"],
         a["final_norm_g_2"][None], a["rwkv_mu"][0], a["conv_w_2"][0]]
    vectors = np.concatenate(v).reshape(N_VEC, KT, P).transpose(2, 0, 1)
    g2 = np.zeros((2 * P, D), np.float32)
    g2[:160] = a["rwkv_g2"][0]
    lora2 = np.zeros((P, 4, D), np.float32)
    lora2[:64, 0], lora2[64, 0] = a["rwkv_w2"][0], a["rwkv_w0"][0]
    lora2[:64, 1], lora2[64, 1] = a["rwkv_a2"][0], a["rwkv_a0"][0]
    lora2[:, 2], lora2[:, 3] = g2[:P], g2[P:]
    gate_up = np.zeros((P, T), np.float32)
    gate_up[:16], gate_up[32] = a["gate_w_up_2"][0], a["gate_b_2"][0]
    out = constants()
    out.update(
        x=np.ascontiguousarray(a["x"][0].T.reshape(KT, P, T).transpose(1, 0, 2)), weights=stream(a), vec=vectors,
        lora2=lora2, gate_up=gate_up,
        prm=np.stack([a["rwkv_k_k"][0], a["rwkv_k_a"][0], a["rwkv_r_k"][0].reshape(D), a["rwkv_lnx_w"][0], a["rwkv_lnx_b"][0]]),
        gla_g=a["gla_norm_g_2"][0].reshape(1, D),
    )
    return {k: np.ascontiguousarray(v) for k, v in out.items()}


def kernel(**inputs):
    import concourse.bacc as bacc
    from concourse.bass_utils import run_bass_kernel_spmd

    nc = bacc.Bacc("TRN2", target_bir_lowering=False, num_devices=1)
    arrays = arrays_of(inputs)
    io = {k: nc.dram_tensor(k + "_dram", v.shape, mybir.dt.from_np(v.dtype), kind="ExternalInput").ap() for k, v in arrays.items()}
    out = nc.dram_tensor("out_dram", (P, KT, T), F32, kind="ExternalOutput").ap()
    build(nc, io, out)
    r = run_bass_kernel_spmd(nc, [{k + "_dram": v for k, v in arrays.items()}], core_ids=[0])
    got = r.results[0]["out_dram"]
    return got.transpose(2, 1, 0).reshape(1, T, D)
```

```python
from contextlib import ExitStack

import numpy as np

import concourse.bass as bass
from concourse import mybir

F32 = mybir.dt.float32
F32R = mybir.dt.float32r
I32 = mybir.dt.int32
ALU = mybir.AluOpType
ACT = mybir.ActivationFunctionType
AX = mybir.AxisListType

P = 128
T = 512
D = 1024
KT = D // P
NT = T // P
UNIT = 1024
SPLITS = 4
PAIRS = 2
AHEAD = 3

N_DSA_IN = 18
N_PROJ = 8
N_MLP = 64
N_RWKV_IN = 28
FFN_CHUNKS = (8, 8, 6)
N_FFN = sum(2 * c + 8 for c in FFN_CHUNKS)
N_MIX_IN = 24 + 24 + 2 + 8 + 8 + 8

U_DSA = 0
U_DSA_O = U_DSA + N_DSA_IN
U_MLP0 = U_DSA_O + N_PROJ
U_RWKV = U_MLP0 + N_MLP
U_RWKV_O = U_RWKV + N_RWKV_IN
U_MLP1 = U_RWKV_O + N_PROJ
U_FFN1 = U_MLP1 + N_MLP
U_MIX = U_FFN1 + N_FFN
U_GLA_O = U_MIX + N_MIX_IN
U_MIX_O = U_GLA_O + N_PROJ
U_FFN2 = U_MIX_O + N_PROJ
U_END = U_FFN2 + N_FFN

F_DSA, F_DSA_O = 0, 17
F_MLP0 = F_DSA_O + 8
F_RWKV = F_MLP0 + 64
F_RWKV_O = F_RWKV + 4
F_MLP1 = F_RWKV_O + 8
F_FFN1 = F_MLP1 + 64
F_MIX = F_FFN1 + N_FFN
F_GLA_O = F_MIX + 24 + 1 + 24
F_MIX_O = F_GLA_O + 8
F_FFN2 = F_MIX_O + 8

(V_MIX0, V_MIX1, V_MLP0, V_MLP1, V_FINAL, V_FFN1, V_MIXG, V_FFN2, V_OUT) = range(9)
V_MU, V_CONV, N_VEC = 9, 15, 18

LEVELS = (1, 2, 4, 8, 16, 32)
CHUNK = 64
EPS = 1e-6
LNX_EPS = 64e-5
NEG = -1.0e30
SCORE_OUT = -3.0e38
SCORE_TAKEN = -3.4e38
TOPK = 128
E_HALF = float(np.exp(-0.5))


class Tally:

    def __init__(self, eng, sem):
        self.eng, self.sem, self.n, self.reg = eng, sem, 0, 0

    def mark(self, inst):
        inst.then_inc(self.sem, 1)
        self.n += 1
        return self.n + self.reg

    def wait(self, label=None):
        self.eng.wait_ge(self.sem, self.n + self.reg if label is None else label)

    def loop(self, trips, per):
        return _TallyLoop(self, trips, per)


class _TallyLoop:
    def __init__(self, tally, trips, per):
        self.t, self.trips, self.per = tally, trips, per

    def __enter__(self):
        self.n0, self.reg0 = self.t.n, self.t.reg
        return self

    def at(self, i):
        self.t.reg = self.reg0 + i * self.per

    def __exit__(self, kind, *rest):
        if kind is None:
            assert self.t.n - self.n0 == self.per, ("marks in the loop's body", self.t.n - self.n0)
            self.t.n, self.t.reg = self.n0 + self.per * self.trips, self.reg0


def bcast(ap, n, inner):
    return ap.rearrange("p (o i) -> p o i", o=1).to_broadcast([ap.shape[0], n, inner])


def over(ap, inner):
    return ap.rearrange("p (n o) -> p n o", o=1).to_broadcast([ap.shape[0], ap.shape[1], inner])


class Steps:

    def __init__(self, *names):
        self.names = [n for group in names for n in group.split()]

    def value(self, name, rnd):
        return self.names.index(name) + 1 + rnd * len(self.names)


PE_FRONT = Steps("decay chunk_decay turn_ar turn_bk m1 m2 a bv")
ACT_FRONT = Steps("ex_in ex_before ex_neg pc ar bk bv")
DVE_FRONT = Steps("kkr sq ss ssm t kf rkf rkr bs kk b al rho be ka m1_0 m1_1 m2_0 m2_1 t0_0 t0_1 tt0_0 tt0_1")
POOL_FRONT = Steps("eye_t eye_tt rn")
PE_INV = Steps(" ".join(f"w{v} tw{v} wt{v}" if v < 5 else f"w{v} wt{v}" for v in range(1, 6)), "u0 ta")
ACT_INV = Steps(" ".join(f"w{v}" for v in range(1, 6)), "ta")
DVE_INV = Steps(" ".join(f"t{v} tt{v}" if v < 5 else f"tt{v}" for v in range(1, 6)), "u0_0 u0_1")
PE_BACK = Steps("u_c0 y_c0 s_c0 u_c1 y_c1 s_c1 yh turn_o")
ACT_BACK = Steps("yh0 yh1 o_hi")
DVE_BACK = Steps("u_c0 sx_c0 s0_c0 s1_c0 u_c1 sx_c1 s0_c1 s1_c1 y sm mean yc ysq vs ve yn yw yb bonus yv o o_lo")
POOL_BACK = Steps("ri")
ROUNDS = NT * 4
GROUPS = 4
B_UY, B_S, B_YH = 0, 1, 2
B_M1, B_M2, B_A = (0, 2), (3, 4), (1, 4)
B_W, B_TW, B_WT = 5, 6, 7

KKR, SQ, KK, TA, KF, RHO, RKF, BB = range(8)
YY, YC, YSQ, OUT, BON = range(5)
(H_SS, H_SSM, H_RN, H_SM, H_MEAN, H_VS, H_VE, H_RI) = range(8)

PE_GLA = Steps("decay turn scores kv0 kv1 o0 o1 turn_o")
ACT_GLA = Steps("ex ex_neg chunk gT osq o_hi")
DVE_GLA = Steps("qr kr qi ks mask st0 st1 mean on out o_lo")
POOL_GLA = Steps("ri")
GLA_SCALE = 128 ** -0.5
F_GATES = F_MIX + 25
H_MLP0, H_MLP1, H_FFN1, H_CONV, H_MERGED, H_FFN2 = 0, 32, 64, 86, 94, 102


def build(nc, io, out):
    with ExitStack() as ctx:
        def sb(name, shape, dt=F32, at=ctx):
            return at.enter_context(nc.sbuf_tensor(name, shape, dt))

        def sem(name):
            return ctx.enter_context(nc.semaphore(name))

        x = sb("x_res", [P, KT, T])
        gate = sb("gate", [P, 15])
        raw = sb("raw", [P, PAIRS, 2 * UNIT])
        w_hi = sb("w_hi", [P, SPLITS, UNIT], F32R)
        w_lo = sb("w_lo", [P, SPLITS, UNIT], F32R)
        a_hi = sb("a_hi", [P, KT, T], F32R)
        a_lo = sb("a_lo", [P, KT, T], F32R)
        rstd = sb("rstd", [P, T])
        h32 = sb("h32", [P, 3, T])
        ep = sb("ep", [P, 4, T])
        vec = sb("vec", [P, N_VEC, KT])
        ident = sb("ident", [P, P])
        ones = sb("ones", [P, P])
        tri = sb("tri", [P, 6, P])
        strict_incl = sb("strict_incl", [P, 2, P])
        chunk_sum = sb("chunk_sum", [P, 2, 2])
        imask = sb("imask", [P, 14, P], I32)
        pair_mask = sb("pair_mask", [P, P])

        with ExitStack() as attn:
            cos = sb("cos", [P, T], at=attn)
            sin = sb("sin", [P, T], at=attn)
            qT = sb("qT", [P, 8, T], at=attn)
            kd = sb("kd", [P, 4, T], at=attn)
            vT = sb("vT", [P, 2, T], at=attn)
            v_tm = sb("v_tm", [P, NT, 256], at=attn)
            qiT = sb("qiT", [P, 4, T], at=attn)
            kiwi = sb("kiwi", [P, T], at=attn)
            kid = sb("kid", [P, T], at=attn)
            wi = sb("wi", [P, NT, 8], at=attn)
            swap = sb("swap", [P, 2, T], at=attn)
            rope1 = sb("rope1", [P, T], at=attn)
            score = sb("score", [P, T], at=attn)
            top8 = sb("top8", [P, 8], at=attn)
            fill = sb("fill", [P, P], at=attn)
            causal = sb("causal", [P, P], at=attn)
            amask = sb("amask", [P, NT, T], at=attn)
            prob = sb("prob", [P, 3, T], at=attn)
            probT = sb("probT", [P, 2, T], at=attn)
            stat = sb("stat", [P, 4, 64], at=attn)
        with ExitStack() as gla:
            gin = sb("gin", [P, 2, 896], at=gla)
            gex = sb("gex", [P, 4, P], at=gla)
            gdc = sb("gdc", [P, 2], at=gla)
            gqk = sb("gqk", [P, 4, P], at=gla)
            gT = sb("gT", [P, 3, P], at=gla)
            scT = sb("scT", [P, P], at=gla)
            St = sb("St", [P, 256], at=gla)
            gsq = sb("gsq", [P, 256], at=gla)
            gst = sb("gst", [P, 4], at=gla)
            on = sb("on", [P, 256], at=gla)
            gout = sb("gout", [P, 256], at=gla)
            gla_g = sb("gla_g", [P, D], at=gla)
        u_scope = ExitStack()
        u_hi = sb("u_hi", [P, KT, T], F32R, at=u_scope)
        u_lo = sb("u_lo", [P, KT, T], F32R, at=u_scope)
        with ExitStack() as shift:
            h_pad = sb("h_pad", [P, KT, T + 2], at=shift)
            mu1 = sb("mu1", [P, 6, KT], at=shift)
            lora = sb("lora", [P, 4, T], at=shift)
            lora2 = sb("lora2", [P, 4, D], at=shift)
        with ExitStack() as conv:
            uc = sb("uc", [P, 2, T + 2], at=conv)
            uc2 = sb("uc2", [P, 2, T], at=conv)
            merged = sb("merged", [P, KT, T], at=conv)
            sig_b = sb("sig_b", [P, KT, T], at=conv)
            glr = sb("glr", [P, T], at=conv)
            gate_up = sb("gate_up", [P, 512], at=conv)
        u_scope.close()
        with ExitStack() as core:
            rin_f = sb("rin_f", [P, 5, 256], at=core)
            rin_b = sb("rin_b", [P, 2, 256], at=core)
            prm = sb("prm", [P, 5, D], at=core)
            ex = sb("ex", [P, 3, 256], at=core)
            hst = sb("hst", [P, 2, 8, 4], at=core)
            bs = sb("bs", [P, GROUPS, 4], at=core)
            h_half = sb("h_half", [P, 4], at=core)
            pc = sb("pc", [P, 2, 2, 2], at=core)
            be_ka = sb("be_ka", [P, 2, 2, 256], at=core)
            arT = sb("arT", [P, 2, 2, 2, P], at=core)
            bkT = sb("bkT", [P, 2, 2, P], at=core)
            m1 = sb("m1", [P, 2, 2, 2, 2, P], at=core)
            m2 = sb("m2", [P, 2, 2, 2, 2, P], at=core)
            Tm = sb("Tm", [P, 2, 4, P], at=core)
            TT = sb("TT", [P, 2, 4, P], at=core)
            Wm = sb("Wm", [P, 4, P], at=core)
            bv = sb("bv", [P, 2, 4, P], at=core)
            u0 = sb("u0", [P, 2, 2, 64], at=core)
            taT = sb("taT", [P, 2, P], at=core)
            U = sb("U", [P, 2, P], at=core)
            S = sb("S", [P, GROUPS, 2, P], at=core)
            yh = sb("yh", [P, 2, 2, 64], at=core)
        front_t = ep[:].rearrange("p a (b n) -> p (a b) n", b=2)
        back_t = h32[:].rearrange("p a (b n) -> p (a b) n", b=2)
        al_t = rstd[:].rearrange("p (a n) -> p a n", a=2)
        ps = ctx.enter_context(nc.psum_tensor("ps", [P, 8, T], F32))

        rk_dram = nc.dram_tensor("rwkv_scratch", (NT, GROUPS, P, 6, 256), F32).ap()

        gla_dram = nc.dram_tensor("gla_scratch", (4, NT, P, 896), F32).ap()

        raw_in = [sem("raw_in0"), sem("raw_in1")]
        hi_ready = sem("hi_ready")
        split_ready = sem("split_ready")
        unit_done = sem("unit_done")
        bank_free = sem("bank_free")
        tm_free = sem("tm_free")
        const_in = sem("const_in")
        x_in = sem("x_in")
        squared = sem("squared")
        summed = sem("summed")
        rooted = sem("rooted")
        normed = sem("normed")
        a_hi_ready = sem("a_hi_ready")
        a_ready = sem("a_ready")
        ep_act = sem("ep_act")
        ep_dve = sem("ep_dve")
        u_hi_ready = sem("u_hi_ready")
        u_ready = sem("u_ready")
        dve_chain = sem("dve_chain")
        act_chain = sem("act_chain")
        pool_chain = sem("pool_chain")
        pe_step = sem("pe_step")
        act_step = sem("act_step")
        dve_step = sem("dve_step")
        pool_step = sem("pool_step")
        spilled = sem("spilled")
        rin_f_in = sem("rin_f_in")
        rin_b_in = sem("rin_b_in")
        prm_in = sem("prm_in")
        swap_ready = sem("swap_ready")
        roped = sem("roped")
        kiwi_ready = sem("kiwi_ready")
        vt_ps = sem("vt_ps")
        v_read = sem("v_read")
        wi_read = sem("wi_read")
        idx_ps = sem("idx_ps")
        idx_relu = sem("idx_relu")
        idx_added = sem("idx_added")
        lg_ps = sem("lg_ps")
        lg_read = sem("lg_read")
        lg_bias = sem("lg_bias")
        exp_ready = sem("exp_ready")
        prob_ready = sem("prob_ready")
        tr_ps = sem("tr_ps")
        probT_ready = sem("probT_ready")
        o_ps = sem("o_ps")
        o_hi = sem("o_hi")
        o_ready = sem("o_ready")
        out_done = sem("out_done")
        late_in = sem("late_in")
        xs32 = sem("xs32")
        xs_hi = sem("xs_hi")
        xs_ready = sem("xs_ready")
        lora_in = sem("lora_in")
        lora_act = sem("lora_act")
        lora_ready = sem("lora_ready")
        lora_ps = sem("lora_ps")
        lora_read = sem("lora_read")
        spill = [sem(f"spill{i}") for i in range(4)]
        pe_front, act_front, dve_front, pool_front = (sem(n) for n in ("pe_front", "act_front", "dve_front", "pool_front"))
        pe_inv, act_inv, dve_inv = (sem(n) for n in ("pe_inv", "act_inv", "dve_inv"))
        pe_back, act_back, dve_back, pool_back = (sem(n) for n in ("pe_back", "act_back", "dve_back", "pool_back"))
        state_zero = sem("state_zero")
        x_scaled = sem("x_scaled")
        gated = sem("gated")
        silu_ready = sem("silu_ready")
        la_act = sem("la_act")
        la_ps = sem("la_ps")
        la_ready = sem("la_ready")
        gate_in = sem("gate_in")
        gla_in = sem("gla_in")
        gin_in = [sem("gin_in0"), sem("gin_in1")]
        st_zero = sem("st_zero")
        pe_gla, act_gla, dve_gla, pool_gla = (sem(n) for n in ("pe_gla", "act_gla", "dve_gla", "pool_gla"))
        merged_ready = sem("merged_ready")
        pool_gla_const = sem("pool_gla_const")
        block = ctx.enter_context(nc.Block())

        @block.sync
        def _(sp):
            for dst, name in ((x, "x"), (vec, "vec"), (ident, "ident"), (ones, "ones"), (tri, "tri"),
                              (strict_incl, "strict_incl"), (chunk_sum, "chunk_sum"), (imask, "imask"),
                              (pair_mask, "pair_mask"), (cos, "cos"), (sin, "sin"), (causal, "causal"),
                              (fill, "fill")):
                sp.dma_start(dst[:], io[name]).then_inc(x_in, 16)
            pairs = U_END // 2
            for s in range(PAIRS):
                sp.dma_start(raw[:, s], io["weights"][s]).then_inc(raw_in[s], 16)
            with sp.Fori(1, pairs // PAIRS) as i:
                for s in range(PAIRS):
                    sp.wait_ge(split_ready, 2 * PAIRS * i + 2 * s - 2 * PAIRS + 2)
                    sp.dma_start(raw[:, s], io["weights"][bass.ds(PAIRS * i + s, 1)].rearrange("o p n -> p (o n)"))\
                        .then_inc(raw_in[s], 16)
            for k in range(KT):
                sp.wait_ge(x_scaled, KT + k + 1)
                sp.dma_start(out[:, k], x[:, k]).then_inc(out_done, 16)
            sp.wait_ge(out_done, 16 * KT)

        @block.tensor
        def _(pe):
            def fm_unit(m, f, hi, lo, off=0, foff=0, k0=0, nk=KT, first=True, last=True, ready=None):
                bank = ps[:, f % 4]
                pe.wait_ge(split_ready, m + 1 + off)
                if first and f >= 4:
                    pe.wait_ge(bank_free, f - 3 + foff)
                for k in range(nk):
                    if ready is not None:
                        pe.wait_ge(ready[0], ready[1] + k + 1 + ready[2])
                    wh = w_hi[:, m % SPLITS, k * P:(k + 1) * P]
                    wl = w_lo[:, m % SPLITS, k * P:(k + 1) * P]
                    nc.tensor.matmul(bank, wh, hi[:, k0 + k], start=first and k == 0, stop=False)
                    nc.tensor.matmul(bank, wh, lo[:, k0 + k], start=False, stop=False)
                    mm = nc.tensor.matmul(bank, wl, hi[:, k0 + k], start=False, stop=last and k == nk - 1)
                mm.then_inc(unit_done, 1)

            def tm_unit(m, g, hi, lo, q, ready=None):
                pe.wait_ge(split_ready, m + 1)
                for k in (2 * q, 2 * q + 1):
                    if ready is not None:
                        pe.wait_ge(ready[0], ready[1] + k + 1)
                    wk = slice((k % 2) * T, (k % 2 + 1) * T)
                    for t in range(NT):
                        if k == 0 and g >= 2:
                            pe.wait_ge(tm_free, 4 * (g - 2) + t + 1)
                        bank = ps[:, 4 * (g % 2) + t]
                        at = slice(t * P, (t + 1) * P)
                        nc.tensor.matmul(bank, hi[:, k, at], w_hi[:, m % SPLITS, wk], start=k == 0, stop=False)
                        nc.tensor.matmul(bank, hi[:, k, at], w_lo[:, m % SPLITS, wk], start=False, stop=False)
                        mm = nc.tensor.matmul(bank, lo[:, k, at], w_hi[:, m % SPLITS, wk], start=False, stop=k == KT - 1)
                mm.then_inc(unit_done, 1)

            def norm_sum(n):
                for k in range(KT):
                    pe.wait_ge(squared, KT * n + k + 1)
                    nc.tensor.matmul(ps[:, 7], ones[:], ep[:, k % 4], start=k == 0, stop=k == KT - 1)\
                        .then_inc(summed, 1)

            def proj(u, f, ready, hi=a_hi, lo=a_lo):
                for j in range(N_PROJ):
                    fm_unit(u + j, f + j, hi, lo, ready=ready if j == 0 else None)

            def mlp(u, f, h, n):
                with pe.Fori(0, 4) as i:
                    off, hoff = 16 * i, 8 * i
                    for j in range(8):
                        fm_unit(u + j, f + j, a_hi, a_lo, off, off,
                                ready=(a_ready, KT * n, 0) if j == 0 else None)
                    for j in range(8):
                        fm_unit(u + 8 + j, f + 8 + j, u_hi, u_lo, off, off,
                                ready=(u_ready, h, hoff) if j == 0 else None)

            def ffn(u, f, h, n):
                def chunk(size, u, f, h, off, hoff, first):
                    for j in range(2 * size):
                        fm_unit(u + j, f + j, a_hi, a_lo, off, off,
                                ready=(a_ready, KT * n, 0) if j == 0 and first else None)
                    for j in range(8):
                        fm_unit(u + 2 * size + j, f + 2 * size + j, u_hi, u_lo, off, off, nk=size,
                                ready=(u_ready, h, hoff) if j == 0 else None)

                with pe.Fori(0, 2) as i:
                    chunk(8, u, f, h, 24 * i, 8 * i, True)
                chunk(6, u + 48, f + 48, h + 16, 0, 0, False)

            pe.wait_ge(x_in, 16 * 13)
            norm_sum(0)
            for j in range(16):
                fm_unit(U_DSA + j, F_DSA + j, a_hi, a_lo, ready=(a_ready, 0, 0) if j == 0 else None)
            fm_unit(U_DSA + 16, F_DSA + 16, a_hi, a_lo, nk=4, last=False)
            fm_unit(U_DSA + 17, F_DSA + 16, a_hi, a_lo, nk=4, k0=4, first=False)
            pe.wait_ge(bank_free, 12)
            for t in range(NT):
                for j in range(2):
                    tr = nc.tensor.transpose(ps[:, 4 + t // 2, (t % 2) * 256 + j * P:(t % 2) * 256 + (j + 1) * P],
                                             vT[:, j, t * P:(t + 1) * P], ident[:])
            tr.then_inc(vt_ps, 1)
            pe.wait_ge(kiwi_ready, 1)
            for t in range(NT):
                tr = nc.tensor.transpose(ps[:, 6, t * P:t * P + 72], kiwi[0:72, t * P:(t + 1) * P], ident[0:72, 0:72])
            tr.then_inc(vt_ps, 1)
            pe.wait_ge(roped, 16)
            pe.wait_ge(v_read, 2)
            pe.wait_ge(wi_read, 1)
            for i in range(24):
                qb, h = 1 + i // 8, i % 8
                n, e = (qb + 1) * P, 64 * (h % 2)
                if i >= 2:
                    pe.wait_ge(idx_relu, i - 1)
                nc.tensor.matmul(ps[:, 4 + i % 2, 0:n], qiT[e:e + 64, h // 2, qb * P:(qb + 1) * P],
                                 kid[e:e + 64, 0:n], start=True, stop=True).then_inc(idx_ps, 1)
            pe.wait_ge(idx_relu, 24)

            def logits(n):
                qb, h = n // 16, n % 16
                e = 64 * (h % 2)
                if n >= 2:
                    pe.wait_ge(lg_read, n - 1)
                nc.tensor.matmul(ps[:, 4 + n % 2, 0:(qb + 1) * P], qT[e:e + 64, h // 2, qb * P:(qb + 1) * P],
                                 kd[e:e + 64, h // 4, 0:(qb + 1) * P], start=True, stop=True).then_inc(lg_ps, 1)

            def turn(n):
                pe.wait_ge(prob_ready, n + 1)
                if n >= 2:
                    pe.wait_ge(probT_ready, n - 1)
                for b in range(n // 16 + 1):
                    tr = nc.tensor.transpose(ps[:, 6 + n % 2, b * P:(b + 1) * P], prob[:, n % 3, b * P:(b + 1) * P], ident[:])
                tr.then_inc(tr_ps, 1)

            def weigh(n):
                qb, h = n // 16, n % 16
                e = 64 * (h % 2)
                pe.wait_ge(probT_ready, n + 1)
                if n % 8 == 0 and n >= 16:
                    pe.wait_ge(o_ready, n // 8 - 1)
                o = ps[e:e + 64, (n // 8) % 2, (h % 8 // 2) * P:(h % 8 // 2 + 1) * P]
                for b in range(qb + 1):
                    mm = nc.tensor.matmul(o, v_tm[:, b, (h // 4) * 64:(h // 4 + 1) * 64],
                                          probT[:, n % 2, b * P:(b + 1) * P], start=b == 0, stop=b == qb)
                mm.then_inc(o_ps, 1)

            pe.wait_ge(bank_free, F_DSA_O)
            for n in range(66):
                if n < 64:
                    logits(n)
                if 1 <= n < 65:
                    turn(n - 1)
                if n >= 2:
                    weigh(n - 2)
            pe.wait_ge(o_ready, 8)
            proj(U_DSA_O, F_DSA_O, None)
            norm_sum(1)
            mlp(U_MLP0, F_MLP0, 0, 1)
            norm_sum(2)
            pe.wait_ge(bank_free, F_RWKV)
            for g in range(6):
                c = g // 2
                hi, lo = (u_hi, u_lo) if c % 2 else (a_hi, a_lo)
                for q in range(4):
                    tm_unit(U_RWKV + 4 * g + q, g, hi, lo, q, ready=(xs_ready, 8 * c) if g % 2 == 0 else None)
            pe.wait_ge(tm_free, 20)
            for j, c in enumerate((3, 4, 5, 5)):
                hi, lo = (u_hi, u_lo) if c % 2 else (a_hi, a_lo)
                fm_unit(U_RWKV + 24 + j, F_RWKV + j, hi, lo, ready=(xs_ready, 8 * c, 0) if j < 3 else None)
            pe.wait_ge(tm_free, 24)
            pe.wait_ge(lora_in, 16)
            for i in range(24):
                kind, t, half = i // 8, i % 8 // 2, i % 2
                if i % 8 == 0:
                    pe.wait_ge(lora_act, (1, 1, 3)[kind])
                    pe.wait_ge(bank_free, F_RWKV + (1, 2, 4)[kind])
                if i >= 4:
                    pe.wait_ge(lora_read, i - 3)
                cols, at = slice(half * T, half * T + T), slice(t * P, t * P + P)
                if kind < 2:
                    mm = nc.tensor.matmul(ps[:, 4 + i % 4], lora[0:65, kind, at], lora2[0:65, kind, cols], start=True, stop=True)
                else:
                    nc.tensor.matmul(ps[:, 4 + i % 4], lora[:, 2, at], lora2[:, 2, cols], start=True, stop=False)
                    mm = nc.tensor.matmul(ps[:, 4 + i % 4], lora[0:32, 3, at], lora2[0:32, 3, cols], start=False, stop=True)
                mm.then_inc(lora_ps, 1)
            pe.wait_ge(lora_read, 24)
            pe.wait_ge(bank_free, F_RWKV + 4)
            heads = [(e, p) for e in range(2) for p in range(2)]

            def quarter(e, p):
                return slice((2 * e + p) * P, (2 * e + p + 1) * P)

            def core_decay(r, first):
                pe.wait_ge(rin_f_in, 16 * r + 16)
                if not first:
                    pe.wait_ge(act_front, ACT_FRONT.value("bv", r - 1))
                sg = rin_f[:, 2]
                nc.tensor.matmul(ps[:, B_M2[0], 0:256], tri[:, 0], sg, start=True, stop=True)
                nc.tensor.matmul(ps[:, B_M2[0], 256:512], tri[:, 1], sg, start=True, stop=True).then_inc(pe_front, 1)
                if not first:
                    pe.wait_ge(dve_front, DVE_FRONT.value("t0_1", r - 1))
                for p in range(2):
                    mm = nc.tensor.matmul(ps[:, B_M2[1], 2 * p:2 * p + 2], sg[:, p * P:(p + 1) * P], chunk_sum[:, 0], start=True, stop=True)
                mm.then_inc(pe_front, 1)

            def core_turn(r, b):
                pe.wait_ge(dve_front, DVE_FRONT.value("rho", r))
                for p in range(2):
                    for w, src in enumerate((al_t[:, b], front_t[:, RHO])):
                        tr = nc.tensor.transpose(ps[:, B_M2[0], (2 * p + w) * P:(2 * p + w + 1) * P], src[:, p * P:(p + 1) * P], ident[:])
                tr.then_inc(pe_front, 1)
                pe.wait_ge(dve_front, DVE_FRONT.value("ka", r))
                pe.wait_ge(act_front, ACT_FRONT.value("pc", r))
                for w in range(2):
                    for p in range(2):
                        tr = nc.tensor.transpose(ps[:, B_M2[1], (2 * w + p) * P:(2 * w + p + 1) * P], be_ka[:, b, w, p * P:(p + 1) * P], ident[:])
                tr.then_inc(pe_front, 1)

            def core_m1(r, b, old):
                pe.wait_ge(act_front, ACT_FRONT.value("bk", r))
                if old:
                    pe.wait_ge(dve_back, DVE_BACK.value("y", r - 2))
                for e, p in heads:
                    rows = slice(64 * e, 64 * e + 64)
                    mm = nc.tensor.matmul(ps[:, B_M1[e], 256 * p:256 * p + 256], bkT[rows, 0, p], arT[rows, b, p], start=True, stop=True)
                mm.then_inc(pe_front, 1)

            def core_m2(r, b):
                for e, p in heads:
                    rows = slice(64 * e, 64 * e + 64)
                    mm = nc.tensor.matmul(ps[:, B_M2[e], 256 * p:256 * p + 256], bkT[rows, 1, p], arT[rows, b, p], start=True, stop=True)
                mm.then_inc(pe_front, 1)

            def core_a(r, b, old):
                pe.wait_ge(dve_front, DVE_FRONT.value("m2_1", r))
                if old:
                    pe.wait_ge(dve_back, DVE_BACK.value("o_lo", r - 2))
                for e, p in heads:
                    rows = slice(64 * e, 64 * e + 64)
                    mm = nc.tensor.matmul(ps[:, B_A[e], P * p:P * p + P], arT[rows, b, p, 0], bkT[rows, 0, p], start=True, stop=True)
                mm.then_inc(pe_front, 1)

            def core_bv(r, b):
                for e, p in heads:
                    mm = nc.tensor.matmul(ps[:, B_M2[0], quarter(e, p)], m2[:, b, e, p, 0], rin_f[:, 4, p * P:(p + 1) * P], start=True, stop=True)
                mm.then_inc(pe_front, 1)

            def core_level(r, b, lv, first=False):
                if lv > 1:
                    pe.wait_ge(dve_inv, DVE_INV.value(f"t{lv - 1}", r))
                else:
                    pe.wait_ge(dve_front, DVE_FRONT.value("tt0_1", r))
                if lv == 1 and not first:
                    pe.wait_ge(act_inv, ACT_INV.value("ta", r - 1))
                for e, p in heads:
                    mm = nc.tensor.matmul(ps[:, B_W, quarter(e, p)], m1[:, b, e, p, 0], Tm[:, b, 2 * e + p], start=True, stop=True)
                mm.then_inc(pe_inv, 1)

            def core_level_2(r, b, lv, first=False):
                pe.wait_ge(act_inv, ACT_INV.value(f"w{lv}", r))
                if lv > 1:
                    pe.wait_ge(dve_inv, DVE_INV.value(f"tt{lv - 1}", r))
                if lv == 1 and not first:
                    pe.wait_ge(dve_inv, DVE_INV.value("u0_1", r - 1))
                if lv < 5:
                    for e, p in heads:
                        mm = nc.tensor.matmul(ps[:, B_TW, quarter(e, p)], TT[:, b, 2 * e + p], Wm[:, 2 * e + p], start=True, stop=True)
                    mm.then_inc(pe_inv, 1)
                for e, p in heads:
                    mm = nc.tensor.matmul(ps[:, B_WT, quarter(e, p)], Wm[:, 2 * e + p], TT[:, b, 2 * e + p], start=True, stop=True)
                mm.then_inc(pe_inv, 1)

            def core_solved(r, b):
                pe.wait_ge(dve_inv, DVE_INV.value("tt5", r))
                pe.wait_ge(act_front, ACT_FRONT.value("bv", r))
                for e, p in heads:
                    mm = nc.tensor.matmul(ps[:, B_TW, quarter(e, p)], TT[:, b, 2 * e + p], bv[:, b, 2 * e + p], start=True, stop=True)
                mm.then_inc(pe_inv, 1)
                for e, p in heads:
                    mm = nc.tensor.matmul(ps[64 * e:64 * e + 64, B_W, P * p:P * p + P], al_t[:, b, P * p + 64 * e:P * p + 64 * e + 64],
                                          TT[:, b, 2 * e + p], start=True, stop=True)
                mm.then_inc(pe_inv, 1)

            def core_read_state(r, b, g, c, more):
                if c:
                    pe.wait_ge(dve_back, DVE_BACK.value("s1_c0", r))
                else:
                    pe.wait_ge(act_inv, ACT_INV.value("ta", r))
                    if more:
                        pe.wait_ge(dve_front, DVE_FRONT.value("tt0_1", r + 1))
                rows = slice(64 * c, 64 * c + 64)
                for p in range(2):
                    mm = nc.tensor.matmul(ps[rows, B_UY, P * p:P * p + P], taT[:, p, rows], S[:, g, p], start=True, stop=True)
                mm.then_inc(pe_back, 1)
                for p in range(2):
                    mm = nc.tensor.matmul(ps[rows, B_UY, 256 + P * p:256 + P * p + P], arT[:, b, p, 1, rows], S[:, g, p], start=True, stop=True)
                mm.then_inc(pe_back, 1)

            def core_write_state(r, b, c):
                if c == 0:
                    pe.wait_ge(rin_b_in, 16 * r + 16)
                pe.wait_ge(dve_back, DVE_BACK.value(f"u_c{c}", r))
                rows = slice(64 * c, 64 * c + 64)
                for p in range(2):
                    cols, dst = slice(P * p, P * p + P), ps[:, B_S, 256 * c + P * p:256 * c + P * p + P]
                    nc.tensor.matmul(dst, be_ka[rows, b, 0, cols], U[rows, p], start=True, stop=False)
                    mm = nc.tensor.matmul(dst, be_ka[rows, b, 1, cols], rin_b[rows, 0, cols], start=False, stop=True)
                mm.then_inc(pe_back, 1)

            def core_yh(r, b):
                for e, p in heads:
                    o = ps[:, B_YH, quarter(e, p)]
                    nc.tensor.matmul(o, m2[:, b, e, p, 1], rin_b[:, 0, P * p:P * p + P], start=True, stop=False)
                    mm = nc.tensor.matmul(o, m1[:, b, e, p, 1], U[:, p], start=False, stop=True)
                mm.then_inc(pe_back, 1)

            def core_out(r):
                pe.wait_ge(dve_back, DVE_BACK.value("o", r))
                for p in range(2):
                    tr = nc.tensor.transpose(ps[:, B_S, P * p:P * p + P], back_t[:, OUT, P * p:P * p + P], ident[:])
                tr.then_inc(pe_back, 1)

            def core_round(t, g, front, inv):
                n, b = GROUPS * t + g, g % 2
                r, q = n + 2, 1 - b
                core_read_state(n, b, g, 0, inv)
                if inv:
                    core_level(n + 1, q, 1)
                core_write_state(n, b, 0)
                if inv:
                    core_level_2(n + 1, q, 1)
                core_read_state(n, b, g, 1, inv)
                if inv:
                    core_level(n + 1, q, 2)
                core_write_state(n, b, 1)
                if inv:
                    core_level_2(n + 1, q, 2)
                core_yh(n, b)
                if front:
                    core_decay(r, False)
                if inv:
                    core_level(n + 1, q, 3)
                    core_level_2(n + 1, q, 3)
                    core_level(n + 1, q, 4)
                if front:
                    core_turn(r, b)
                if inv:
                    core_level_2(n + 1, q, 4)
                if front:
                    core_m1(r, b, True)
                core_out(n)
                if inv:
                    core_level(n + 1, q, 5)
                if front:
                    core_m2(r, b)
                if inv:
                    core_level_2(n + 1, q, 5)
                if front:
                    core_a(r, b, True)
                    core_bv(r, b)
                if inv:
                    core_solved(n + 1, q)

            for r in range(2):
                core_decay(r, r == 0)
                core_turn(r, r)
                core_m1(r, r, False)
                core_m2(r, r)
                if r:
                    pe.wait_ge(dve_front, DVE_FRONT.value("tt0_1", r - 1))
                core_a(r, r, False)
                core_bv(r, r)
            for lv in range(1, 6):
                core_level(0, 0, lv, True)
                core_level_2(0, 0, lv, True)
            core_solved(0, 0)
            pe.wait_ge(state_zero, 1)
            with pe.Fori(0, NT - 1) as t:
                for g in range(GROUPS):
                    core_round(t, g, True, True)
            for g in range(GROUPS):
                core_round(NT - 1, g, g < 2, g < 3)
            pe.wait_ge(dve_back, DVE_BACK.value("o_lo", ROUNDS - 1))
            proj(U_RWKV_O, F_RWKV_O, None)
            norm_sum(3)
            mlp(U_MLP1, F_MLP1, 32, 3 - 1)
            norm_sum(4)
            norm_sum(5)
            ffn(U_FFN1, F_FFN1, H_FFN1, 3)
            norm_sum(6)
            with pe.Fori(0, 2) as i:
                for j in range(12):
                    fm_unit(U_MIX + j, F_MIX + j, a_hi, a_lo, 12 * i, 12 * i, ready=(a_ready, KT * 4, 0) if j == 0 else None)
            pe.wait_ge(bank_free, F_MIX + 24)
            for g in range(6, 12):
                for q in range(4):
                    tm_unit(U_MIX + 24 + 4 * (g - 6) + q, g, a_hi, a_lo, q)
            pe.wait_ge(silu_ready, 4)
            fm_unit(U_MIX + 48, F_MIX + 24, a_hi, a_lo, nk=4, last=False)
            fm_unit(U_MIX + 49, F_MIX + 24, a_hi, a_lo, nk=4, k0=4, first=False)
            pe.wait_ge(silu_ready, 8)
            pe.wait_ge(gate_in, 16)
            pe.wait_ge(bank_free, F_MIX + 25)
            for t in range(NT):
                nc.tensor.matmul(ps[:, 4 + t], glr[0:33, t * P:(t + 1) * P], gate_up[0:33], start=True, stop=True).then_inc(la_ps, 1)
            for j in range(16):
                fm_unit(U_MIX + 50 + j, F_GATES + j, a_hi, a_lo)
            for j in range(8):
                fm_unit(U_MIX + 66 + j, F_GATES + 16 + j, u_hi, u_lo, ready=(u_ready, H_CONV, 0) if j == 0 else None)
            pe.wait_ge(bank_free, F_GLA_O)
            pe.wait_ge(la_ready, 4)
            with pe.Fori(0, 4) as h:
                with pe.Fori(0, 2) as tp:
                    for s in range(2):
                        n = 4 * h + 2 * tp + s

                        def after(sem_, steps, name):
                            pe.wait_ge(sem_, steps.value(name, n))

                        v_, la = gin[:, s, 256:512], gin[:, s, 768:896]
                        pe.wait_ge(gin_in[s], 32 * h + 16 * tp + 16)
                        for w in range(3):
                            nc.tensor.matmul(ps[:, 0, w * P:(w + 1) * P], tri[:, 2 + w], la, start=True, stop=True)
                        nc.tensor.matmul(ps[:, 0, 384:386], la, chunk_sum[:, 1], start=True, stop=True).then_inc(pe_gla, 1)
                        after(dve_gla, DVE_GLA, "qi")
                        for w in range(3):
                            tr = nc.tensor.transpose(ps[:, 1, w * P:(w + 1) * P], gqk[:, w], ident[:])
                        tr.then_inc(pe_gla, 1)
                        after(act_gla, ACT_GLA, "gT")
                        nc.tensor.matmul(ps[:, 2, 0:P], gT[:, 1], gT[:, 0], start=True, stop=True).then_inc(pe_gla, 1)
                        after(dve_gla, DVE_GLA, "ks")
                        for c in range(2):
                            rows = slice(64 * c, 64 * c + 64)
                            nc.tensor.matmul(ps[:, 4 + c, 0:256], gqk[rows, 3], v_[rows], start=True, stop=True).then_inc(pe_gla, 1)
                        after(dve_gla, DVE_GLA, "mask")
                        if s == 0:
                            pe.wait_ge(st_zero, h + 1)
                        for c in range(2):
                            rows = slice(64 * c, 64 * c + 64)
                            if c:
                                after(dve_gla, DVE_GLA, "st0")
                            nc.tensor.matmul(ps[rows, 3, 0:256], gT[:, 2, rows], St[:], start=True, stop=False)
                            nc.tensor.matmul(ps[rows, 3, 0:256], scT[:, rows], v_, start=False, stop=True).then_inc(pe_gla, 1)
                        after(dve_gla, DVE_GLA, "out")
                        for p in range(2):
                            tr = nc.tensor.transpose(ps[:, 6, P * p:P * p + P], gout[:, P * p:P * p + P], ident[:])
                        tr.then_inc(pe_gla, 1)
                        after(dve_gla, DVE_GLA, "o_lo")
            proj(U_GLA_O, F_GLA_O, None)
            proj(U_MIX_O, F_MIX_O, (u_ready, H_MERGED, 0), u_hi, u_lo)
            norm_sum(7)
            ffn(U_FFN2, F_FFN2, H_FFN2, 5)
            norm_sum(8)

        @block.scalar
        def _(act):
            def split_hi(m, off=0):
                if isinstance(off, int) and m + off >= U_END:
                    return
                act.wait_ge(raw_in[(m // 2) % 2], 16 * (m // 4 + 1) + 4 * off)
                if m >= SPLITS:
                    act.wait_ge(unit_done, m - 3 + off)
                nc.scalar.copy(w_hi[:, m % SPLITS], raw[:, (m // 2) % 2, (m % 2) * UNIT:(m % 2 + 1) * UNIT])\
                    .then_inc(hi_ready, 1)

            def norm(n, f):
                if f:
                    act.wait_ge(bank_free, f)
                else:
                    act.wait_ge(x_in, 16 * 13)
                for k in range(KT):
                    if k >= 4:
                        act.wait_ge(summed, KT * n + k - 3)
                    nc.scalar.activation(ep[:, k % 4], x[:, k], ACT.Square).then_inc(squared, 1)
                act.wait_ge(summed, KT * (n + 1))
                nc.scalar.activation(rstd[:], ps[:, 7], ACT.Sqrt, bias=EPS, scale=1.0 / D).then_inc(rooted, 1)

            def norm_hi(na, u):
                if u:
                    act.wait_ge(unit_done, u)
                for k in range(KT):
                    act.wait_ge(normed, KT * na + k + 1)
                    nc.scalar.copy(a_hi[:, k], h32[:, k % 3]).then_inc(a_hi_ready, 1)

            def hidden_hi(m, f, j, off=0, foff=0):
                act.wait_ge(bank_free, f + 1 + foff)
                nc.scalar.copy(u_hi[:, j], ep[:, 2 + j % 2]).then_inc(u_hi_ready, 1)

            def mlp(u, f):
                with act.Fori(0, 4) as i:
                    off = 16 * i
                    for j in range(8):
                        split_hi(u + j + AHEAD, off)
                        act.wait_ge(unit_done, u + j + 1 + off)
                        nc.scalar.activation(ep[:, j % 2], ps[:, (f + j) % 4], ACT.Relu).then_inc(ep_act, 1)
                        hidden_hi(u + j, f + j, j, off, off)
                    for j in range(8):
                        split_hi(u + 8 + j + AHEAD, off)

            def ffn(u, f):
                def chunk(size, u, f, off):
                    for q in range(0, 2 * size, 4):
                        for e in range(2):
                            split_hi(u + q + e + AHEAD, off)
                            act.wait_ge(unit_done, u + q + e + 1 + off)
                            nc.scalar.activation(ep[:, e], ps[:, (f + q + e) % 4], ACT.Sigmoid).then_inc(ep_act, 1)
                        for e in range(2):
                            split_hi(u + q + 2 + e + AHEAD, off)
                            hidden_hi(u + q + 2 + e, f + q + 2 + e, q // 2 + e, off, off)
                    for j in range(8):
                        split_hi(u + 2 * size + j + AHEAD, off)

                with act.Fori(0, 2) as i:
                    chunk(8, u, f, 24 * i)
                chunk(6, u + 48, f + 48, 0)

            for m in range(AHEAD):
                split_hi(m)
            norm(0, 0)
            norm_hi(0, 0)

            def swap_halves(j, r, rows):
                act.wait_ge(unit_done, j + 1)
                if r >= 2:
                    act.wait_ge(roped, r - 1)
                for q in range(0, rows, 32):
                    nc.scalar.copy(swap[q ^ 32:(q ^ 32) + 32, r % 2], ps[q:q + 32, (F_DSA + j) % 4 if j < 16 else F_DSA % 4])\
                        .then_inc(swap_ready, 1)

            r = 0
            for j in range(16):
                split_hi(j + AHEAD)
                if j in (10, 11):
                    continue
                else:
                    swap_halves(j, r, P)
                    r += 1
            split_hi(16 + AHEAD)
            split_hi(17 + AHEAD)
            swap_halves(17, r, 64)
            for j in range(2):
                act.wait_ge(vt_ps, 1)
                nc.scalar.copy(v_tm[:, 2 * j:2 * j + 2], ps[:, 4 + j].rearrange("p (t n) -> p t n", t=2)).then_inc(v_read, 1)
            for i in range(24):
                n = (2 + i // 8) * P
                act.wait_ge(idx_ps, i + 1)
                if i >= 2:
                    act.wait_ge(idx_added, i - 1)
                nc.scalar.activation(ep[:, i % 2, 0:n], ps[:, 4 + i % 2, 0:n], ACT.Relu).then_inc(idx_relu, 1)

            def probs(n):
                w = (n // 16 + 1) * P
                act.wait_ge(lg_bias, n + 1)
                nc.scalar.activation(prob[:, n % 3, 0:w], prob[:, n % 3, 0:w], ACT.Exp, bias=stat[:, 1, n:n + 1],
                                     scale=0.125, accum_out=stat[:, 2, n:n + 1]).then_inc(exp_ready, 1)

            def turned(n):
                w = (n // 16 + 1) * P
                act.wait_ge(tr_ps, n + 1)
                if n >= 2:
                    act.wait_ge(o_ps, n - 1)
                nc.scalar.copy(probT[:, n % 2, 0:w], ps[:, 6 + n % 2, 0:w]).then_inc(probT_ready, 1)

            def out_hi(g):
                act.wait_ge(o_ps, 8 * g + 8)
                nc.scalar.copy(a_hi[:, 4 * (g % 2):4 * (g % 2) + 4, (g // 2) * P:(g // 2 + 1) * P],
                               ps[:, g % 2].rearrange("p (j t) -> p j t", j=4)).then_inc(o_hi, 1)

            for n in range(66):
                if n < 64:
                    probs(n)
                if 1 <= n < 65:
                    turned(n - 1)
                if n >= 10 and (n - 10) % 8 == 0:
                    out_hi((n - 10) // 8)
            out_hi(7)
            for j in range(N_PROJ):
                split_hi(U_DSA_O + j + AHEAD)
            norm(1, F_MLP0)
            norm_hi(1, U_MLP0)
            mlp(U_MLP0, F_MLP0)
            norm(2, F_RWKV)

            def mixed_hi(c, k):
                if k == 0:
                    act.wait_ge(unit_done, U_RWKV + (0, 0, 8, 16, 24, 25)[c])
                act.wait_ge(xs32, 8 * c + k + 1)
                nc.scalar.copy((u_hi if c % 2 else a_hi)[:, k], h32[:, (8 * c + k) % 3]).then_inc(xs_hi, 1)

            for k in range(KT):
                mixed_hi(0, k)
            for g in range(6):
                for q in range(4):
                    split_hi(U_RWKV + 4 * g + q + AHEAD)
                    mixed_hi(g // 2 + 1, (4 * g + q) % 8)
                act.wait_ge(unit_done, U_RWKV + 4 * g + 4)
                for t in range(NT):
                    if g:
                        act.wait_ge(spill[t], 16 * g)
                    nc.scalar.copy(ep[:, t], ps[:, 4 * (g % 2) + t]).then_inc(tm_free, 1)
            split_hi(U_RWKV + 24 + AHEAD)
            for k in range(KT):
                mixed_hi(4, k)
            split_hi(U_RWKV + 25 + AHEAD)
            for k in range(KT):
                mixed_hi(5, k)
            split_hi(U_RWKV + 26 + AHEAD)
            split_hi(U_RWKV + 27 + AHEAD)
            act.wait_ge(bank_free, F_RWKV + 1)
            nc.scalar.activation(lora[0:64, 0], lora[0:64, 0], ACT.Tanh).then_inc(lora_act, 1)
            act.wait_ge(bank_free, F_RWKV + 3)
            nc.scalar.activation(lora[:, 2], lora[:, 2], ACT.Sigmoid).then_inc(lora_act, 1)
            act.wait_ge(bank_free, F_RWKV + 4)
            nc.scalar.activation(lora[0:32, 3], lora[0:32, 3], ACT.Sigmoid).then_inc(lora_act, 1)
            for i in range(24):
                act.wait_ge(lora_ps, i + 1)
                act.wait_ge(spill[i % 4], 16 * (6 + i // 4))
                nc.scalar.activation(ep[:, i % 4], ps[:, 4 + i % 4], ACT.Sigmoid if i < 16 else ACT.Copy).then_inc(lora_read, 1)
            def core_exps(r, b, old):
                act.wait_ge(pe_front, PE_FRONT.value("decay", r))
                nc.scalar.activation(ex[:, 0], ps[:, B_M2[0], 0:256], ACT.Exp).then_inc(act_front, 1)
                nc.scalar.activation(ex[:, 1], ps[:, B_M2[0], 256:512], ACT.Exp).then_inc(act_front, 1)
                nc.scalar.activation(ex[:, 2], ps[:, B_M2[0], 0:256], ACT.Exp, scale=-1.0).then_inc(act_front, 1)
                act.wait_ge(pe_front, PE_FRONT.value("chunk_decay", r))
                if old:
                    act.wait_ge(dve_back, DVE_BACK.value("s1_c1", r - 2))
                nc.scalar.activation(pc[:, b].rearrange("p a b -> p (a b)"), ps[:, B_M2[1], 0:4], ACT.Exp).then_inc(act_front, 1)

            def core_turned(r, b):
                act.wait_ge(pe_front, PE_FRONT.value("turn_ar", r))
                nc.scalar.copy(arT[:, b].rearrange("p a b c -> p (a b c)"), ps[:, B_M2[0]]).then_inc(act_front, 1)
                act.wait_ge(pe_front, PE_FRONT.value("turn_bk", r))
                nc.scalar.copy(bkT[:].rearrange("p a b c -> p (a b c)"), ps[:, B_M2[1]]).then_inc(act_front, 1)

            def core_bv(r, b):
                act.wait_ge(pe_front, PE_FRONT.value("bv", r))
                nc.scalar.copy(bv[:, b].rearrange("p a b -> p (a b)"), ps[:, B_M2[0]]).then_inc(act_front, 1)

            def core_level(r, lv):
                act.wait_ge(pe_inv, PE_INV.value(f"w{lv}", r))
                nc.scalar.copy(Wm[:].rearrange("p a b -> p (a b)"), ps[:, B_W]).then_inc(act_inv, 1)

            def core_ta(r):
                act.wait_ge(pe_inv, PE_INV.value("ta", r))
                nc.scalar.copy(taT[:].rearrange("p a b -> p (a b)"), ps[:, B_W, 0:256]).then_inc(act_inv, 1)

            def core_yh(r):
                act.wait_ge(pe_back, PE_BACK.value("yh", r))
                for e in range(2):
                    nc.scalar.copy(yh[:, :, e], ps[:, B_YH, 256 * e:256 * e + 256].rearrange("p (a b) -> p a b", a=2)[:, :, 64 * e:64 * e + 64])\
                        .then_inc(act_back, 1)

            def core_out(r, t, g):
                act.wait_ge(pe_back, PE_BACK.value("turn_o", r))
                cols = slice(P * t, P * t + P) if isinstance(t, int) else bass.ds(P * t, P)
                nc.scalar.copy(a_hi[:, 2 * g:2 * g + 2, cols], ps[:, B_S, 0:256].rearrange("p (a b) -> p a b", a=2)).then_inc(act_back, 1)

            def core_round(t, g, front, inv):
                n, b = GROUPS * t + g, g % 2
                if inv:
                    core_level(n + 1, 1)
                    core_level(n + 1, 2)
                core_yh(n)
                if front:
                    core_exps(n + 2, b, True)
                if inv:
                    core_level(n + 1, 3)
                    core_level(n + 1, 4)
                if front:
                    core_turned(n + 2, b)
                core_out(n, t, g)
                if inv:
                    core_level(n + 1, 5)
                if front:
                    core_bv(n + 2, b)
                if inv:
                    core_ta(n + 1)

            for r in range(2):
                core_exps(r, r, False)
                core_turned(r, r)
                core_bv(r, r)
            for lv in range(1, 6):
                core_level(0, lv)
            core_ta(0)
            with act.Fori(0, NT - 1) as t:
                for g in range(GROUPS):
                    core_round(t, g, True, True)
            for g in range(GROUPS):
                core_round(NT - 1, g, g < 2, g < 3)
            for j in range(N_PROJ):
                split_hi(U_RWKV_O + j + AHEAD)
            norm(3, F_MLP1)
            norm_hi(2, U_MLP1)
            mlp(U_MLP1, F_MLP1)
            norm(4, F_FFN1)
            act.wait_ge(x_scaled, KT)
            norm(5, F_FFN1)
            norm_hi(3, U_FFN1)
            ffn(U_FFN1, F_FFN1)
            norm(6, F_MIX)
            norm_hi(4, U_MIX)
            with act.Fori(0, 2) as i:
                for j in range(12):
                    split_hi(U_MIX + j + AHEAD, 12 * i)
                    if j % 6 >= 4:
                        tile = 2 * (j // 6) + j % 2
                        act.wait_ge(bank_free, F_MIX + j + 1 + 12 * i)
                        nc.scalar.copy(u_hi[:, bass.ds(4 * i + tile, 1)].rearrange("p o t -> p (o t)"), ep[:, 2 + j % 2]).then_inc(u_hi_ready, 1)
            for g in range(6, 12):
                for q in range(4):
                    split_hi(U_MIX + 4 * g + q + AHEAD)
                act.wait_ge(unit_done, U_MIX + 4 * g + 4)
                for t in range(NT):
                    if g > 6:
                        act.wait_ge(spill[t], 16 * (6 + g))
                    if g < 10:
                        nc.scalar.copy(ep[:, t], ps[:, 4 * (g % 2) + t]).then_inc(tm_free, 1)
                    else:
                        nc.scalar.activation(ep[:, t], ps[:, 4 * (g % 2) + t], ACT.Sigmoid).then_inc(tm_free, 1)
            split_hi(U_MIX + 48 + AHEAD)
            split_hi(U_MIX + 49 + AHEAD)
            for t in range(NT):
                act.wait_ge(la_ps, t + 1)
                act.wait_ge(spill[t], 16 * 18)
                nc.scalar.activation(ep[:, t], ps[:, 4 + t], ACT.Abs).then_inc(la_act, 1)
            for t in range(NT):
                act.wait_ge(la_act, t + 1)
                nc.scalar.activation(ep[:, t], ep[:, t], ACT.Exp, scale=-1.0).then_inc(la_act, 1)
            act.wait_ge(la_act, 8)
            for t in range(NT):
                nc.scalar.activation(ep[:, t], ep[:, t], ACT.Ln, bias=1.0).then_inc(la_act, 1)
            for j in range(16):
                split_hi(U_MIX + 50 + j + AHEAD)
                gate = (merged if j < 8 else sig_b)[:, j % 8]
                act.wait_ge(bank_free, F_GATES + j + 1)
                nc.scalar.activation(gate, gate, ACT.Sigmoid).then_inc(gated, 1)
            for j in range(8):
                split_hi(U_MIX + 66 + j + AHEAD)
            with act.Fori(0, 4) as h:
                with act.Fori(0, 2) as tp:
                    for s in range(2):
                        n = 4 * h + 2 * tp + s

                        def after(name):
                            act.wait_ge(pe_gla, PE_GLA.value(name, n))

                        after("decay")
                        nc.scalar.activation(gex[:, 0:3].rearrange("p a b -> p (a b)"), ps[:, 0, 0:384], ACT.Exp).then_inc(act_gla, 1)
                        nc.scalar.activation(gex[:, 3], ps[:, 0, 0:P], ACT.Exp, scale=-1.0).then_inc(act_gla, 1)
                        nc.scalar.activation(gdc[:], ps[:, 0, 384:386], ACT.Exp).then_inc(act_gla, 1)
                        after("turn")
                        nc.scalar.copy(gT[:].rearrange("p a b -> p (a b)"), ps[:, 1, 0:384]).then_inc(act_gla, 1)
                        after("o1")
                        nc.scalar.activation(gsq[:], ps[:, 3, 0:256], ACT.Square, accum_out=gst[:, 0:1]).then_inc(act_gla, 1)
                        after("turn_o")
                        nc.scalar.copy(a_hi[:, bass.ds(2 * h, 2), bass.ds(2 * P * tp + P * s, P)],
                                       ps[:, 6, 0:256].rearrange("p (a b) -> p a b", a=2)).then_inc(act_gla, 1)
            for j in range(8):
                split_hi(U_GLA_O + j + AHEAD)
                act.wait_ge(merged_ready, j + 1)
                nc.scalar.copy(u_hi[:, j], merged[:, j]).then_inc(u_hi_ready, 1)
            for j in range(8):
                split_hi(U_MIX_O + j + AHEAD)
            norm(7, F_FFN2)
            norm_hi(5, U_FFN2)
            ffn(U_FFN2, F_FFN2)
            norm(8, F_FFN2 + N_FFN)

        @block.vector
        def _(dve):
            chain = Tally(dve, dve_chain)

            def split_lo(m, off=0):
                if isinstance(off, int) and m + off >= U_END:
                    return
                dve.wait_ge(hi_ready, m + 1 + off)
                nc.vector.tensor_tensor(w_lo[:, m % SPLITS], raw[:, (m // 2) % 2, (m % 2) * UNIT:(m % 2 + 1) * UNIT],
                                        w_hi[:, m % SPLITS], ALU.subtract).then_inc(split_ready, 1)

            def norm_lo(n, na, col):
                dve.wait_ge(rooted, n + 1)
                chain.mark(nc.vector.reciprocal(rstd[:], rstd[:]))
                chain.wait()

                def low(k):
                    dve.wait_ge(a_hi_ready, KT * na + k + 1)
                    nc.vector.tensor_tensor(a_lo[:, k], h32[:, k % 3], a_hi[:, k], ALU.subtract).then_inc(a_ready, 1)

                for k in range(KT):
                    if k >= 3:
                        dve.wait_ge(a_ready, KT * na + k - 2)
                    nc.vector.scalar_tensor_tensor(h32[:, k % 3], x[:, k], vec[:, col, k:k + 1], rstd[:],
                                                   ALU.mult, ALU.mult).then_inc(normed, 1)
                    if k:
                        low(k - 1)
                low(KT - 1)

            def scale_x(n, col, count):
                dve.wait_ge(rooted, n + 1)
                chain.mark(nc.vector.reciprocal(rstd[:], rstd[:]))
                chain.wait()
                for k in range(KT):
                    nc.vector.scalar_tensor_tensor(x[:, k], x[:, k], vec[:, col, k:k + 1], rstd[:], ALU.mult, ALU.mult)\
                        .then_inc(x_scaled, 1)
                dve.wait_ge(x_scaled, count)

            def add_x(m, f, j, off=0, foff=0, scale=None):
                dve.wait_ge(unit_done, m + 1 + off)
                if scale is None:
                    nc.vector.tensor_tensor(x[:, j], ps[:, f % 4], x[:, j], ALU.add).then_inc(bank_free, 1)
                else:
                    nc.vector.scalar_tensor_tensor(x[:, j], ps[:, f % 4], scale, x[:, j], ALU.mult, ALU.add)\
                        .then_inc(bank_free, 1)

            def hidden_lo(h, j, hoff=0):
                dve.wait_ge(u_hi_ready, h + j + 1 + hoff)
                nc.vector.tensor_tensor(u_lo[:, j], ep[:, 2 + j % 2], u_hi[:, j], ALU.subtract).then_inc(u_ready, 1)

            def proj(u, f):
                for j in range(N_PROJ):
                    split_lo(u + j + AHEAD)
                    add_x(u + j, f + j, j)

            def mlp(u, f, h, e):
                with dve.Fori(0, 4) as i:
                    off, hoff = 16 * i, 8 * i
                    for j in range(8):
                        split_lo(u + j + AHEAD, off)
                        dve.wait_ge(ep_act, e + j + 1 + hoff)
                        nc.vector.tensor_tensor(ep[:, 2 + j % 2], ep[:, j % 2], ps[:, (f + j) % 4], ALU.mult)\
                            .then_inc(bank_free, 1)
                        hidden_lo(h, j, hoff)
                    for j in range(8):
                        split_lo(u + 8 + j + AHEAD, off)
                        add_x(u + 8 + j, f + 8 + j, j, off, off)

            def ffn(u, f, h, e):
                def chunk(size, u, f, h, e, off, hoff):
                    for q in range(0, 2 * size, 4):
                        for s in range(2):
                            split_lo(u + q + s + AHEAD, off)
                            dve.wait_ge(ep_act, e + q // 2 + s + 1 + hoff)
                            if q:
                                dve.wait_ge(u_ready, h + q // 2 + s - 1 + hoff)
                            nc.vector.tensor_tensor(ep[:, 2 + s], ep[:, s], ps[:, (f + q + s) % 4], ALU.mult)\
                                .then_inc(bank_free, 1)
                        for s in range(2):
                            split_lo(u + q + 2 + s + AHEAD, off)
                            dve.wait_ge(unit_done, u + q + 3 + s + off)
                            dve.wait_ge(bank_free, f + q + s + 1 + off)
                            nc.vector.tensor_tensor(ep[:, 2 + s], ep[:, 2 + s], ps[:, (f + q + 2 + s) % 4], ALU.mult)\
                                .then_inc(bank_free, 1)
                            hidden_lo(h, q // 2 + s, hoff)
                    for j in range(8):
                        split_lo(u + 2 * size + j + AHEAD, off)
                        add_x(u + 2 * size + j, f + 2 * size + j, j, off, off, 0.5)

                with dve.Fori(0, 2) as i:
                    chunk(8, u, f, h, e, 24 * i, 8 * i)
                chunk(6, u + 48, f + 48, h + 16, e + 16, 0, 0)

            for m in range(AHEAD):
                split_lo(m)
            dve.wait_ge(x_in, 16 * 13)
            norm_lo(0, 0, V_MIX0)

            def rope(j, r, rows, swaps):
                dve.wait_ge(swap_ready, swaps)
                if r:
                    dve.wait_ge(roped, r)
                chain.mark(nc.vector.tensor_tensor(swap[0:rows, r % 2], swap[0:rows, r % 2], sin[0:rows], ALU.mult))
                if rows == 64:
                    nc.vector.tensor_copy(kiwi[0:72], ps[0:72, 0]).then_inc(kiwi_ready, 1)
                nc.vector.tensor_tensor(rope1[0:rows], ps[0:rows, j % 4], cos[0:rows], ALU.mult).then_inc(bank_free, 1)
                chain.wait()

            r = 0
            for j in range(16):
                split_lo(j + AHEAD)
                if j in (10, 11):
                    dve.wait_ge(unit_done, j + 1)
                    nc.vector.tensor_copy(vT[:, j - 10], ps[:, j % 4]).then_inc(bank_free, 1)
                    continue
                rope(j, r, P, 4 * (r + 1))
                dve.wait_ge(bank_free, j + 1)
                if j < 8 or j >= 12:
                    dst = qT[:, j] if j < 8 else qiT[:, j - 12]
                    nc.vector.tensor_tensor(dst, rope1[:], swap[:, r % 2], ALU.add).then_inc(roped, 1)
                else:
                    for s in range(2):
                        rows, other = slice(64 * s, 64 * s + 64), slice(64 - 64 * s, 128 - 64 * s)
                        chain.mark(nc.vector.tensor_tensor(kd[rows, 2 * (j - 8) + s], rope1[rows], swap[rows, r % 2], ALU.add))
                    chain.wait()
                    for s in range(2):
                        rows, other = slice(64 * s, 64 * s + 64), slice(64 - 64 * s, 128 - 64 * s)
                        cp = nc.vector.tensor_copy(kd[other, 2 * (j - 8) + s], kd[rows, 2 * (j - 8) + s])
                        if s == 0:
                            chain.mark(cp)
                        else:
                            cp.then_inc(roped, 1)
                    chain.wait()
                r += 1
            split_lo(16 + AHEAD)
            split_lo(17 + AHEAD)
            rope(16, r, 64, 4 * 14 + 2)
            dve.wait_ge(bank_free, 17)
            nc.vector.tensor_tensor(kid[0:64], rope1[0:64], swap[0:64, r % 2], ALU.add).then_inc(roped, 1)
            dve.wait_ge(roped, 15)
            nc.vector.tensor_copy(kid[64:128], kid[0:64]).then_inc(roped, 1)
            dve.wait_ge(vt_ps, 2)
            nc.vector.tensor_scalar(wi[:], ps[:, 6].rearrange("p (t n) -> p t n", t=4)[:, :, 64:72],
                                    float(512 ** -0.5), None, ALU.mult).then_inc(wi_read, 1)
            dve.wait_ge(wi_read, 1)
            chain.mark(nc.vector.tensor_copy(amask[:, 0, 0:P], causal[:]))
            for i in range(24):
                qb, h = 1 + i // 8, i % 8
                n = (qb + 1) * P
                dve.wait_ge(idx_relu, i + 1)
                if i:
                    dve.wait_ge(idx_added, i)
                if h == 0:
                    nc.vector.tensor_scalar(score[:, 0:n], ep[:, i % 2, 0:n], wi[:, qb, 0:1], None, ALU.mult).then_inc(idx_added, 1)
                else:
                    nc.vector.scalar_tensor_tensor(score[:, 0:n], ep[:, i % 2, 0:n], wi[:, qb, h:h + 1], score[:, 0:n],
                                                   ALU.mult, ALU.add).then_inc(idx_added, 1)
                if h < 7:
                    continue
                dve.wait_ge(idx_added, i + 1)
                chain.mark(nc.vector.copy_predicated(score[:, n - P:n], imask[:, 12], fill[:]))
                chain.wait()
                for rnd in range(TOPK // 8):
                    chain.mark(nc.vector.max(top8[:], score[:, 0:n]))
                    chain.wait()
                    chain.mark(nc.vector.match_replace(score[:, 0:n], top8[:], score[:, 0:n], SCORE_TAKEN))
                    chain.wait()
                chain.mark(nc.vector.tensor_scalar(amask[:, qb, 0:n], score[:, 0:n], -3.2e38, NEG, ALU.is_gt, ALU.mult))
                chain.wait()

            def peak(n):
                w = (n // 16 + 1) * P
                dve.wait_ge(lg_ps, n + 1)
                if n >= 3:
                    dve.wait_ge(tr_ps, n - 2)
                nc.vector.tensor_tensor_reduce(prob[:, n % 3, 0:w], ps[:, 4 + n % 2, 0:w], amask[:, n // 16, 0:w], 1.0, -3.0e38,
                                               ALU.add, ALU.max, stat[:, 0, n:n + 1]).then_inc(lg_read, 1)
                dve.wait_ge(lg_read, n + 1)
                nc.vector.tensor_scalar(stat[:, 1, n:n + 1], stat[:, 0, n:n + 1], -0.125, None, ALU.mult).then_inc(lg_bias, 1)

            def normalise(n):
                w = (n // 16 + 1) * P
                dve.wait_ge(exp_ready, n + 1)
                chain.mark(nc.vector.reciprocal(stat[:, 3, n:n + 1], stat[:, 2, n:n + 1]))
                chain.wait()
                nc.vector.tensor_scalar(prob[:, n % 3, 0:w], prob[:, n % 3, 0:w], stat[:, 3, n:n + 1], None, ALU.mult)\
                    .then_inc(prob_ready, 1)

            def out_lo(g):
                dve.wait_ge(o_hi, g + 1)
                at = (slice(None), slice(4 * (g % 2), 4 * (g % 2) + 4), slice((g // 2) * P, (g // 2 + 1) * P))
                nc.vector.tensor_tensor(a_lo[at], ps[:, g % 2].rearrange("p (j t) -> p j t", j=4), a_hi[at], ALU.subtract)\
                    .then_inc(o_ready, 1)

            for n in range(66):
                if n < 64:
                    peak(n)
                if 1 <= n < 65:
                    normalise(n - 1)
                if n >= 11 and (n - 11) % 8 == 0:
                    out_lo((n - 11) // 8)
            out_lo(7)
            proj(U_DSA_O, F_DSA_O)
            norm_lo(1, 1, V_MLP0)
            mlp(U_MLP0, F_MLP0, 0, 0)
            dve.wait_ge(unit_done, U_RWKV)
            chain.mark(nc.vector.memset(h_pad[:, :, 0:2], 0.0))
            chain.mark(nc.vector.memset(lora[64:65, 0:2], 1.0))
            chain.mark(nc.vector.tensor_scalar(mu1[:], vec[:, V_MU:V_MU + 6], -1.0, 1.0, ALU.mult, ALU.add))
            dve.wait_ge(rooted, 3)
            chain.mark(nc.vector.reciprocal(rstd[:], rstd[:]))
            chain.wait()
            for k in range(KT):
                chain.mark(nc.vector.scalar_tensor_tensor(h_pad[:, k, 2:T + 2], x[:, k], vec[:, V_MIX1, k:k + 1], rstd[:], ALU.mult, ALU.mult))
            chain.wait()

            def mixed(c, k):
                i = 8 * c + k
                if i >= 3:
                    dve.wait_ge(xs_ready, i - 2)
                chain.mark(nc.vector.tensor_scalar(h32[:, (8 * c + k) % 3], h_pad[:, k, 2:T + 2], mu1[:, c, k:k + 1], None, ALU.mult))
                chain.wait()
                nc.vector.scalar_tensor_tensor(h32[:, (8 * c + k) % 3], h_pad[:, k, 1:T + 1], vec[:, V_MU + c, k:k + 1], h32[:, (8 * c + k) % 3],
                                               ALU.mult, ALU.add).then_inc(xs32, 1)

            def mixed_lo(c, k):
                dve.wait_ge(xs_hi, 8 * c + k + 1)
                nc.vector.tensor_tensor((u_lo if c % 2 else a_lo)[:, k], h32[:, (8 * c + k) % 3], (u_hi if c % 2 else a_hi)[:, k],
                                        ALU.subtract).then_inc(xs_ready, 1)

            def mixed_all(c):
                for k in range(KT):
                    mixed(c, k)
                    if k:
                        mixed_lo(c, k - 1)
                mixed_lo(c, KT - 1)

            mixed_all(0)
            for m in range(24):
                split_lo(U_RWKV + m + AHEAD)
                mixed(m // 8 + 1, m % 8)
                mixed_lo(m // 8 + 1, m % 8)
            split_lo(U_RWKV + 24 + AHEAD)
            mixed_all(4)
            dve.wait_ge(unit_done, U_RWKV + 25)
            nc.vector.tensor_copy(lora[0:64, 0], ps[0:64, F_RWKV % 4]).then_inc(bank_free, 1)
            split_lo(U_RWKV + 25 + AHEAD)
            mixed_all(5)
            for j, (rows, slot) in enumerate(((64, 1), (P, 2), (32, 3))):
                if j:
                    split_lo(U_RWKV + 25 + j + AHEAD)
                dve.wait_ge(unit_done, U_RWKV + 26 + j)
                nc.vector.tensor_copy(lora[0:rows, slot], ps[0:rows, (F_RWKV + 1 + j) % 4]).then_inc(bank_free, 1)
            dve.wait_ge(prm_in, 16)
            for i in range(4):
                dve.wait_ge(spill[i], 16 * 12)
            nc.vector.memset(S[:], 0.0).then_inc(state_zero, 1)

            def predicated(cell, dst, mask, src):
                nc.vector.memset(gate[:, cell:cell + 1], 0.0)
                return nc.vector.copy_predicated(dst, mask, src)

            def tt(dst, a, b, op=ALU.mult):
                return nc.vector.tensor_tensor(dst, a, b, op)

            def stt(dst, a, sc, b, op0, op1):
                return nc.vector.scalar_tensor_tensor(dst, a, sc, b, op0, op1)

            def by_head(ap):
                return ap.rearrange("p (h d) -> p h d", h=4)

            F, B = [front_t[:, i] for i in range(8)], [back_t[:, i] for i in range(5)]
            r_, k_, _, a_, v_ = (rin_f[:, c] for c in range(5))

            def prm_(j, g):
                return prm[:, j, 256 * g:256 * g + 256]

            def own_front(name, r):
                dve.wait_ge(dve_front, DVE_FRONT.value(name, r))

            def core_keys(r, b, g):
                dve.wait_ge(rin_f_in, 16 * r + 16)
                tt(F[KKR], k_, prm_(0, g)).then_inc(dve_front, 1)
                own_front("kkr", r)
                tt(F[SQ], F[KKR], F[KKR]).then_inc(dve_front, 1)
                own_front("sq", r)
                nc.vector.tensor_reduce(hst[:, b, H_SS], by_head(F[SQ]), AX.X, ALU.add).then_inc(dve_front, 1)
                own_front("ss", r)
                nc.vector.tensor_scalar(hst[:, b, H_SSM], hst[:, b, H_SS], 1e-24, None, ALU.max).then_inc(dve_front, 1)

            def core_bonus(r, b, g):
                stt(F[TA], a_, -1.0, prm_(1, g), ALU.add, ALU.mult).then_inc(dve_front, 1)
                own_front("t", r)
                stt(F[KF], F[TA], 1.0, k_, ALU.add, ALU.mult).then_inc(dve_front, 1)
                own_front("kf", r)
                tt(F[RKF], r_, F[KF]).then_inc(dve_front, 1)
                own_front("rkf", r)
                tt(F[RKF], F[RKF], prm_(2, g)).then_inc(dve_front, 1)
                own_front("rkr", r)
                nc.vector.tensor_reduce(bs[:, g], by_head(F[RKF]), AX.X, ALU.add).then_inc(dve_front, 1)

            def core_scaled(r, b, old):
                dve.wait_ge(pool_front, POOL_FRONT.value("rn", r))
                tt(by_head(F[KK]), by_head(F[KKR]), over(hst[:, b, H_RN], 64)).then_inc(dve_front, 1)
                own_front("kk", r)
                tt(F[BB], F[KK], a_).then_inc(dve_front, 1)
                dve.wait_ge(act_front, ACT_FRONT.value("ex_neg", r))
                if old:
                    dve.wait_ge(pe_inv, PE_INV.value("ta", r - 2))
                stt(al_t[:, b], F[KK], -1.0, ex[:, 1], ALU.mult, ALU.mult).then_inc(dve_front, 1)
                tt(F[RHO], r_, ex[:, 0]).then_inc(dve_front, 1)
                own_front("b", r)
                tt(be_ka[:, b, 0], F[BB], ex[:, 2]).then_inc(dve_front, 1)
                tt(be_ka[:, b, 1], F[KF], ex[:, 2]).then_inc(dve_front, 1)

            both = strict_incl[:].rearrange("p (o a) b -> p o a b", o=1).to_broadcast([P, 2, 2, P])

            def core_masked(r, b, m, banks, name):
                dve.wait_ge(pe_front, PE_FRONT.value(name, r))
                for e in range(2):
                    tt(m[:, b, e], ps[:, banks[e]].rearrange("p (a b c) -> p a b c", a=2, b=2), both).then_inc(dve_front, 1)

            def core_start(r, b):
                dve.wait_ge(pool_front, POOL_FRONT.value("eye_tt", r))
                dve.wait_ge(pe_front, PE_FRONT.value("a", r))
                for e in range(2):
                    predicated(e, Tm[:, b, 2 * e:2 * e + 2], bcast(imask[:, 0], 2, P),
                               ps[:, B_A[e], 0:256].rearrange("p (a b) -> p a b", a=2)).then_inc(dve_front, 1)
                for e in range(2):
                    predicated(2 + e, TT[:, b, 2 * e:2 * e + 2], bcast(imask[:, 6], 2, P),
                               ps[:, B_M1[e]].rearrange("p (a b c) -> p a b c", a=2, b=2)[:, :, 0]).then_inc(dve_front, 1)

            def core_level(r, b, lv):
                if lv < 5:
                    dve.wait_ge(pe_inv, PE_INV.value(f"tw{lv}", r))
                    predicated(3 + lv, Tm[:, b], bcast(imask[:, lv], 4, P), ps[:, B_TW].rearrange("p (a b) -> p a b", a=4)).then_inc(dve_inv, 1)
                dve.wait_ge(pe_inv, PE_INV.value(f"wt{lv}", r))
                if lv == 1:
                    own_front("tt0_1", r)
                else:
                    dve.wait_ge(dve_inv, DVE_INV.value(f"tt{lv - 1}", r))
                predicated(8 + lv, TT[:, b], bcast(imask[:, 6 + lv], 4, P), ps[:, B_WT].rearrange("p (a b) -> p a b", a=4)).then_inc(dve_inv, 1)

            def core_u0(r):
                dve.wait_ge(pe_inv, PE_INV.value("u0", r))
                for e in range(2):
                    nc.vector.tensor_copy(u0[:, :, e], ps[:, B_TW, 256 * e:256 * e + 256].rearrange("p (a b) -> p a b", a=2)[:, :, 64 * e:64 * e + 64])\
                        .then_inc(dve_inv, 1)

            def own_back(name, r):
                dve.wait_ge(dve_back, DVE_BACK.value(name, r))

            def core_u(r, c):
                rows = slice(64 * c, 64 * c + 64)
                if c == 0:
                    dve.wait_ge(dve_inv, DVE_INV.value("u0_1", r))
                dve.wait_ge(pe_back, PE_BACK.value(f"y_c{c}", r))
                tt(U[rows], ps[rows, B_UY, 0:256].rearrange("p (a b) -> p a b", a=2),
                   u0[rows].rearrange("p a b c -> p a (b c)"), ALU.add).then_inc(dve_back, 1)

            def core_state(r, b, g, c):
                dve.wait_ge(pe_back, PE_BACK.value(f"s_c{c}", r))
                own_back(f"u_c{c}", r)
                tt(S[:, g], ps[:, B_S, 256 * c:256 * c + 256].rearrange("p (a b) -> p a b", a=2), S[:, g], ALU.add).then_inc(dve_back, 1)
                own_back(f"sx_c{c}", r)
                for p in range(2):
                    stt(S[:, g, p], S[:, g, p], pc[:, b, p, c:c + 1], pair_mask[:], ALU.mult, ALU.mult).then_inc(dve_back, 1)
                own_back(f"s1_c{c}", r)

            def core_y(r, b):
                dve.wait_ge(act_back, ACT_BACK.value("yh1", r))
                tt(B[YY], ps[:, B_UY, 256:512], yh[:].rearrange("p a b c -> p (a b c)"), ALU.add).then_inc(dve_back, 1)
                own_back("y", r)
                nc.vector.tensor_reduce(hst[:, b, H_SM], by_head(B[YY]), AX.X, ALU.add).then_inc(dve_back, 1)
                own_back("sm", r)
                nc.vector.tensor_scalar(hst[:, b, H_MEAN], hst[:, b, H_SM], 1.0 / 64, None, ALU.mult).then_inc(dve_back, 1)

            def core_var(r, b):
                own_back("mean", r)
                tt(by_head(B[YC]), by_head(B[YY]), over(hst[:, b, H_MEAN], 64), ALU.subtract).then_inc(dve_back, 1)
                own_back("yc", r)
                tt(B[YSQ], B[YC], B[YC]).then_inc(dve_back, 1)
                own_back("ysq", r)
                nc.vector.tensor_reduce(hst[:, b, H_VS], by_head(B[YSQ]), AX.X, ALU.add).then_inc(dve_back, 1)
                own_back("vs", r)
                nc.vector.tensor_scalar(hst[:, b, H_VE], hst[:, b, H_VS], 1.0 / 64, LNX_EPS, ALU.mult, ALU.add).then_inc(dve_back, 1)

            def core_out(r, b, g):
                dve.wait_ge(pool_back, POOL_BACK.value("ri", r))
                tt(by_head(B[YC]), by_head(B[YC]), over(hst[:, b, H_RI], 64)).then_inc(dve_back, 1)
                own_back("yn", r)
                tt(B[YC], B[YC], prm_(3, g)).then_inc(dve_back, 1)
                own_back("yw", r)
                tt(B[YC], B[YC], prm_(4, g), ALU.add).then_inc(dve_back, 1)
                tt(by_head(B[BON]), by_head(rin_b[:, 0]), over(bs[:, g], 64)).then_inc(dve_back, 1)
                own_back("bonus", r)
                tt(B[YC], B[YC], B[BON], ALU.add).then_inc(dve_back, 1)
                own_back("yv", r)
                tt(B[OUT], B[YC], rin_b[:, 1]).then_inc(dve_back, 1)

            def core_out_lo(r, t, g):
                dve.wait_ge(act_back, ACT_BACK.value("o_hi", r))
                at = (slice(None), slice(2 * g, 2 * g + 2), slice(P * t, P * t + P) if isinstance(t, int) else bass.ds(P * t, P))
                tt(a_lo[at], ps[:, B_S, 0:256].rearrange("p (a b) -> p a b", a=2), a_hi[at], ALU.subtract).then_inc(dve_back, 1)

            def core_round(t, g, front, inv):
                n, b = GROUPS * t + g, g % 2
                r, q, g2 = n + 2, 1 - b, (g + 2) % GROUPS
                core_u(n, 0)
                if front:
                    core_keys(r, b, g2)
                core_state(n, b, g, 0)
                if inv:
                    core_level(n + 1, q, 1)
                core_u(n, 1)
                if front:
                    core_bonus(r, b, g2)
                core_state(n, b, g, 1)
                if inv:
                    core_level(n + 1, q, 2)
                core_y(n, b)
                core_var(n, b)
                if front:
                    core_scaled(r, b, True)
                if inv:
                    core_level(n + 1, q, 3)
                core_out(n, b, g)
                if inv:
                    core_level(n + 1, q, 4)
                if front:
                    core_masked(r, b, m1, B_M1, "m1")
                if front:
                    core_masked(r, b, m2, B_M2, "m2")
                core_out_lo(n, t, g)
                if inv:
                    core_level(n + 1, q, 5)
                if front:
                    core_start(r, b)
                if inv:
                    core_u0(n + 1)

            for r in range(2):
                core_keys(r, r, r)
                core_bonus(r, r, r)
                core_scaled(r, r, False)
                core_masked(r, r, m1, B_M1, "m1")
                core_masked(r, r, m2, B_M2, "m2")
                core_start(r, r)
            for lv in range(1, 6):
                core_level(0, 0, lv)
            core_u0(0)
            with dve.Fori(0, NT - 1) as t:
                for g in range(GROUPS):
                    core_round(t, g, True, True)
            for g in range(GROUPS):
                core_round(NT - 1, g, g < 2, g < 3)
            proj(U_RWKV_O, F_RWKV_O)
            norm_lo(3, 2, V_MLP1)
            mlp(U_MLP1, F_MLP1, 32, 32)
            scale_x(4, V_FINAL, KT)
            norm_lo(5, 3, V_FFN1)
            ffn(U_FFN1, F_FFN1, H_FFN1, 64)
            dve.wait_ge(unit_done, U_MIX)
            chain.mark(nc.vector.memset(uc[:, :, 0:2], 0.0))
            norm_lo(6, 4, V_MIXG)
            with chain.loop(2, 4 * 3) as lp:
                with dve.Fori(0, 2) as i:
                    lp.at(i)
                    for jj in range(0, 12, 6):
                        def done(q):
                            dve.wait_ge(unit_done, U_MIX + jj + q + 1 + 12 * i)

                        for e in range(2):
                            split_lo(U_MIX + jj + e + AHEAD, 12 * i)
                            done(e)
                            dve.wait_ge(u_ready, H_CONV + 2 * (jj // 6) + e - 1 + 4 * i)
                            nc.vector.tensor_copy(ep[:, 2 + e], ps[:, (F_MIX + jj + e) % 4]).then_inc(bank_free, 1)
                        for e in range(2):
                            split_lo(U_MIX + jj + 2 + e + AHEAD, 12 * i)
                            done(2 + e)
                            dve.wait_ge(bank_free, F_MIX + jj + e + 1 + 12 * i)
                            nc.vector.tensor_tensor(uc[:, e, 2:T + 2], ep[:, 2 + e], ps[:, (F_MIX + jj + 2 + e) % 4], ALU.mult)\
                                .then_inc(bank_free, 1)
                            dve.wait_ge(bank_free, F_MIX + jj + 2 + e + 1 + 12 * i)
                            tile = 2 * (jj // 6) + e
                            for w in range(3):
                                tap = vec[:, V_CONV + w, bass.ds(4 * i + tile, 1)]
                                if w == 0:
                                    chain.mark(nc.vector.tensor_scalar(uc2[:, e], uc[:, e, 0:T], tap, None, ALU.mult))
                                else:
                                    chain.wait()
                                    chain.mark(nc.vector.scalar_tensor_tensor(uc2[:, e], uc[:, e, w:T + w], tap, uc2[:, e], ALU.mult, ALU.add))
                            chain.wait()
                        for e in range(2):
                            split_lo(U_MIX + jj + 4 + e + AHEAD, 12 * i)
                            done(4 + e)
                            nc.vector.tensor_tensor(ep[:, 2 + e], uc2[:, e], ps[:, (F_MIX + jj + 4 + e) % 4], ALU.mult).then_inc(bank_free, 1)
                            tile = 2 * (jj // 6) + e
                            dve.wait_ge(u_hi_ready, H_CONV + tile + 1 + 4 * i)
                            nc.vector.tensor_tensor(u_lo[:, bass.ds(4 * i + tile, 1)].rearrange("p o t -> p (o t)"), ep[:, 2 + e],
                                                    u_hi[:, bass.ds(4 * i + tile, 1)].rearrange("p o t -> p (o t)"), ALU.subtract).then_inc(u_ready, 1)
            for g in range(6, 12):
                for q in range(4):
                    split_lo(U_MIX + 4 * g + q + AHEAD)
                if g >= 10:
                    for t in range(NT):
                        dve.wait_ge(tm_free, 4 * g + t + 1)
                        nc.vector.tensor_tensor(ep[:, t], ep[:, t], ps[:, 4 * (g % 2) + t], ALU.mult).then_inc(silu_ready, 1)
            chain.mark(nc.vector.memset(glr[:], 0.0))
            chain.wait()
            chain.mark(nc.vector.memset(glr[32:33], 1.0))
            split_lo(U_MIX + 48 + AHEAD)
            split_lo(U_MIX + 49 + AHEAD)
            dve.wait_ge(unit_done, U_MIX + 50)
            chain.wait()
            nc.vector.tensor_copy(glr[0:16], ps[0:16, (F_MIX + 24) % 4]).then_inc(bank_free, 1)
            for t in range(NT):
                dve.wait_ge(la_act, 9 + t)
                nc.vector.scalar_tensor_tensor(ep[:, t], ps[:, 4 + t], 0.0, ep[:, t], ALU.min, ALU.subtract).then_inc(la_ready, 1)
            for j in range(16):
                split_lo(U_MIX + 50 + j + AHEAD)
                dve.wait_ge(unit_done, U_MIX + 51 + j)
                nc.vector.tensor_copy((merged if j < 8 else sig_b)[:, j % 8], ps[:, (F_GATES + j) % 4]).then_inc(bank_free, 1)
            for j in range(8):
                split_lo(U_MIX + 66 + j + AHEAD)
                dve.wait_ge(unit_done, U_MIX + 67 + j)
                dve.wait_ge(gated, j + 1)
                nc.vector.tensor_tensor(merged[:, j], merged[:, j], ps[:, (F_GATES + 16 + j) % 4], ALU.mult).then_inc(bank_free, 1)
            chain.mark(nc.vector.memset(scT[:], 0.0))
            dve.wait_ge(gla_in, 16)
            chain.wait()
            with dve.Fori(0, 4) as h:
                nc.vector.memset(St[:], 0.0).then_inc(st_zero, 1)
                with dve.Fori(0, 2) as tp:
                    for s in range(2):
                        n = 4 * h + 2 * tp + s
                        todo = list(DVE_GLA.names)

                        def step(name, inst):
                            assert todo.pop(0) == name, name
                            inst.then_inc(dve_gla, 1)

                        def own(name):
                            dve.wait_ge(dve_gla, DVE_GLA.value(name, n))

                        def pe_(name):
                            dve.wait_ge(pe_gla, PE_GLA.value(name, n))

                        def act_(name):
                            dve.wait_ge(act_gla, ACT_GLA.value(name, n))

                        def stt(dst, a, sc, b, op0, op1):
                            return nc.vector.scalar_tensor_tensor(dst, a, sc, b, op0, op1)

                        q_, k_ = gin[:, s, 0:P], gin[:, s, P:2 * P]
                        dve.wait_ge(gin_in[s], 32 * h + 16 * tp + 16)
                        act_("ex_neg")
                        step("qr", stt(gqk[:, 0], q_, GLA_SCALE, gex[:, 0], ALU.mult, ALU.mult))
                        step("kr", nc.vector.tensor_tensor(gqk[:, 1], k_, gex[:, 3], ALU.mult))
                        step("qi", stt(gqk[:, 2], q_, GLA_SCALE, gex[:, 1], ALU.mult, ALU.mult))
                        step("ks", nc.vector.tensor_tensor(gqk[:, 3], k_, gex[:, 2], ALU.mult))
                        pe_("scores")
                        nc.vector.memset(gate[:, 14:15], 0.0)
                        step("mask", nc.vector.copy_predicated(scT[:], imask[:, 13], ps[:, 2, 0:P]))
                        act_("chunk")
                        if s == 0:
                            dve.wait_ge(st_zero, h + 1)
                        for c in range(2):
                            pe_(f"o{c}")
                            step(f"st{c}", stt(St[:], St[:], gdc[:, c:c + 1], ps[:, 4 + c, 0:256], ALU.mult, ALU.add))
                            own(f"st{c}")
                        act_("osq")
                        step("mean", nc.vector.tensor_scalar(gst[:, 1:2], gst[:, 0:1], 1.0 / 256, EPS, ALU.mult, ALU.add))
                        dve.wait_ge(pool_gla, POOL_GLA.value("ri", n))
                        step("on", stt(on[:], ps[:, 3, 0:256], gst[:, 2:3], gla_g[:, bass.ds(256 * h, 256)], ALU.mult, ALU.mult))
                        own("on")
                        step("out", nc.vector.tensor_tensor(gout[:], on[:], gin[:, s, 512:768], ALU.mult))
                        act_("o_hi")
                        at = (slice(None), bass.ds(2 * h, 2), bass.ds(2 * P * tp + P * s, P))
                        step("o_lo", nc.vector.tensor_tensor(a_lo[at], ps[:, 6, 0:256].rearrange("p (a b) -> p a b", a=2), a_hi[at], ALU.subtract))
                        own("o_lo")
                        assert not todo
            for j in range(8):
                split_lo(U_GLA_O + j + AHEAD)
                dve.wait_ge(unit_done, U_GLA_O + j + 1)
                dve.wait_ge(gated, 9 + j)
                nc.vector.tensor_tensor(sig_b[:, j], sig_b[:, j], ps[:, (F_GLA_O + j) % 4], ALU.mult).then_inc(bank_free, 1)
                dve.wait_ge(bank_free, F_GLA_O + j + 1)
                nc.vector.tensor_tensor(merged[:, j], merged[:, j], sig_b[:, j], ALU.add).then_inc(merged_ready, 1)
                dve.wait_ge(u_hi_ready, H_MERGED + j + 1)
                nc.vector.tensor_tensor(u_lo[:, j], merged[:, j], u_hi[:, j], ALU.subtract).then_inc(u_ready, 1)
            proj(U_MIX_O, F_MIX_O)
            norm_lo(7, 5, V_FFN2)
            ffn(U_FFN2, F_FFN2, H_FFN2, 86)
            scale_x(8, V_OUT, 2 * KT)

        @block.gpsimd
        def _(pool):
            def spill_out(slot, c, t, half):
                pool.dma_start(rk_dram[t, 2 * half:2 * half + 2, :, c].rearrange("g p n -> p g n"),
                               ep[:, slot].rearrange("p (g n) -> p g n", g=2)).then_inc(spill[slot], 16)

            pool.wait_ge(unit_done, U_RWKV)
            pool.dma_start(lora2[:], io["lora2"]).then_inc(lora_in, 16)
            for g in range(6):
                for t in range(NT):
                    pool.wait_ge(tm_free, 4 * g + t + 1)
                    spill_out(t, (0, 1, 4)[g // 2], t, g % 2)
            for i in range(24):
                pool.wait_ge(lora_read, i + 1)
                spill_out(i % 4, (2, 3, 5)[i // 8], i % 8 // 2, i % 2)
            pool.wait_ge(bank_free, F_RWKV + 4)
            nc.gpsimd.memset(h_half[:], -0.5).then_inc(pool_step, 1)
            pool.dma_start(prm[:], io["prm"].rearrange("(o j) n -> o j n", o=1).to_broadcast([P, 5, D])).then_inc(prm_in, 16)
            for s in range(4):
                pool.wait_ge(spill[s], 16 * 12)
            rounds = rk_dram.rearrange("t g p c n -> (t g) p (c n)")

            def fetch(r, columns, dst, sem_):
                src = rounds[r] if isinstance(r, int) else rounds[bass.ds(r, 1)].rearrange("o p n -> p (o n)")
                pool.dma_start(dst.rearrange("p c n -> p (c n)"), src[:, columns]).then_inc(sem_, 16)

            FRONT_COLS, BACK_COLS = slice(0, 5 * 256), slice(4 * 256, 6 * 256)
            fetch(0, FRONT_COLS, rin_f[:], rin_f_in)
            fetch(0, BACK_COLS, rin_b[:], rin_b_in)
            pool.wait_ge(pool_step, 1)
            eye = bcast(ident[:], 4, P)

            def front_part(r, b, old):
                if old:
                    pool.wait_ge(pe_inv, PE_INV.value("ta", r - 2))
                nc.gpsimd.tensor_tensor(Tm[:, b], eye, eye, ALU.mult).then_inc(pool_front, 1)
                nc.gpsimd.tensor_tensor(TT[:, b], eye, eye, ALU.mult).then_inc(pool_front, 1)
                pool.wait_ge(dve_front, DVE_FRONT.value("ssm", r))
                nc.gpsimd.tensor_tensor(hst[:, b, H_RN], hst[:, b, H_SSM], h_half[:], ALU.pow).then_inc(pool_front, 1)

            def back_part(r, b):
                pool.wait_ge(dve_back, DVE_BACK.value("ve", r))
                nc.gpsimd.tensor_tensor(hst[:, b, H_RI], hst[:, b, H_VE], h_half[:], ALU.pow).then_inc(pool_back, 1)

            def next_front(r):
                pool.wait_ge(pe_front, PE_FRONT.value("bv", r - 1))
                fetch(r, FRONT_COLS, rin_f[:], rin_f_in)

            def next_back(r):
                pool.wait_ge(dve_back, DVE_BACK.value("o", r - 1))
                fetch(r, BACK_COLS, rin_b[:], rin_b_in)

            front_part(0, 0, False)
            next_front(1)
            front_part(1, 1, False)
            next_front(2)
            with pool.Fori(0, NT - 1) as t:
                for s in range(GROUPS):
                    n = GROUPS * t + s
                    front_part(n + 2, s % 2, True)
                    back_part(n, s % 2)
                    next_back(n + 1)
                    next_front(n + 3)
            for n in range(ROUNDS - GROUPS, ROUNDS):
                if n + 2 < ROUNDS:
                    front_part(n + 2, n % 2, True)
                back_part(n, n % 2)
                if n + 1 < ROUNDS:
                    next_back(n + 1)
                if n + 3 < ROUNDS:
                    next_front(n + 3)
            def spill_gla(slot, t, heads, cols):
                dst = gla_dram[heads, t, :, cols].rearrange("g p n -> p g n")
                n = dst.shape[1]
                pool.dma_start(dst, ep[:, slot].rearrange("p (g n) -> p g n", g=n)).then_inc(spill[slot], 16)

            pool.wait_ge(unit_done, U_MIX)
            pool.dma_start(gate_up[:], io["gate_up"]).then_inc(gate_in, 16)
            for g in range(6, 12):
                for t in range(NT):
                    if g < 10:
                        pool.wait_ge(tm_free, 4 * g + t + 1)
                    else:
                        pool.wait_ge(silu_ready, 4 * (g - 10) + t + 1)
                    if g < 8:
                        spill_gla(t, t, slice(0, 4), slice(P * (g - 6), P * (g - 5)))
                    else:
                        half = 2 * (g % 2)
                        spill_gla(t, t, slice(half, half + 2), slice(256, 512) if g < 10 else slice(512, 768))
            for t in range(NT):
                pool.wait_ge(la_ready, t + 1)
                spill_gla(t, t, slice(0, 4), slice(768, 896))
            for t in range(NT):
                pool.wait_ge(spill[t], 16 * 19)
            pool.wait_ge(unit_done, U_GLA_O)
            pool.dma_start(gla_g[:], io["gla_g"].to_broadcast([P, D])).then_inc(gla_in, 16)
            nc.gpsimd.memset(gst[:, 3:4], -0.5).then_inc(pool_gla_const, 1)
            rounds = gla_dram.rearrange("h t p n -> (h t) p n")
            for s in range(2):
                pool.dma_start(gin[:, s], rounds[s]).then_inc(gin_in[s], 16)
            pool.wait_ge(pool_gla_const, 1)

            def round_(n, s, more):
                pool.wait_ge(dve_gla, DVE_GLA.value("mean", n))
                nc.gpsimd.tensor_tensor(gst[:, 2:3], gst[:, 1:2], gst[:, 3:4], ALU.pow).then_inc(pool_gla, 1)
                pool.wait_ge(pe_gla, PE_GLA.value("turn_o", n))
                if more:
                    pool.dma_start(gin[:, s], rounds[bass.ds(n + 2, 1)].rearrange("o p n -> p (o n)")).then_inc(gin_in[s], 16)

            with pool.Fori(0, 7) as i:
                for s in range(2):
                    round_(2 * i + s, s, True)
            for s in range(2):
                round_(14 + s, s, False)


def constants():
    t = np.arange(T, dtype=np.float32)
    inv = (1.0 / (np.float32(10000.0) ** (np.arange(0, 64, 2, dtype=np.float32) / np.float32(64)))).astype(np.float32)
    ang = (inv[:, None] * t[None, :]).astype(np.float32)
    cos, sin = np.cos(ang), np.sin(ang)
    j, i = np.arange(P)[:, None], np.arange(P)[None, :]
    same = j // CHUNK == i // CHUNK
    upto, before = same & (j <= i), same & (j < i)
    ref = i // CHUNK * CHUNK + CHUNK // 2 - 1
    tri = np.stack([upto * -E_HALF, before * -E_HALF,
                    (upto * 1.0 - (same & (j <= ref))) / 16, upto / 16.0, (same & (j > i)) / 16.0, 0.0 * upto], 1)
    chunk = (np.arange(P)[:, None] // CHUNK == np.arange(2)[None, :]).astype(np.float32)
    levels = [((j // s) % 2 == 1) & ((i // s) % 2 == 0) & (j // (2 * s) == i // (2 * s)) for s in LEVELS]
    imask = np.stack(levels + [m.T for m in levels] + [i > j, upto], 1)
    out = dict(
        cos=np.tile(cos, (4, 1)), sin=np.concatenate([-sin, sin, -sin, sin]), ident=np.eye(P), ones=np.ones((P, P)),
        tri=tri, strict_incl=np.stack([before, upto], 1), chunk_sum=np.stack([chunk * -E_HALF, chunk / 16], 1),
        pair_mask=same, causal=np.where(i > j, NEG, 0.0), fill=np.full((P, P), SCORE_OUT),
    )
    out = {k: np.ascontiguousarray(v, np.float32) for k, v in out.items()}
    out["imask"] = np.ascontiguousarray(imask, np.int32)
    return out


def fm(w, col, rows=range(KT)):
    u = np.zeros((P, KT, P), np.float32)
    for n, k in enumerate(rows):
        part = w[k * P:(k + 1) * P, col:col + P]
        u[:, n, :part.shape[1]] = part
    return u.reshape(P, UNIT)


def tm(w, col):
    return [np.ascontiguousarray(w[2 * q * P:(2 * q + 2) * P, col:col + T].reshape(2, P, T).transpose(1, 0, 2)).reshape(P, UNIT)
            for q in range(4)]


def stream(a):
    s = []
    w = a["dsa_w_in"][0]
    s += [fm(w, P * j) for j in range(16)] + [fm(w, 2048, range(4)), fm(w, 2048, range(4, 8))]
    s += [fm(a["dsa_w_o"][0], P * j) for j in range(8)]

    def mlp(n):
        for c in range(4):
            yield from (fm(a["mlp_w_up"][n], D * c + P * j) for j in range(8))
            yield from (fm(a["mlp_w_down"][n], P * j, range(8 * c, 8 * c + 8)) for j in range(8))

    def ffn(gu, down):
        at = 0
        for size in FFN_CHUNKS:
            for j in range(at, at + size, 2):
                yield from (fm(gu, P * j), fm(gu, P * j + P), fm(gu, 2816 + P * j), fm(gu, 2816 + P * j + P))
            yield from (fm(down, P * j, range(at, at + size)) for j in range(8))
            at += size

    s += mlp(0)
    for c in range(3):
        s += tm(a["rwkv_w_rkv"][0, c], 0) + tm(a["rwkv_w_rkv"][0, c], 512)
    s += [fm(a["rwkv_w1"][0], 0), fm(a["rwkv_a1"][0], 0), fm(a["rwkv_g1"][0], 0), fm(a["rwkv_g1"][0], P)]
    s += [fm(a["rwkv_w_o"][0], P * j) for j in range(8)]
    s += mlp(1)
    s += ffn(a["ffn1_w_gu_2"][0], a["ffn1_w_down_2"][0])
    w = a["w_in_2"][0]
    for j in range(0, 8, 2):
        s += [fm(w, D * c + P * (j + e)) for c in (1, 2, 0) for e in (0, 1)]
    for col in (3072, 3584, 4096, 4608, 5136, 5648):
        s += tm(w, col)
    s += [fm(w[:, 5120:5136], 0, range(4)), fm(w[:, 5120:5136], 0, range(4, 8))]
    s += [fm(w, 6160 + P * j) for j in range(16)]
    for name in ("w_out_conv_2", "w_out_gla_2", "w_o_2"):
        s += [fm(a[name][0], P * j) for j in range(8)]
    s += ffn(a["ffn2_w_gu_2"][0], a["ffn2_w_down_2"][0])
    assert len(s) == U_END
    return np.stack(s).reshape(U_END // 2, 2, P, UNIT).transpose(0, 2, 1, 3).reshape(U_END // 2, P, 2 * UNIT)


def arrays_of(inputs):
    a = {k: np.asarray(v) for k, v in inputs.items()}
    v = [a["mixer_norm"], a["mlp_norm"], a["final_norm"][None], a["norm_ffn1_g_2"], a["norm_mix_g_2"], a["norm_ffn2_g_2"],
         a["final_norm_g_2"][None], a["rwkv_mu"][0], a["conv_w_2"][0]]
    vectors = np.concatenate(v).reshape(N_VEC, KT, P).transpose(2, 0, 1)
    g2 = np.zeros((2 * P, D), np.float32)
    g2[:160] = a["rwkv_g2"][0]
    lora2 = np.zeros((P, 4, D), np.float32)
    lora2[:64, 0], lora2[64, 0] = a["rwkv_w2"][0], a["rwkv_w0"][0]
    lora2[:64, 1], lora2[64, 1] = a["rwkv_a2"][0], a["rwkv_a0"][0]
    lora2[:, 2], lora2[:, 3] = g2[:P], g2[P:]
    gate_up = np.zeros((P, T), np.float32)
    gate_up[:16], gate_up[32] = a["gate_w_up_2"][0], a["gate_b_2"][0]
    out = constants()
    out.update(
        x=np.ascontiguousarray(a["x"][0].T.reshape(KT, P, T).transpose(1, 0, 2)), weights=stream(a), vec=vectors,
        lora2=lora2, gate_up=gate_up,
        prm=np.stack([a["rwkv_k_k"][0], a["rwkv_k_a"][0], a["rwkv_r_k"][0].reshape(D), a["rwkv_lnx_w"][0], a["rwkv_lnx_b"][0]]),
        gla_g=a["gla_norm_g_2"][0].reshape(1, D),
    )
    return {k: np.ascontiguousarray(v) for k, v in out.items()}


def kernel(**inputs):
    import concourse.bacc as bacc
    from concourse.bass_utils import run_bass_kernel_spmd

    nc = bacc.Bacc("TRN2", target_bir_lowering=False, num_devices=1)
    arrays = arrays_of(inputs)
    io = {k: nc.dram_tensor(k + "_dram", v.shape, mybir.dt.from_np(v.dtype), kind="ExternalInput").ap() for k, v in arrays.items()}
    out = nc.dram_tensor("out_dram", (P, KT, T), F32, kind="ExternalOutput").ap()
    build(nc, io, out)
    r = run_bass_kernel_spmd(nc, [{k + "_dram": v for k, v in arrays.items()}], core_ids=[0])
    got = r.results[0]["out_dram"]
    return got.transpose(2, 1, 0).reshape(1, T, D)
```

```python
from contextlib import ExitStack

import numpy as np

import concourse.bass as bass
from concourse import mybir

F32 = mybir.dt.float32
F32R = mybir.dt.float32r
I32 = mybir.dt.int32
ALU = mybir.AluOpType
ACT = mybir.ActivationFunctionType
AX = mybir.AxisListType

P = 128
T = 512
D = 1024
KT = D // P
NT = T // P
UNIT = 1024
SPLITS = 4
PAIRS = 2
AHEAD = 3

N_DSA_IN = 18
N_PROJ = 8
N_MLP = 64
N_RWKV_IN = 28
FFN_CHUNKS = (8, 8, 6)
N_FFN = sum(2 * c + 8 for c in FFN_CHUNKS)
N_MIX_IN = 24 + 24 + 2 + 8 + 8 + 8

U_DSA = 0
U_DSA_O = U_DSA + N_DSA_IN
U_MLP0 = U_DSA_O + N_PROJ
U_RWKV = U_MLP0 + N_MLP
U_RWKV_O = U_RWKV + N_RWKV_IN
U_MLP1 = U_RWKV_O + N_PROJ
U_FFN1 = U_MLP1 + N_MLP
U_MIX = U_FFN1 + N_FFN
U_GLA_O = U_MIX + N_MIX_IN
U_MIX_O = U_GLA_O + N_PROJ
U_FFN2 = U_MIX_O + N_PROJ
U_END = U_FFN2 + N_FFN

F_DSA, F_DSA_O = 0, 17
F_MLP0 = F_DSA_O + 8
F_RWKV = F_MLP0 + 64
F_RWKV_O = F_RWKV + 4
F_MLP1 = F_RWKV_O + 8
F_FFN1 = F_MLP1 + 64
F_MIX = F_FFN1 + N_FFN
F_GLA_O = F_MIX + 24 + 1 + 24
F_MIX_O = F_GLA_O + 8
F_FFN2 = F_MIX_O + 8

F_OF_NORM = (0, F_MLP0, F_RWKV, F_MLP1, F_FFN1, 0, F_MIX, F_FFN2, F_FFN2 + N_FFN)

(V_MIX0, V_MIX1, V_MLP0, V_MLP1, V_FINAL, V_FFN1, V_MIXG, V_FFN2, V_OUT) = range(9)
V_MU, V_CONV, N_VEC = 9, 15, 18

LEVELS = (1, 2, 4, 8, 16, 32)
CHUNK = 64
EPS = 1e-6
LNX_EPS = 64e-5
NEG = -1.0e30
SCORE_OUT = -3.0e38
SCORE_TAKEN = -3.4e38
TOPK = 128
E_HALF = float(np.exp(-0.5))


class Tally:

    def __init__(self, eng, sem):
        self.eng, self.sem, self.n, self.reg = eng, sem, 0, 0

    def mark(self, inst):
        inst.then_inc(self.sem, 1)
        self.n += 1
        return self.n + self.reg

    def wait(self, label=None):
        self.eng.wait_ge(self.sem, self.n + self.reg if label is None else label)

    def loop(self, trips, per):
        return _TallyLoop(self, trips, per)


class _TallyLoop:
    def __init__(self, tally, trips, per):
        self.t, self.trips, self.per = tally, trips, per

    def __enter__(self):
        self.n0, self.reg0 = self.t.n, self.t.reg
        return self

    def at(self, i):
        self.t.reg = self.reg0 + i * self.per

    def __exit__(self, kind, *rest):
        if kind is None:
            assert self.t.n - self.n0 == self.per, ("marks in the loop's body", self.t.n - self.n0)
            self.t.n, self.t.reg = self.n0 + self.per * self.trips, self.reg0


def later(r, first):
    return not isinstance(r, int) or r >= first


def bcast(ap, n, inner):
    return ap.rearrange("p (o i) -> p o i", o=1).to_broadcast([ap.shape[0], n, inner])


def over(ap, inner):
    return ap.rearrange("p (n o) -> p n o", o=1).to_broadcast([ap.shape[0], ap.shape[1], inner])


class Steps:

    def __init__(self, *names):
        self.names = [n for group in names for n in group.split()]

    def value(self, name, rnd):
        return self.names.index(name) + 1 + rnd * len(self.names)


PE_FRONT = Steps("decay chunk_decay turn_ar turn_bk m1 m2 bv")
ACT_FRONT = Steps("ex_in ex_before ex_neg pc ar bk bv")
DVE_FRONT = Steps("kkr sq ss ssm t kf rkf rkr bs kk b al rho be ka m1_0 m1_1 m2_0 m2_1 tt0 t0")
POOL_FRONT = Steps("eye rn")
PE_INV = Steps(" ".join(f"w{v} tw{v} wt{v}" if v < 5 else f"w{v} wt{v}" for v in range(1, 6)), "ta u0")
ACT_INV = Steps(" ".join(f"w{v}" for v in range(1, 6)), "ta")
DVE_INV = Steps(" ".join(f"t{v} tt{v}" if v < 5 else f"tt{v}" for v in range(1, 6)), "u0_0 u0_1")
PE_BACK = Steps("u_c0 y_c0 s_c0 u_c1 y_c1 s_c1 yh turn_o")
ACT_BACK = Steps("yh0 yh1 o_hi")
DVE_BACK = Steps("u_c0 sx_c0 s0_c0 s1_c0 u_c1 sx_c1 s0_c1 s1_c1 y sm mean yc ysq vs ve yn yw yb bonus yv o o_lo")
POOL_BACK = Steps("ri")
GROUPS = 4
ROUNDS = NT * GROUPS
B_UY, B_S, B_YH = 0, 1, 2
B_M1, B_M2 = (0, 2), (3, 4)
B_W, B_TW, B_WT = 5, 6, 7

KKR, SQ, KK, TA, KF, RHO, RKF, BB = range(8)
YY, YC, YSQ, OUT, BON = range(5)
(H_SS, H_SSM, H_RN, H_SM, H_MEAN, H_VS, H_VE, H_RI) = range(8)

PE_GF, ACT_GF, DVE_GF = Steps("decay"), Steps("ex ex_neg chunk"), Steps("qr kr qi ks")
PE_GT, ACT_GT, DVE_GT = Steps("turn scores"), Steps("gT"), Steps("mask")
PE_GS, ACT_GS, DVE_GS = Steps("kv0 kv1 o0 o1"), Steps("osq"), Steps("st0 st1 mean")
PE_GO, ACT_GO, DVE_GO = Steps("turn_o"), Steps("o_hi"), Steps("on out o_lo")
POOL_GS = Steps("ri")
G_DECAY, G_TURN, G_SCORE, G_OUT, G_KV, G_TURN_O = 0, 1, 2, (3, 7), 4, 6
GLA_SCALE = 128 ** -0.5
F_GATES = F_MIX + 25
H_MLP0, H_MLP1, H_FFN1, H_CONV, H_MERGED, H_FFN2 = 0, 32, 64, 86, 94, 102


def build(nc, io, out):
    with ExitStack() as ctx:
        def sb(name, shape, dt=F32, at=ctx):
            return at.enter_context(nc.sbuf_tensor(name, shape, dt))

        def sem(name):
            return ctx.enter_context(nc.semaphore(name))

        x = sb("x_res", [P, KT, T])
        warm = sb("warm", [P, 1])
        gate = sb("gate", [P, 15])
        raw = sb("raw", [P, PAIRS, 2 * UNIT])
        w_hi = sb("w_hi", [P, SPLITS, UNIT], F32R)
        w_lo = sb("w_lo", [P, SPLITS, UNIT], F32R)
        a_hi = sb("a_hi", [P, KT, T], F32R)
        a_lo = sb("a_lo", [P, KT, T], F32R)
        root_t = sb("root_t", [P, NT])
        inv_t = sb("inv_t", [P, NT])
        rstd = sb("rstd", [P, T])
        sq_sum = sb("sq_sum", [P, T])
        h32 = sb("h32", [P, 3, T])
        ep = sb("ep", [P, 4, T])
        vec = sb("vec", [P, N_VEC, KT])
        ident = sb("ident", [P, P])
        ones = sb("ones", [P, P])
        tri = sb("tri", [P, 6, P])
        strict_incl = sb("strict_incl", [P, 2, P])
        chunk_sum = sb("chunk_sum", [P, 2, 2])
        imask = sb("imask", [P, 14, P], I32)
        pair_mask = sb("pair_mask", [P, P])

        with ExitStack() as attn:
            cos = sb("cos", [P, T], at=attn)
            sin = sb("sin", [P, T], at=attn)
            qT = sb("qT", [P, 8, T], at=attn)
            kd = sb("kd", [P, 4, T], at=attn)
            vT = sb("vT", [P, 2, T], at=attn)
            v_tm = sb("v_tm", [P, NT, 256], at=attn)
            qiT = sb("qiT", [P, 4, T], at=attn)
            kiwi = sb("kiwi", [P, T], at=attn)
            kid = sb("kid", [P, T], at=attn)
            wi = sb("wi", [P, NT, 8], at=attn)
            swap = sb("swap", [P, 2, T], at=attn)
            rope1 = sb("rope1", [P, T], at=attn)
            top8 = sb("top8", [P, 8], at=attn)
            fill = sb("fill", [P, P], at=attn)
            causal = sb("causal", [P, P], at=attn)
            amask = sb("amask", [P, NT, T], at=attn)
            prob = sb("prob", [P, 4, T], at=attn)
            probT = sb("probT", [P, 2, T], at=attn)
            stat = sb("stat", [P, 4, 64], at=attn)
        with ExitStack() as gla:
            gex = sb("gex", [P, 4, P], at=gla)
            gdc = sb("gdc", [P, GROUPS, 2], at=gla)
            gqk = sb("gqk", [P, 2, 3, P], at=gla)
            gks = sb("gks", [P, GROUPS, P], at=gla)
            gT = sb("gT", [P, 2, 3, P], at=gla)
            scT = sb("scT", [P, 2, P], at=gla)
            St = sb("St", [P, GROUPS, 256], at=gla)
            gsq = sb("gsq", [P, 256], at=gla)
            gst = sb("gst", [P, 2, 3], at=gla)
            g_half = sb("g_half", [P, 1], at=gla)
            on = sb("on", [P, 256], at=gla)
            gout = sb("gout", [P, 256], at=gla)
            gla_g = sb("gla_g", [P, D], at=gla)
        u_scope = ExitStack()
        u_hi = sb("u_hi", [P, KT, T], F32R, at=u_scope)
        u_lo = sb("u_lo", [P, KT, T], F32R, at=u_scope)
        with ExitStack() as shift:
            h_pad = sb("h_pad", [P, KT, T + 2], at=shift)
            mu1 = sb("mu1", [P, 6, KT], at=shift)
            lora = sb("lora", [P, 4, T], at=shift)
            lora2 = sb("lora2", [P, 4, D], at=shift)
        with ExitStack() as conv:
            uc = sb("uc", [P, 2, T + 2], at=conv)
            uc2 = sb("uc2", [P, 2, T], at=conv)
            gin_f = uc
            gin_b = uc2
            merged = sb("merged", [P, KT, T], at=conv)
            sig_b = sb("sig_b", [P, KT, T], at=conv)
            glr = sb("glr", [P, T], at=conv)
            gate_up = sb("gate_up", [P, 512], at=conv)
        u_scope.close()
        with ExitStack() as core:
            rin_f = sb("rin_f", [P, 5, 256], at=core)
            rin_b = sb("rin_b", [P, 2, 256], at=core)
            prm = sb("prm", [P, 5, D], at=core)
            ex = sb("ex", [P, 3, 256], at=core)
            hst = sb("hst", [P, 2, 8, 4], at=core)
            bs = sb("bs", [P, GROUPS, 4], at=core)
            h_half = sb("h_half", [P, 4], at=core)
            pc = sb("pc", [P, 2, 2, 2], at=core)
            be_ka = sb("be_ka", [P, 2, 2, 256], at=core)
            arT = sb("arT", [P, 2, 2, 2, P], at=core)
            bkT = sb("bkT", [P, 2, 2, P], at=core)
            m1 = sb("m1", [P, 2, 2, 2, 2, P], at=core)
            m2 = sb("m2", [P, 2, 2, 2, 2, P], at=core)
            Tm = sb("Tm", [P, 2, 4, P], at=core)
            TT = sb("TT", [P, 2, 4, P], at=core)
            Wm = sb("Wm", [P, 4, P], at=core)
            bv = sb("bv", [P, 2, 4, P], at=core)
            u0 = sb("u0", [P, 2, 2, 64], at=core)
            taT = sb("taT", [P, 2, P], at=core)
            U = sb("U", [P, 2, P], at=core)
            S = sb("S", [P, GROUPS, 2, P], at=core)
            yh = sb("yh", [P, 2, 2, 64], at=core)
        front_t = ep[:].rearrange("p a (b n) -> p (a b) n", b=2)
        back_t = h32[:].rearrange("p a (b n) -> p (a b) n", b=2)
        al_t = rstd[:].rearrange("p (a n) -> p a n", a=2)
        ps = ctx.enter_context(nc.psum_tensor("ps", [P, 8, T], F32))

        rk_dram = nc.dram_tensor("rwkv_scratch", (NT, GROUPS, P, 6, 256), F32).ap()

        gla_dram = nc.dram_tensor("gla_scratch", (NT, GROUPS, P, 896), F32).ap()

        raw_in = [sem("raw_in0"), sem("raw_in1")]
        hi_ready = sem("hi_ready")
        split_ready = sem("split_ready")
        unit_done = sem("unit_done")
        bank_free = sem("bank_free")
        tm_free = sem("tm_free")
        const_in = sem("const_in")
        norm_in = sem("norm_in")
        x_in = [sem("x_in0"), sem("x_in1")]
        squared = sem("squared")
        summed = sem("summed")
        rooted = sem("rooted")
        diag_ready = sem("diag_ready")
        spread = sem("spread")
        sq_added = sem("sq_added")
        normed = sem("normed")
        a_hi_ready = sem("a_hi_ready")
        a_ready = sem("a_ready")
        ep_act = sem("ep_act")
        u_hi_ready = sem("u_hi_ready")
        u_ready = sem("u_ready")
        dve_chain = sem("dve_chain")
        pool_step = sem("pool_step")
        rin_f_in = sem("rin_f_in")
        rin_b_in = sem("rin_b_in")
        prm_in = [sem(f"prm_in{g}") for g in range(GROUPS)]
        swap_ready = sem("swap_ready")
        roped = sem("roped")
        kiwi_ready = sem("kiwi_ready")
        vt_ps = sem("vt_ps")
        v_read = sem("v_read")
        wi_read = sem("wi_read")
        idx_ps = sem("idx_ps")
        idx_relu = sem("idx_relu")
        idx_added = sem("idx_added")
        lg_ps = sem("lg_ps")
        lg_read = sem("lg_read")
        lg_bias = sem("lg_bias")
        exp_ready = sem("exp_ready")
        prob_ready = sem("prob_ready")
        tr_ps = sem("tr_ps")
        probT_ready = sem("probT_ready")
        o_ps = sem("o_ps")
        o_hi = sem("o_hi")
        o_ready = sem("o_ready")
        out_done = sem("out_done")
        xs32 = sem("xs32")
        xs_hi = sem("xs_hi")
        xs_ready = sem("xs_ready")
        lora_in = sem("lora_in")
        lora_act = sem("lora_act")
        lora_ps = sem("lora_ps")
        lora_read = sem("lora_read")
        spill = [sem(f"spill{i}") for i in range(4)]
        pe_front, act_front, dve_front, pool_front = (sem(n) for n in ("pe_front", "act_front", "dve_front", "pool_front"))
        pe_inv, act_inv, dve_inv = (sem(n) for n in ("pe_inv", "act_inv", "dve_inv"))
        pe_back, act_back, dve_back, pool_back = (sem(n) for n in ("pe_back", "act_back", "dve_back", "pool_back"))
        state_zero = sem("state_zero")
        x_scaled = sem("x_scaled")
        gated = sem("gated")
        silu_ready = sem("silu_ready")
        la_act = sem("la_act")
        la_ps = sem("la_ps")
        la_ready = sem("la_ready")
        gate_in = sem("gate_in")
        gla_in = sem("gla_in")
        gin_f_in = [sem("gin_f_in0"), sem("gin_f_in1")]
        gin_b_in = [sem("gin_b_in0"), sem("gin_b_in1")]
        st_zero = sem("st_zero")
        pe_gf, act_gf, dve_gf = (sem(n) for n in ("pe_gf", "act_gf", "dve_gf"))
        pe_gt, act_gt, dve_gt = (sem(n) for n in ("pe_gt", "act_gt", "dve_gt"))
        pe_gs, act_gs, dve_gs, pool_gs = (sem(n) for n in ("pe_gs", "act_gs", "dve_gs", "pool_gs"))
        pe_go, act_go, dve_go = (sem(n) for n in ("pe_go", "act_go", "dve_go"))
        merged_ready = sem("merged_ready")
        pool_gla_const = sem("pool_gla_const")
        block = ctx.enter_context(nc.Block())

        @block.sync
        def _(sp):
            for i in range(2):
                half = slice(4 * i, 4 * i + 4)
                sp.dma_start(x[:, half], io["x"][:, half]).then_inc(x_in[i], 16)
            for dst, name in ((ident, "ident"), (ones, "ones"), (vec, "vec")):
                sp.dma_start(dst[:], io[name]).then_inc(norm_in, 16)
            pairs = U_END // 2
            for s in range(PAIRS):
                sp.dma_start(raw[:, s], io["weights"][s]).then_inc(raw_in[s], 16)
            for dst, name in ((cos, "cos"), (sin, "sin"), (causal, "causal"), (fill, "fill"), (imask, "imask"),
                              (tri, "tri"), (strict_incl, "strict_incl"), (chunk_sum, "chunk_sum"), (pair_mask, "pair_mask")):
                sp.dma_start(dst[:], io[name]).then_inc(const_in, 16)
            with sp.Fori(1, pairs // PAIRS) as i:
                for s in range(PAIRS):
                    sp.wait_ge(split_ready, 2 * PAIRS * i + 2 * s - 2 * PAIRS + 2)
                    sp.dma_start(raw[:, s], io["weights"][bass.ds(PAIRS * i + s, 1)].rearrange("o p n -> p (o n)"))\
                        .then_inc(raw_in[s], 16)
            for k in range(KT):
                sp.wait_ge(x_scaled, KT + k + 1)
                sp.dma_start(out[:, k], x[:, k]).then_inc(out_done, 16)
            sp.wait_ge(out_done, 16 * KT)

        @block.tensor
        def _(pe):
            def fm_unit(m, f, hi, lo, off=0, foff=0, k0=0, nk=KT, first=True, last=True, ready=None):
                bank = ps[:, f % 4]
                pe.wait_ge(split_ready, m + 1 + off)
                if first and f >= 4:
                    pe.wait_ge(bank_free, f - 3 + foff)
                for k in range(nk):
                    if ready is not None:
                        pe.wait_ge(ready[0], ready[1] + k + 1 + ready[2])
                    wh = w_hi[:, m % SPLITS, k * P:(k + 1) * P]
                    wl = w_lo[:, m % SPLITS, k * P:(k + 1) * P]
                    nc.tensor.matmul(bank, wh, hi[:, k0 + k], start=first and k == 0, stop=False)
                    nc.tensor.matmul(bank, wh, lo[:, k0 + k], start=False, stop=False)
                    mm = nc.tensor.matmul(bank, wl, hi[:, k0 + k], start=False, stop=last and k == nk - 1)
                mm.then_inc(unit_done, 1)

            def tm_unit(m, g, hi, lo, q, ready=None):
                pe.wait_ge(split_ready, m + 1)
                for k in (2 * q, 2 * q + 1):
                    if ready is not None:
                        pe.wait_ge(ready[0], ready[1] + k + 1)
                    wk = slice((k % 2) * T, (k % 2 + 1) * T)
                    for t in range(NT):
                        if k == 0 and g >= 2:
                            pe.wait_ge(tm_free, 4 * (g - 2) + t + 1)
                        bank = ps[:, 4 * (g % 2) + t]
                        at = slice(t * P, (t + 1) * P)
                        nc.tensor.matmul(bank, hi[:, k, at], w_hi[:, m % SPLITS, wk], start=k == 0, stop=False)
                        nc.tensor.matmul(bank, hi[:, k, at], w_lo[:, m % SPLITS, wk], start=False, stop=False)
                        mm = nc.tensor.matmul(bank, lo[:, k, at], w_hi[:, m % SPLITS, wk], start=False, stop=k == KT - 1)
                mm.then_inc(unit_done, 1)

            def norm_sum(n):
                pe.wait_ge(sq_added, 5 * n + 5)
                for i, sq in enumerate((sq_sum[:], ep[:, 2], ep[:, 3])):
                    if i:
                        pe.wait_ge(squared, KT * n + 6 + i)
                    for t in range(NT):
                        mm = nc.tensor.matmul(ps[:, 7, t:t + 1], sq[:, t * P:(t + 1) * P], ones[:, 0:1],
                                              start=i == 0 and t == 0, stop=i == 2 and t == NT - 1)
                mm.then_inc(summed, 1)
                pe.wait_ge(diag_ready, n + 1)
                nc.tensor.matmul(ps[:, 6], ones[:], rstd[:], start=True, stop=True).then_inc(spread, 1)

            def fm_two(m, f, ready, off=0, foff=0):
                for j in range(2):
                    pe.wait_ge(split_ready, m + j + 1 + off)
                    if f + j >= 4:
                        pe.wait_ge(bank_free, f + j - 3 + foff)
                for k in range(KT):
                    pe.wait_ge(a_ready, ready + k + 1)
                    for j in range(2):
                        bank = ps[:, (f + j) % 4]
                        wh = w_hi[:, (m + j) % SPLITS, k * P:(k + 1) * P]
                        wl = w_lo[:, (m + j) % SPLITS, k * P:(k + 1) * P]
                        nc.tensor.matmul(bank, wh, a_hi[:, k], start=k == 0, stop=False)
                        nc.tensor.matmul(bank, wh, a_lo[:, k], start=False, stop=False)
                        mm = nc.tensor.matmul(bank, wl, a_hi[:, k], start=False, stop=k == KT - 1)
                        if k == KT - 1:
                            mm.then_inc(unit_done, 1)

            def proj(u, f, ready, hi=a_hi, lo=a_lo):
                for j in range(N_PROJ):
                    fm_unit(u + j, f + j, hi, lo, ready=ready if j == 0 else None)

            def mlp(u, f, h, n):
                with pe.Fori(0, 4) as i:
                    off, hoff = 16 * i, 8 * i
                    fm_two(u, f, KT * n, off, off)
                    for j in range(2, 8):
                        fm_unit(u + j, f + j, a_hi, a_lo, off, off)
                    for j in range(8):
                        fm_unit(u + 8 + j, f + 8 + j, u_hi, u_lo, off, off,
                                ready=(u_ready, h, hoff) if j == 0 else None)

            def ffn(u, f, h, n):
                def chunk(size, u, f, h, off, hoff):
                    fm_two(u, f, KT * n, off, off)
                    for j in range(2, 2 * size):
                        fm_unit(u + j, f + j, a_hi, a_lo, off, off)
                    for j in range(8):
                        fm_unit(u + 2 * size + j, f + 2 * size + j, u_hi, u_lo, off, off, nk=size,
                                ready=(u_ready, h, hoff) if j == 0 else None)

                with pe.Fori(0, 2) as i:
                    chunk(8, u, f, h, 24 * i, 8 * i)
                chunk(6, u + 48, f + 48, h + 16, 0, 0)

            pe.wait_ge(norm_in, 16 * 3)
            norm_sum(0)
            fm_two(U_DSA, F_DSA, 0)
            for j in range(2, 16):
                fm_unit(U_DSA + j, F_DSA + j, a_hi, a_lo)
            fm_unit(U_DSA + 16, F_DSA + 16, a_hi, a_lo, nk=4, last=False)
            fm_unit(U_DSA + 17, F_DSA + 16, a_hi, a_lo, nk=4, k0=4, first=False)
            pe.wait_ge(const_in, 16 * 9)
            pe.wait_ge(bank_free, 12)
            for t in range(NT):
                for j in range(2):
                    tr = nc.tensor.transpose(ps[:, 4 + t // 2, (t % 2) * 256 + j * P:(t % 2) * 256 + (j + 1) * P],
                                             vT[:, j, t * P:(t + 1) * P], ident[:])
            tr.then_inc(vt_ps, 1)
            pe.wait_ge(kiwi_ready, 1)
            for t in range(NT):
                tr = nc.tensor.transpose(ps[:, 6, t * P:t * P + 72], kiwi[0:72, t * P:(t + 1) * P], ident[0:72, 0:72])
            tr.then_inc(vt_ps, 1)
            pe.wait_ge(roped, 16)
            pe.wait_ge(v_read, 2)
            pe.wait_ge(wi_read, 1)
            for i in range(24):
                qb, h = 1 + i // 8, i % 8
                n, e = (qb + 1) * P, 64 * (h % 2)
                if i >= 4:
                    pe.wait_ge(idx_relu, i - 3)
                nc.tensor.matmul(ps[:, 4 + i % 4, 0:n], qiT[e:e + 64, h // 2, qb * P:(qb + 1) * P],
                                 kid[e:e + 64, 0:n], start=True, stop=True).then_inc(idx_ps, 1)
            pe.wait_ge(idx_relu, 24)

            def logits(n):
                qb, h = n // 16, n % 16
                e = 64 * (h % 2)
                if n >= 2:
                    pe.wait_ge(lg_read, n - 1)
                nc.tensor.matmul(ps[:, 4 + n % 2, 0:(qb + 1) * P], qT[e:e + 64, h // 2, qb * P:(qb + 1) * P],
                                 kd[e:e + 64, h // 4, 0:(qb + 1) * P], start=True, stop=True).then_inc(lg_ps, 1)

            def turn(n):
                pe.wait_ge(prob_ready, n + 1)
                if n >= 2:
                    pe.wait_ge(probT_ready, n - 1)
                for b in range(n // 16 + 1):
                    tr = nc.tensor.transpose(ps[:, 6 + n % 2, b * P:(b + 1) * P], prob[:, n % 4, b * P:(b + 1) * P], ident[:])
                tr.then_inc(tr_ps, 1)

            def weigh(n):
                qb, h = n // 16, n % 16
                e = 64 * (h % 2)
                pe.wait_ge(probT_ready, n + 1)
                if n % 8 == 0 and n >= 16:
                    pe.wait_ge(o_ready, n // 8 - 1)
                o = ps[e:e + 64, (n // 8) % 2, (h % 8 // 2) * P:(h % 8 // 2 + 1) * P]
                for b in range(qb + 1):
                    mm = nc.tensor.matmul(o, v_tm[:, b, (h // 4) * 64:(h // 4 + 1) * 64],
                                          probT[:, n % 2, b * P:(b + 1) * P], start=b == 0, stop=b == qb)
                mm.then_inc(o_ps, 1)

            pe.wait_ge(bank_free, F_DSA_O)
            for n in range(67):
                if n < 64:
                    logits(n)
                if 2 <= n < 66:
                    turn(n - 2)
                if n >= 3:
                    weigh(n - 3)
            pe.wait_ge(o_ready, 8)
            proj(U_DSA_O, F_DSA_O, None)
            norm_sum(1)
            mlp(U_MLP0, F_MLP0, 0, 1)
            norm_sum(2)
            pe.wait_ge(bank_free, F_RWKV)
            for g in range(6):
                c = g // 2
                hi, lo = (u_hi, u_lo) if c % 2 else (a_hi, a_lo)
                for q in range(4):
                    tm_unit(U_RWKV + 4 * g + q, g, hi, lo, q, ready=(xs_ready, 8 * c) if g % 2 == 0 else None)
            pe.wait_ge(tm_free, 20)
            for j, c in enumerate((3, 4, 5, 5)):
                hi, lo = (u_hi, u_lo) if c % 2 else (a_hi, a_lo)
                fm_unit(U_RWKV + 24 + j, F_RWKV + j, hi, lo, ready=(xs_ready, 8 * c, 0) if j < 3 else None)
            pe.wait_ge(tm_free, 24)
            pe.wait_ge(lora_in, 16)
            for i in range(24):
                t, kind, half = i // 6, i % 6 // 2, i % 2
                if t == 0 and half == 0:
                    pe.wait_ge(lora_act, (1, 1, 3)[kind])
                    pe.wait_ge(bank_free, F_RWKV + (1, 2, 4)[kind])
                if i >= 4:
                    pe.wait_ge(lora_read, i - 3)
                cols, at = slice(half * T, half * T + T), slice(t * P, t * P + P)
                if kind < 2:
                    mm = nc.tensor.matmul(ps[:, 4 + i % 4], lora[0:65, kind, at], lora2[0:65, kind, cols], start=True, stop=True)
                else:
                    nc.tensor.matmul(ps[:, 4 + i % 4], lora[:, 2, at], lora2[:, 2, cols], start=True, stop=False)
                    mm = nc.tensor.matmul(ps[:, 4 + i % 4], lora[0:32, 3, at], lora2[0:32, 3, cols], start=False, stop=True)
                mm.then_inc(lora_ps, 1)
            pe.wait_ge(lora_read, 24)
            pe.wait_ge(bank_free, F_RWKV + 4)
            heads = [(e, p) for e in range(2) for p in range(2)]

            def quarter(e, p):
                return slice((2 * e + p) * P, (2 * e + p + 1) * P)

            def core_decay(r):
                pe.wait_ge(rin_f_in, 16 * r + 16)
                if later(r, 1):
                    pe.wait_ge(act_front, ACT_FRONT.value("bv", r - 1))
                sg = rin_f[:, 2]
                nc.tensor.matmul(ps[:, B_M2[0], 0:256], tri[:, 0], sg, start=True, stop=True)
                nc.tensor.matmul(ps[:, B_M2[0], 256:512], tri[:, 1], sg, start=True, stop=True).then_inc(pe_front, 1)
                for p in range(2):
                    mm = nc.tensor.matmul(ps[:, B_M2[1], 2 * p:2 * p + 2], sg[:, p * P:(p + 1) * P], chunk_sum[:, 0], start=True, stop=True)
                mm.then_inc(pe_front, 1)

            def core_turn_ar(r, b):
                pe.wait_ge(dve_front, DVE_FRONT.value("rho", r))
                for p in range(2):
                    for w, src in enumerate((al_t[:, b], front_t[:, RHO])):
                        tr = nc.tensor.transpose(ps[:, B_M2[0], (2 * p + w) * P:(2 * p + w + 1) * P], src[:, p * P:(p + 1) * P], ident[:])
                tr.then_inc(pe_front, 1)

            def core_turn_bk(r, b):
                pe.wait_ge(dve_front, DVE_FRONT.value("ka", r))
                pe.wait_ge(act_front, ACT_FRONT.value("pc", r))
                for w in range(2):
                    for p in range(2):
                        tr = nc.tensor.transpose(ps[:, B_M2[1], (2 * w + p) * P:(2 * w + p + 1) * P], be_ka[:, b, w, p * P:(p + 1) * P], ident[:])
                tr.then_inc(pe_front, 1)

            def core_m1(r, b):
                pe.wait_ge(act_front, ACT_FRONT.value("bk", r))
                if later(r, 2):
                    pe.wait_ge(dve_back, DVE_BACK.value("y", r - 2))
                for e, p in heads:
                    rows = slice(64 * e, 64 * e + 64)
                    mm = nc.tensor.matmul(ps[:, B_M1[e], 256 * p:256 * p + 256], bkT[rows, 0, p], arT[rows, b, p], start=True, stop=True)
                mm.then_inc(pe_front, 1)

            def core_m2(r, b):
                for e, p in heads:
                    rows = slice(64 * e, 64 * e + 64)
                    mm = nc.tensor.matmul(ps[:, B_M2[e], 256 * p:256 * p + 256], bkT[rows, 1, p], arT[rows, b, p], start=True, stop=True)
                mm.then_inc(pe_front, 1)

            def core_bv(r, b):
                pe.wait_ge(dve_front, DVE_FRONT.value("m2_1", r))
                for e, p in heads:
                    mm = nc.tensor.matmul(ps[:, B_M2[0], quarter(e, p)], m2[:, b, e, p, 0], rin_f[:, 4, p * P:(p + 1) * P], start=True, stop=True)
                mm.then_inc(pe_front, 1)

            def core_level(r, b, lv):
                if lv > 1:
                    pe.wait_ge(dve_inv, DVE_INV.value(f"t{lv - 1}", r))
                else:
                    pe.wait_ge(dve_front, DVE_FRONT.value("t0", r))
                if lv == 1 and later(r, 1):
                    pe.wait_ge(act_inv, ACT_INV.value("ta", r - 1))
                for e, p in heads:
                    mm = nc.tensor.matmul(ps[:, B_W, quarter(e, p)], m1[:, b, e, p, 0], Tm[:, b, 2 * e + p], start=True, stop=True)
                mm.then_inc(pe_inv, 1)

            def core_level_2(r, b, lv):
                pe.wait_ge(act_inv, ACT_INV.value(f"w{lv}", r))
                if lv > 1:
                    pe.wait_ge(dve_inv, DVE_INV.value(f"tt{lv - 1}", r))
                elif later(r, 1):
                    pe.wait_ge(dve_inv, DVE_INV.value("u0_1", r - 1))
                if lv < 5:
                    for e, p in heads:
                        mm = nc.tensor.matmul(ps[:, B_TW, quarter(e, p)], TT[:, b, 2 * e + p], Wm[:, 2 * e + p], start=True, stop=True)
                    mm.then_inc(pe_inv, 1)
                for e, p in heads:
                    mm = nc.tensor.matmul(ps[:, B_WT, quarter(e, p)], Wm[:, 2 * e + p], TT[:, b, 2 * e + p], start=True, stop=True)
                mm.then_inc(pe_inv, 1)

            def core_solved(r, b):
                pe.wait_ge(dve_inv, DVE_INV.value("tt5", r))
                pe.wait_ge(act_front, ACT_FRONT.value("bv", r))
                for e, p in heads:
                    mm = nc.tensor.matmul(ps[64 * e:64 * e + 64, B_W, P * p:P * p + P], al_t[:, b, P * p + 64 * e:P * p + 64 * e + 64],
                                          TT[:, b, 2 * e + p], start=True, stop=True)
                mm.then_inc(pe_inv, 1)
                for e, p in heads:
                    mm = nc.tensor.matmul(ps[:, B_TW, quarter(e, p)], TT[:, b, 2 * e + p], bv[:, b, 2 * e + p], start=True, stop=True)
                mm.then_inc(pe_inv, 1)

            def core_read_state(r, b, g, c, more):
                if c:
                    pe.wait_ge(dve_back, DVE_BACK.value("s1_c0", r))
                else:
                    pe.wait_ge(act_inv, ACT_INV.value("ta", r))
                    if more:
                        pe.wait_ge(dve_front, DVE_FRONT.value("m1_1", r + 1))
                rows = slice(64 * c, 64 * c + 64)
                for p in range(2):
                    mm = nc.tensor.matmul(ps[rows, B_UY, P * p:P * p + P], taT[:, p, rows], S[:, g, p], start=True, stop=True)
                mm.then_inc(pe_back, 1)
                for p in range(2):
                    mm = nc.tensor.matmul(ps[rows, B_UY, 256 + P * p:256 + P * p + P], arT[:, b, p, 1, rows], S[:, g, p], start=True, stop=True)
                mm.then_inc(pe_back, 1)

            def core_write_state(r, b, c):
                if c == 0:
                    pe.wait_ge(rin_b_in, 16 * r + 16)
                    if later(r, 1):
                        pe.wait_ge(dve_back, DVE_BACK.value("o_lo", r - 1))
                pe.wait_ge(dve_back, DVE_BACK.value(f"u_c{c}", r))
                rows = slice(64 * c, 64 * c + 64)
                for p in range(2):
                    cols, dst = slice(P * p, P * p + P), ps[:, B_S, 256 * c + P * p:256 * c + P * p + P]
                    nc.tensor.matmul(dst, be_ka[rows, b, 0, cols], U[rows, p], start=True, stop=False)
                    mm = nc.tensor.matmul(dst, be_ka[rows, b, 1, cols], rin_b[rows, 0, cols], start=False, stop=True)
                mm.then_inc(pe_back, 1)

            def core_yh_v(r, b):
                for i, (e, p) in enumerate(heads):
                    nc.tensor.matmul(ps[:, B_YH, quarter(e, p)], m2[:, b, e, p, 1], rin_b[:, 0, P * p:P * p + P], start=i == 0, stop=False)

            def core_yh_u(r, b):
                pe.wait_ge(dve_back, DVE_BACK.value("u_c1", r))
                for i, (e, p) in enumerate(heads):
                    mm = nc.tensor.matmul(ps[:, B_YH, quarter(e, p)], m1[:, b, e, p, 1], U[:, p], start=False, stop=i == 3)
                mm.then_inc(pe_back, 1)

            def core_out(r):
                pe.wait_ge(dve_back, DVE_BACK.value("o", r))
                for p in range(2):
                    tr = nc.tensor.transpose(ps[:, B_S, P * p:P * p + P], back_t[:, OUT, P * p:P * p + P], ident[:])
                tr.then_inc(pe_back, 1)

            def core_round(t, g, front=True, inv=True, back=True):
                n, b = GROUPS * t + g, g % 2
                r, q = n + 2, 1 - b
                if back:
                    core_read_state(n, b, g, 0, inv)
                if inv:
                    core_level(n + 1, q, 1)
                if back:
                    core_write_state(n, b, 0)
                if inv:
                    core_level_2(n + 1, q, 1)
                if back:
                    core_read_state(n, b, g, 1, inv)
                    core_yh_v(n, b)
                if inv:
                    core_level(n + 1, q, 2)
                if back:
                    core_write_state(n, b, 1)
                if inv:
                    core_level_2(n + 1, q, 2)
                if back:
                    core_yh_u(n, b)
                if inv:
                    core_level(n + 1, q, 3)
                if front:
                    core_decay(r)
                if inv:
                    core_level_2(n + 1, q, 3)
                    core_level(n + 1, q, 4)
                if front:
                    core_turn_ar(r, b)
                if inv:
                    core_level_2(n + 1, q, 4)
                if front:
                    core_turn_bk(r, b)
                if inv:
                    core_level(n + 1, q, 5)
                if front:
                    core_m1(r, b)
                    core_m2(r, b)
                if back:
                    core_out(n)
                if inv:
                    core_level_2(n + 1, q, 5)
                if front:
                    core_bv(r, b)
                if inv:
                    core_solved(n + 1, q)

            core_round(0, -2, inv=False, back=False)
            core_round(0, -1, back=False)
            pe.wait_ge(state_zero, 1)
            with pe.Fori(0, NT - 1) as t:
                for g in range(GROUPS):
                    core_round(t, g)
            for g in range(GROUPS):
                core_round(NT - 1, g, g < 2, g < 3)
            pe.wait_ge(dve_back, DVE_BACK.value("o_lo", ROUNDS - 1))
            proj(U_RWKV_O, F_RWKV_O, None)
            norm_sum(3)
            mlp(U_MLP1, F_MLP1, 32, 3 - 1)
            norm_sum(4)
            norm_sum(5)
            ffn(U_FFN1, F_FFN1, H_FFN1, 3)
            norm_sum(6)
            with pe.Fori(0, 2) as i:
                for j in range(12):
                    fm_unit(U_MIX + j, F_MIX + j, a_hi, a_lo, 12 * i, 12 * i, ready=(a_ready, KT * 4, 0) if j == 0 else None)
            pe.wait_ge(bank_free, F_MIX + 24)
            for g in range(6, 12):
                for q in range(4):
                    tm_unit(U_MIX + 24 + 4 * (g - 6) + q, g, a_hi, a_lo, q)
            pe.wait_ge(silu_ready, 4)
            fm_unit(U_MIX + 48, F_MIX + 24, a_hi, a_lo, nk=4, last=False)
            fm_unit(U_MIX + 49, F_MIX + 24, a_hi, a_lo, nk=4, k0=4, first=False)
            pe.wait_ge(silu_ready, 8)
            pe.wait_ge(gate_in, 16)
            pe.wait_ge(bank_free, F_MIX + 25)
            for t in range(NT):
                nc.tensor.matmul(ps[:, 4 + t], glr[0:33, t * P:(t + 1) * P], gate_up[0:33], start=True, stop=True).then_inc(la_ps, 1)
            for j in range(16):
                fm_unit(U_MIX + 50 + j, F_GATES + j, a_hi, a_lo)
            for j in range(8):
                fm_unit(U_MIX + 66 + j, F_GATES + 16 + j, u_hi, u_lo, ready=(u_ready, H_CONV, 0) if j == 0 else None)
            pe.wait_ge(bank_free, F_GLA_O)
            pe.wait_ge(la_ready, 4)
            def gla_decay(r, s):
                pe.wait_ge(gin_f_in[s], 8 * (r - s) + 16)
                if later(r, 1):
                    pe.wait_ge(act_gf, ACT_GF.value("chunk", r - 1))
                la = gin_f[:, s, 256:384]
                for w in range(3):
                    nc.tensor.matmul(ps[:, G_DECAY, w * P:(w + 1) * P], tri[:, 2 + w], la, start=True, stop=True)
                nc.tensor.matmul(ps[:, G_DECAY, 384:386], la, chunk_sum[:, 1], start=True, stop=True).then_inc(pe_gf, 1)

            def gla_turn(r, s):
                pe.wait_ge(dve_gf, DVE_GF.value("qi", r))
                if later(r, 1):
                    pe.wait_ge(act_gt, ACT_GT.value("gT", r - 1))
                for w in range(3):
                    tr = nc.tensor.transpose(ps[:, G_TURN, w * P:(w + 1) * P], gqk[:, s, w], ident[:])
                tr.then_inc(pe_gt, 1)

            def gla_scores(r, s):
                pe.wait_ge(act_gt, ACT_GT.value("gT", r))
                if later(r, 1):
                    pe.wait_ge(dve_gt, DVE_GT.value("mask", r - 1))
                nc.tensor.matmul(ps[:, G_SCORE, 0:P], gT[:, s, 1], gT[:, s, 0], start=True, stop=True).then_inc(pe_gt, 1)

            def gla_state(r, s, g):
                pe.wait_ge(gin_b_in[s], 8 * (r - s) + 16)
                pe.wait_ge(dve_gf, DVE_GF.value("ks", r))
                if later(r, 1):
                    pe.wait_ge(dve_gs, DVE_GS.value("st1", r - 1))
                for c in range(2):
                    rows = slice(64 * c, 64 * c + 64)
                    nc.tensor.matmul(ps[:, G_KV + c, 0:256], gks[rows, g], gin_b[rows, s, 0:256], start=True, stop=True).then_inc(pe_gs, 1)
                pe.wait_ge(dve_gt, DVE_GT.value("mask", r))
                gla_output(r, s, g, 0)

            def gla_output(r, s, g, c):
                if c:
                    pe.wait_ge(dve_gs, DVE_GS.value("st0", r))
                rows = slice(64 * c, 64 * c + 64)
                nc.tensor.matmul(ps[rows, G_OUT[s], 0:256], gT[:, s, 2, rows], St[:, g], start=True, stop=False)
                nc.tensor.matmul(ps[rows, G_OUT[s], 0:256], scT[:, s, rows], gin_b[:, s, 0:256], start=False, stop=True).then_inc(pe_gs, 1)

            def gla_turn_out(r):
                pe.wait_ge(dve_go, DVE_GO.value("out", r))
                for p in range(2):
                    tr = nc.tensor.transpose(ps[:, G_TURN_O, P * p:P * p + P], gout[:, P * p:P * p + P], ident[:])
                tr.then_inc(pe_go, 1)

            def gla_round(t, g, front, turn, state):
                n, s, z = GROUPS * t + g, g % 2, 1 - g % 2
                if front:
                    gla_decay(n + 3, z)
                if state:
                    gla_state(n + 1, z, (g + 1) % GROUPS)
                if turn:
                    gla_turn(n + 2, s)
                gla_turn_out(n)
                if state:
                    gla_output(n + 1, z, (g + 1) % GROUPS, 1)
                if turn:
                    gla_scores(n + 2, s)

            pe.wait_ge(st_zero, 1)
            for r in range(3):
                gla_decay(r, r % 2)
            for r in range(2):
                gla_turn(r, r)
                gla_scores(r, r)
            gla_state(0, 0, 0)
            gla_output(0, 0, 0, 1)
            with pe.Fori(0, NT - 1) as t:
                for g in range(GROUPS):
                    gla_round(t, g, True, True, True)
            for g in range(GROUPS):
                gla_round(NT - 1, g, g < 1, g < 2, g < 3)
            pe.wait_ge(dve_go, DVE_GO.value("o_lo", ROUNDS - 1))
            proj(U_GLA_O, F_GLA_O, None)
            proj(U_MIX_O, F_MIX_O, (u_ready, H_MERGED, 0), u_hi, u_lo)
            norm_sum(7)
            ffn(U_FFN2, F_FFN2, H_FFN2, 5)
            norm_sum(8)

        @block.scalar
        def _(act):
            def split_hi(m, off=0):
                if isinstance(off, int) and m + off >= U_END:
                    return
                act.wait_ge(raw_in[(m // 2) % 2], 16 * (m // 4 + 1) + 4 * off)
                if m >= SPLITS:
                    act.wait_ge(unit_done, m - 3 + off)
                nc.scalar.copy(w_hi[:, m % SPLITS], raw[:, (m // 2) % 2, (m % 2) * UNIT:(m % 2 + 1) * UNIT])\
                    .then_inc(hi_ready, 1)

            def square(n, k):
                if n == 0:
                    act.wait_ge(x_in[k // 4], 16)
                elif n == 5:
                    act.wait_ge(x_scaled, k + 1)
                else:
                    act.wait_ge(bank_free, F_OF_NORM[n] - KT + k + 1)
                if k >= 4:
                    act.wait_ge(sq_added, 5 * n + (1, 1, 2, 3)[k - 4])
                nc.scalar.activation(ep[:, k % 4], x[:, k], ACT.Square).then_inc(squared, 1)

            def last_square(n):
                if n == 0:
                    act.wait_ge(norm_in, 16 * 3)
                nc.scalar.activation(warm[:], ident[:, 0:1], ACT.Sqrt)
                square(n, KT - 1)
                act.wait_ge(summed, n + 1)
                nc.scalar.activation(root_t[:], ps[:, 7, 0:NT], ACT.Sqrt, bias=EPS, scale=1.0 / D).then_inc(rooted, 1)

            def proj(u, n):
                for j in range(N_PROJ):
                    split_hi(u + j + AHEAD)
                    if j:
                        square(n, j - 1)
                last_square(n)

            def norm_hi(na, u):
                if u:
                    act.wait_ge(unit_done, u)
                for k in range(KT):
                    act.wait_ge(normed, KT * na + k + 1)
                    nc.scalar.copy(a_hi[:, k], h32[:, k % 3]).then_inc(a_hi_ready, 1)

            def hidden_hi(m, f, j, off=0, foff=0):
                act.wait_ge(bank_free, f + 1 + foff)
                nc.scalar.copy(u_hi[:, j], ep[:, 2 + j % 2]).then_inc(u_hi_ready, 1)

            def mlp(u, f, n):
                def chunk(off, last):
                    for j in range(8):
                        split_hi(u + j + AHEAD, off)
                        act.wait_ge(unit_done, u + j + 1 + off)
                        nc.scalar.activation(ep[:, j % 2], ps[:, (f + j) % 4], ACT.Relu).then_inc(ep_act, 1)
                        hidden_hi(u + j, f + j, j, off, off)
                    for j in range(8):
                        split_hi(u + 8 + j + AHEAD, off)
                        if last and j:
                            square(n, j - 1)

                with act.Fori(0, 3) as i:
                    chunk(16 * i, False)
                chunk(48, True)
                last_square(n)

            def ffn(u, f, n):
                def chunk(size, u, f, off, last=False):
                    for q in range(0, 2 * size, 4):
                        for e in range(2):
                            split_hi(u + q + e + AHEAD, off)
                            act.wait_ge(unit_done, u + q + e + 1 + off)
                            nc.scalar.activation(ep[:, e], ps[:, (f + q + e) % 4], ACT.Sigmoid).then_inc(ep_act, 1)
                        for e in range(2):
                            split_hi(u + q + 2 + e + AHEAD, off)
                            hidden_hi(u + q + 2 + e, f + q + 2 + e, q // 2 + e, off, off)
                    for j in range(8):
                        split_hi(u + 2 * size + j + AHEAD, off)
                        if last and j:
                            square(n, j - 1)

                with act.Fori(0, 2) as i:
                    chunk(8, u, f, 24 * i)
                chunk(6, u + 48, f + 48, 0, True)
                last_square(n)

            for k in range(KT - 1):
                square(0, k)
            last_square(0)
            for m in range(AHEAD):
                split_hi(m)
            norm_hi(0, 0)

            def swap_halves(j, r, rows):
                act.wait_ge(unit_done, j + 1)
                if r >= 2:
                    act.wait_ge(roped, r - 1)
                for q in range(0, rows, 32):
                    nc.scalar.copy(swap[q ^ 32:(q ^ 32) + 32, r % 2], ps[q:q + 32, (F_DSA + j) % 4 if j < 16 else F_DSA % 4])\
                        .then_inc(swap_ready, 1)

            r = 0
            for j in range(16):
                split_hi(j + AHEAD)
                if j in (10, 11):
                    continue
                else:
                    swap_halves(j, r, P)
                    r += 1
            split_hi(16 + AHEAD)
            split_hi(17 + AHEAD)
            swap_halves(17, r, 64)
            for j in range(2):
                act.wait_ge(vt_ps, 1)
                nc.scalar.copy(v_tm[:, 2 * j:2 * j + 2], ps[:, 4 + j].rearrange("p (t n) -> p t n", t=2)).then_inc(v_read, 1)
            for i in range(24):
                n = (2 + i // 8) * P
                act.wait_ge(idx_ps, i + 1)
                if i >= 4:
                    act.wait_ge(idx_added, i - 3)
                nc.scalar.activation(ep[:, i % 4, 0:n], ps[:, 4 + i % 4, 0:n], ACT.Relu).then_inc(idx_relu, 1)

            def probs(n):
                w = (n // 16 + 1) * P
                act.wait_ge(lg_bias, n + 1)
                nc.scalar.activation(prob[:, n % 4, 0:w], prob[:, n % 4, 0:w], ACT.Exp, bias=stat[:, 1, n:n + 1],
                                     scale=0.125, accum_out=stat[:, 2, n:n + 1]).then_inc(exp_ready, 1)

            def turned(n):
                w = (n // 16 + 1) * P
                act.wait_ge(tr_ps, n + 1)
                if n >= 2:
                    act.wait_ge(o_ps, n - 1)
                nc.scalar.copy(probT[:, n % 2, 0:w], ps[:, 6 + n % 2, 0:w]).then_inc(probT_ready, 1)

            def out_hi(g):
                act.wait_ge(o_ps, 8 * g + 8)
                nc.scalar.copy(a_hi[:, 4 * (g % 2):4 * (g % 2) + 4, (g // 2) * P:(g // 2 + 1) * P],
                               ps[:, g % 2].rearrange("p (j t) -> p j t", j=4)).then_inc(o_hi, 1)

            for n in range(67):
                if n < 64:
                    probs(n)
                if 2 <= n < 66:
                    turned(n - 2)
                if n >= 11 and (n - 11) % 8 == 0:
                    out_hi((n - 11) // 8)
            out_hi(7)
            proj(U_DSA_O, 1)
            norm_hi(1, U_MLP0)
            mlp(U_MLP0, F_MLP0, 2)

            def mixed_hi(c, k):
                if k == 0:
                    act.wait_ge(unit_done, U_RWKV + (0, 0, 8, 16, 24, 25)[c])
                act.wait_ge(xs32, 8 * c + k + 1)
                nc.scalar.copy((u_hi if c % 2 else a_hi)[:, k], h32[:, (8 * c + k) % 3]).then_inc(xs_hi, 1)

            for k in range(KT):
                mixed_hi(0, k)
            for g in range(6):
                for q in range(4):
                    split_hi(U_RWKV + 4 * g + q + AHEAD)
                    mixed_hi(g // 2 + 1, (4 * g + q) % 8)
                act.wait_ge(unit_done, U_RWKV + 4 * g + 4)
                for t in range(NT):
                    if g:
                        act.wait_ge(spill[t], 16 * g)
                    nc.scalar.copy(ep[:, t], ps[:, 4 * (g % 2) + t]).then_inc(tm_free, 1)
            split_hi(U_RWKV + 24 + AHEAD)
            for k in range(KT):
                mixed_hi(4, k)
            split_hi(U_RWKV + 25 + AHEAD)
            for k in range(KT):
                mixed_hi(5, k)
            split_hi(U_RWKV + 26 + AHEAD)
            split_hi(U_RWKV + 27 + AHEAD)
            act.wait_ge(bank_free, F_RWKV + 1)
            nc.scalar.activation(lora[0:64, 0], lora[0:64, 0], ACT.Tanh).then_inc(lora_act, 1)
            act.wait_ge(bank_free, F_RWKV + 3)
            nc.scalar.activation(lora[:, 2], lora[:, 2], ACT.Sigmoid).then_inc(lora_act, 1)
            act.wait_ge(bank_free, F_RWKV + 4)
            nc.scalar.activation(lora[0:32, 3], lora[0:32, 3], ACT.Sigmoid).then_inc(lora_act, 1)
            for i in range(24):
                act.wait_ge(lora_ps, i + 1)
                act.wait_ge(spill[i % 4], 16 * (6 + i // 4))
                nc.scalar.activation(ep[:, i % 4], ps[:, 4 + i % 4], ACT.Sigmoid if i % 6 < 4 else ACT.Copy).then_inc(lora_read, 1)
            def core_exps(r, b):
                act.wait_ge(pe_front, PE_FRONT.value("decay", r))
                nc.scalar.activation(ex[:, 0], ps[:, B_M2[0], 0:256], ACT.Exp).then_inc(act_front, 1)
                nc.scalar.activation(ex[:, 1], ps[:, B_M2[0], 256:512], ACT.Exp).then_inc(act_front, 1)
                nc.scalar.activation(ex[:, 2], ps[:, B_M2[0], 0:256], ACT.Exp, scale=-1.0).then_inc(act_front, 1)
                act.wait_ge(pe_front, PE_FRONT.value("chunk_decay", r))
                if later(r, 2):
                    act.wait_ge(dve_back, DVE_BACK.value("s1_c1", r - 2))
                nc.scalar.activation(pc[:, b].rearrange("p a b -> p (a b)"), ps[:, B_M2[1], 0:4], ACT.Exp).then_inc(act_front, 1)

            def core_turned(r, b):
                act.wait_ge(pe_front, PE_FRONT.value("turn_ar", r))
                nc.scalar.copy(arT[:, b].rearrange("p a b c -> p (a b c)"), ps[:, B_M2[0]]).then_inc(act_front, 1)
                act.wait_ge(pe_front, PE_FRONT.value("turn_bk", r))
                nc.scalar.copy(bkT[:].rearrange("p a b c -> p (a b c)"), ps[:, B_M2[1]]).then_inc(act_front, 1)

            def core_bv(r, b):
                act.wait_ge(pe_front, PE_FRONT.value("bv", r))
                nc.scalar.copy(bv[:, b].rearrange("p a b -> p (a b)"), ps[:, B_M2[0]]).then_inc(act_front, 1)

            def core_level(r, lv):
                act.wait_ge(pe_inv, PE_INV.value(f"w{lv}", r))
                nc.scalar.copy(Wm[:].rearrange("p a b -> p (a b)"), ps[:, B_W]).then_inc(act_inv, 1)

            def core_ta(r):
                act.wait_ge(pe_inv, PE_INV.value("ta", r))
                nc.scalar.copy(taT[:].rearrange("p a b -> p (a b)"), ps[:, B_W, 0:256]).then_inc(act_inv, 1)

            def core_yh(r):
                act.wait_ge(pe_back, PE_BACK.value("yh", r))
                for e in range(2):
                    nc.scalar.copy(yh[:, :, e], ps[:, B_YH, 256 * e:256 * e + 256].rearrange("p (a b) -> p a b", a=2)[:, :, 64 * e:64 * e + 64])\
                        .then_inc(act_back, 1)

            def core_out(r, t, g):
                act.wait_ge(pe_back, PE_BACK.value("turn_o", r))
                cols = slice(P * t, P * t + P) if isinstance(t, int) else bass.ds(P * t, P)
                nc.scalar.copy(a_hi[:, 2 * g:2 * g + 2, cols], ps[:, B_S, 0:256].rearrange("p (a b) -> p a b", a=2)).then_inc(act_back, 1)

            def core_round(t, g, front=True, inv=True, back=True):
                n, b = GROUPS * t + g, g % 2
                if inv:
                    core_level(n + 1, 1)
                    core_level(n + 1, 2)
                if back:
                    core_yh(n)
                if inv:
                    core_level(n + 1, 3)
                if front:
                    core_exps(n + 2, b)
                if inv:
                    core_level(n + 1, 4)
                if front:
                    core_turned(n + 2, b)
                if inv:
                    core_level(n + 1, 5)
                if back:
                    core_out(n, t, g)
                if inv:
                    core_ta(n + 1)
                if front:
                    core_bv(n + 2, b)

            core_round(0, -2, inv=False, back=False)
            core_round(0, -1, back=False)
            with act.Fori(0, NT - 1) as t:
                for g in range(GROUPS):
                    core_round(t, g)
            for g in range(GROUPS):
                core_round(NT - 1, g, g < 2, g < 3)
            proj(U_RWKV_O, 3)
            norm_hi(2, U_MLP1)
            mlp(U_MLP1, F_MLP1, 4)
            for k in range(KT - 1):
                square(5, k)
            last_square(5)
            norm_hi(3, U_FFN1)
            ffn(U_FFN1, F_FFN1, 6)
            norm_hi(4, U_MIX)
            with act.Fori(0, 2) as i:
                for j in range(12):
                    split_hi(U_MIX + j + AHEAD, 12 * i)
                    if j % 6 >= 4:
                        tile = 2 * (j // 6) + j % 2
                        act.wait_ge(bank_free, F_MIX + j + 1 + 12 * i)
                        nc.scalar.copy(u_hi[:, bass.ds(4 * i + tile, 1)].rearrange("p o t -> p (o t)"), ep[:, 2 + j % 2]).then_inc(u_hi_ready, 1)
            for g in range(6, 12):
                for q in range(4):
                    split_hi(U_MIX + 4 * g + q + AHEAD)
                act.wait_ge(unit_done, U_MIX + 4 * g + 4)
                for t in range(NT):
                    if g > 6:
                        act.wait_ge(spill[t], 16 * (6 + g))
                    if g < 10:
                        nc.scalar.copy(ep[:, t], ps[:, 4 * (g % 2) + t]).then_inc(tm_free, 1)
                    else:
                        nc.scalar.activation(ep[:, t], ps[:, 4 * (g % 2) + t], ACT.Sigmoid).then_inc(tm_free, 1)
            split_hi(U_MIX + 48 + AHEAD)
            split_hi(U_MIX + 49 + AHEAD)
            for t in range(NT):
                act.wait_ge(la_ps, t + 1)
                act.wait_ge(spill[t], 16 * 18)
                nc.scalar.activation(ep[:, t], ps[:, 4 + t], ACT.Abs).then_inc(la_act, 1)
            for t in range(NT):
                act.wait_ge(la_act, t + 1)
                nc.scalar.activation(ep[:, t], ep[:, t], ACT.Exp, scale=-1.0).then_inc(la_act, 1)
            act.wait_ge(la_act, 8)
            for t in range(NT):
                nc.scalar.activation(ep[:, t], ep[:, t], ACT.Ln, bias=1.0).then_inc(la_act, 1)
            for j in range(16):
                split_hi(U_MIX + 50 + j + AHEAD)
                gate = (merged if j < 8 else sig_b)[:, j % 8]
                act.wait_ge(bank_free, F_GATES + j + 1)
                nc.scalar.activation(gate, gate, ACT.Sigmoid).then_inc(gated, 1)
            for j in range(8):
                split_hi(U_MIX + 66 + j + AHEAD)
            def gla_exps(r, g):
                act.wait_ge(pe_gf, PE_GF.value("decay", r))
                if later(r, 1):
                    act.wait_ge(dve_gf, DVE_GF.value("ks", r - 1))
                nc.scalar.activation(gex[:, 0:3].rearrange("p a b -> p (a b)"), ps[:, G_DECAY, 0:384], ACT.Exp).then_inc(act_gf, 1)
                nc.scalar.activation(gex[:, 3], ps[:, G_DECAY, 0:P], ACT.Exp, scale=-1.0).then_inc(act_gf, 1)
                nc.scalar.activation(gdc[:, g], ps[:, G_DECAY, 384:386], ACT.Exp).then_inc(act_gf, 1)

            def gla_turned(r, s):
                act.wait_ge(pe_gt, PE_GT.value("turn", r))
                nc.scalar.copy(gT[:, s].rearrange("p a b -> p (a b)"), ps[:, G_TURN, 0:384]).then_inc(act_gt, 1)

            def gla_square(r, s):
                act.wait_ge(pe_gs, PE_GS.value("o1", r))
                if later(r, 1):
                    act.wait_ge(act_gs, ACT_GS.value("osq", r - 1))
                nc.scalar.activation(gsq[:], ps[:, G_OUT[s], 0:256], ACT.Square, accum_out=gst[:, s, 0:1]).then_inc(act_gs, 1)

            def gla_out_hi(r, t, g):
                act.wait_ge(pe_go, PE_GO.value("turn_o", r))
                cols = slice(P * t, P * t + P) if isinstance(t, int) else bass.ds(P * t, P)
                nc.scalar.copy(a_hi[:, 2 * g:2 * g + 2, cols], ps[:, G_TURN_O, 0:256].rearrange("p (a b) -> p a b", a=2)).then_inc(act_go, 1)

            def gla_round(t, g, front, turn, state):
                n, s, z = GROUPS * t + g, g % 2, 1 - g % 2
                if front:
                    gla_exps(n + 3, (g + 3) % GROUPS)
                if turn:
                    gla_turned(n + 2, s)
                gla_out_hi(n, t, g)
                if state:
                    gla_square(n + 1, z)

            for r in range(3):
                gla_exps(r, r)
            for r in range(2):
                gla_turned(r, r)
            gla_square(0, 0)
            with act.Fori(0, NT - 1) as t:
                for g in range(GROUPS):
                    gla_round(t, g, True, True, True)
            for g in range(GROUPS):
                gla_round(NT - 1, g, g < 1, g < 2, g < 3)
            for j in range(8):
                split_hi(U_GLA_O + j + AHEAD)
                act.wait_ge(merged_ready, j + 1)
                nc.scalar.copy(u_hi[:, j], merged[:, j]).then_inc(u_hi_ready, 1)
            proj(U_MIX_O, 7)
            norm_hi(5, U_FFN2)
            ffn(U_FFN2, F_FFN2, 8)

        @block.vector
        def _(dve):
            chain = Tally(dve, dve_chain)

            def split_lo(m, off=0):
                if isinstance(off, int) and m + off >= U_END:
                    return
                dve.wait_ge(hi_ready, m + 1 + off)
                nc.vector.tensor_tensor(w_lo[:, m % SPLITS], raw[:, (m // 2) % 2, (m % 2) * UNIT:(m % 2 + 1) * UNIT],
                                        w_hi[:, m % SPLITS], ALU.subtract).then_inc(split_ready, 1)

            def add_square(n, k):
                dve.wait_ge(squared, KT * n + k + 1)
                if k > 1:
                    dve.wait_ge(sq_added, 5 * n + k - 1)
                nc.vector.tensor_tensor(sq_sum[:], ep[:, 0] if k == 1 else sq_sum[:], ep[:, k % 4], ALU.add).then_inc(sq_added, 1)

            def root(n):
                dve.wait_ge(rooted, n + 1)
                chain.mark(nc.vector.reciprocal(inv_t[:], root_t[:]))
                chain.wait()
                nc.vector.tensor_tensor(rstd[:].rearrange("p (t i) -> p t i", t=NT), bcast(ident[:], NT, P), over(inv_t[:], P), ALU.mult)\
                    .then_inc(diag_ready, 1)
                if n == 0:
                    split_lo(0)
                    split_lo(1)
                dve.wait_ge(spread, n + 1)

            def norm_lo(n, na, col):
                root(n)

                def low(k):
                    dve.wait_ge(a_hi_ready, KT * na + k + 1)
                    nc.vector.tensor_tensor(a_lo[:, k], h32[:, k % 3], a_hi[:, k], ALU.subtract).then_inc(a_ready, 1)

                for k in range(KT):
                    if k >= 3:
                        dve.wait_ge(a_ready, KT * na + k - 2)
                    nc.vector.scalar_tensor_tensor(h32[:, k % 3], x[:, k], vec[:, col, k:k + 1], ps[:, 6],
                                                   ALU.mult, ALU.mult).then_inc(normed, 1)
                    if k:
                        low(k - 1)
                low(KT - 1)

            def scale_x(n, col, count):
                root(n)
                for k in range(KT):
                    nc.vector.scalar_tensor_tensor(x[:, k], x[:, k], vec[:, col, k:k + 1], ps[:, 6], ALU.mult, ALU.mult)\
                        .then_inc(x_scaled, 1)
                    if n == 4 and k >= 3:
                        add_square(5, k - 2)
                dve.wait_ge(x_scaled, count)

            def add_x(m, f, j, off=0, foff=0, scale=None):
                dve.wait_ge(unit_done, m + 1 + off)
                if scale is None:
                    nc.vector.tensor_tensor(x[:, j], ps[:, f % 4], x[:, j], ALU.add).then_inc(bank_free, 1)
                else:
                    nc.vector.scalar_tensor_tensor(x[:, j], ps[:, f % 4], scale, x[:, j], ALU.mult, ALU.add)\
                        .then_inc(bank_free, 1)

            def hidden_lo(h, j, hoff=0):
                dve.wait_ge(u_hi_ready, h + j + 1 + hoff)
                nc.vector.tensor_tensor(u_lo[:, j], ep[:, 2 + j % 2], u_hi[:, j], ALU.subtract).then_inc(u_ready, 1)

            def proj(u, f, n):
                for j in range(N_PROJ):
                    split_lo(u + j + AHEAD)
                    add_x(u + j, f + j, j)
                    if j >= 3:
                        add_square(n, j - 2)

            def mlp(u, f, h, e, n):
                def chunk(off, hoff, last):
                    for j in range(8):
                        split_lo(u + j + AHEAD, off)
                        dve.wait_ge(ep_act, e + j + 1 + hoff)
                        nc.vector.tensor_tensor(ep[:, 2 + j % 2], ep[:, j % 2], ps[:, (f + j) % 4], ALU.mult)\
                            .then_inc(bank_free, 1)
                        hidden_lo(h, j, hoff)
                    for j in range(8):
                        split_lo(u + 8 + j + AHEAD, off)
                        add_x(u + 8 + j, f + 8 + j, j, off, off)
                        if last and j >= 3:
                            add_square(n, j - 2)

                with dve.Fori(0, 3) as i:
                    chunk(16 * i, 8 * i, False)
                chunk(48, 24, True)

            def ffn(u, f, h, e, n):
                def chunk(size, u, f, h, e, off, hoff, last=False):
                    for q in range(0, 2 * size, 4):
                        for s in range(2):
                            split_lo(u + q + s + AHEAD, off)
                            dve.wait_ge(ep_act, e + q // 2 + s + 1 + hoff)
                            if q:
                                dve.wait_ge(u_ready, h + q // 2 + s - 1 + hoff)
                            nc.vector.tensor_tensor(ep[:, 2 + s], ep[:, s], ps[:, (f + q + s) % 4], ALU.mult)\
                                .then_inc(bank_free, 1)
                        for s in range(2):
                            split_lo(u + q + 2 + s + AHEAD, off)
                            dve.wait_ge(unit_done, u + q + 3 + s + off)
                            dve.wait_ge(bank_free, f + q + s + 1 + off)
                            nc.vector.tensor_tensor(ep[:, 2 + s], ep[:, 2 + s], ps[:, (f + q + 2 + s) % 4], ALU.mult)\
                                .then_inc(bank_free, 1)
                            hidden_lo(h, q // 2 + s, hoff)
                    for j in range(8):
                        split_lo(u + 2 * size + j + AHEAD, off)
                        add_x(u + 2 * size + j, f + 2 * size + j, j, off, off, 0.5)
                        if last and j >= 3:
                            add_square(n, j - 2)

                with dve.Fori(0, 2) as i:
                    chunk(8, u, f, h, e, 24 * i, 8 * i)
                chunk(6, u + 48, f + 48, h + 16, e + 16, 0, 0, True)

            for k in range(1, 6):
                add_square(0, k)
            dve.wait_ge(norm_in, 16 * 3)
            norm_lo(0, 0, V_MIX0)
            split_lo(2)
            dve.wait_ge(const_in, 16 * 9)

            def rope(j, r, rows, swaps):
                dve.wait_ge(swap_ready, swaps)
                if r:
                    dve.wait_ge(roped, r)
                chain.mark(nc.vector.tensor_tensor(swap[0:rows, r % 2], swap[0:rows, r % 2], sin[0:rows], ALU.mult))
                if rows == 64:
                    nc.vector.tensor_copy(kiwi[0:72], ps[0:72, 0]).then_inc(kiwi_ready, 1)
                nc.vector.tensor_tensor(rope1[0:rows], ps[0:rows, j % 4], cos[0:rows], ALU.mult).then_inc(bank_free, 1)
                chain.wait()

            r = 0
            for j in range(16):
                split_lo(j + AHEAD)
                if j in (10, 11):
                    dve.wait_ge(unit_done, j + 1)
                    nc.vector.tensor_copy(vT[:, j - 10], ps[:, j % 4]).then_inc(bank_free, 1)
                    continue
                rope(j, r, P, 4 * (r + 1))
                dve.wait_ge(bank_free, j + 1)
                if j < 8 or j >= 12:
                    dst = qT[:, j] if j < 8 else qiT[:, j - 12]
                    nc.vector.tensor_tensor(dst, rope1[:], swap[:, r % 2], ALU.add).then_inc(roped, 1)
                else:
                    for s in range(2):
                        rows = slice(64 * s, 64 * s + 64)
                        chain.mark(nc.vector.tensor_tensor(kd[rows, 2 * (j - 8) + s], rope1[rows], swap[rows, r % 2], ALU.add))
                    chain.wait()
                    for s in range(2):
                        rows, other = slice(64 * s, 64 * s + 64), slice(64 - 64 * s, 128 - 64 * s)
                        cp = nc.vector.tensor_copy(kd[other, 2 * (j - 8) + s], kd[rows, 2 * (j - 8) + s])
                        if s == 0:
                            chain.mark(cp)
                        else:
                            cp.then_inc(roped, 1)
                    chain.wait()
                r += 1
            split_lo(16 + AHEAD)
            split_lo(17 + AHEAD)
            rope(16, r, 64, 4 * 14 + 2)
            dve.wait_ge(bank_free, 17)
            nc.vector.tensor_tensor(kid[0:64], rope1[0:64], swap[0:64, r % 2], ALU.add).then_inc(roped, 1)
            dve.wait_ge(roped, 15)
            nc.vector.tensor_copy(kid[64:128], kid[0:64]).then_inc(roped, 1)
            dve.wait_ge(vt_ps, 2)
            nc.vector.tensor_scalar(wi[:], ps[:, 6].rearrange("p (t n) -> p t n", t=4)[:, :, 64:72],
                                    float(512 ** -0.5), None, ALU.mult).then_inc(wi_read, 1)
            dve.wait_ge(wi_read, 1)
            chain.mark(nc.vector.tensor_copy(amask[:, 0, 0:P], causal[:]))
            for i in range(24):
                qb, h = 1 + i // 8, i % 8
                n = (qb + 1) * P
                dve.wait_ge(idx_relu, i + 1)
                if i:
                    dve.wait_ge(idx_added, i)
                score = amask[:, qb]
                if h == 0:
                    nc.vector.tensor_scalar(score[:, 0:n], ep[:, i % 4, 0:n], wi[:, qb, 0:1], None, ALU.mult).then_inc(idx_added, 1)
                else:
                    nc.vector.scalar_tensor_tensor(score[:, 0:n], ep[:, i % 4, 0:n], wi[:, qb, h:h + 1], score[:, 0:n],
                                                   ALU.mult, ALU.add).then_inc(idx_added, 1)
                if h < 7:
                    continue
                dve.wait_ge(idx_added, i + 1)
                chain.mark(nc.vector.copy_predicated(score[:, n - P:n], imask[:, 12], fill[:]))
                chain.wait()

            def top_max(n):
                chain.mark(nc.vector.max(top8[:], amask[:, n // 16 + 1, 0:(n // 16 + 2) * P]))

            def top_take(n):
                s = amask[:, n // 16 + 1, 0:(n // 16 + 2) * P]
                chain.wait()
                chain.mark(nc.vector.match_replace(s, top8[:], s, SCORE_TAKEN))
                if n % 16 == TOPK // 8 - 1:
                    chain.wait()
                    chain.mark(nc.vector.tensor_scalar(s, s, -3.2e38, NEG, ALU.is_gt, ALU.mult))
                chain.wait()

            def peak(n):
                w = (n // 16 + 1) * P
                dve.wait_ge(lg_ps, n + 1)
                if n >= 4:
                    dve.wait_ge(tr_ps, n - 3)
                nc.vector.tensor_tensor_reduce(prob[:, n % 4, 0:w], ps[:, 4 + n % 2, 0:w], amask[:, n // 16, 0:w], 1.0, -3.0e38,
                                               ALU.add, ALU.max, stat[:, 0, n:n + 1]).then_inc(lg_read, 1)
                dve.wait_ge(lg_read, n + 1)
                nc.vector.tensor_scalar(stat[:, 1, n:n + 1], stat[:, 0, n:n + 1], -0.125, None, ALU.mult).then_inc(lg_bias, 1)

            def normalise(n):
                w = (n // 16 + 1) * P
                dve.wait_ge(exp_ready, n + 1)
                chain.mark(nc.vector.reciprocal(stat[:, 3, n:n + 1], stat[:, 2, n:n + 1]))
                chain.wait()
                nc.vector.tensor_scalar(prob[:, n % 4, 0:w], prob[:, n % 4, 0:w], stat[:, 3, n:n + 1], None, ALU.mult)\
                    .then_inc(prob_ready, 1)

            def out_lo(g):
                dve.wait_ge(o_hi, g + 1)
                at = (slice(None), slice(4 * (g % 2), 4 * (g % 2) + 4), slice((g // 2) * P, (g // 2 + 1) * P))
                nc.vector.tensor_tensor(a_lo[at], ps[:, g % 2].rearrange("p (j t) -> p j t", j=4), a_hi[at], ALU.subtract)\
                    .then_inc(o_ready, 1)

            for n in range(66):
                if n < 64:
                    peak(n)
                if n < 48:
                    top_max(n)
                if 1 <= n < 65:
                    normalise(n - 1)
                if n < 48:
                    top_take(n)
                if n >= 12 and (n - 12) % 8 == 0:
                    out_lo((n - 12) // 8)
            out_lo(7)
            proj(U_DSA_O, F_DSA_O, 1)
            norm_lo(1, 1, V_MLP0)
            mlp(U_MLP0, F_MLP0, 0, 0, 2)
            dve.wait_ge(unit_done, U_RWKV)
            chain.mark(nc.vector.memset(h_pad[:, :, 0:2], 0.0))
            chain.mark(nc.vector.memset(lora[64:65, 0:2], 1.0))
            chain.mark(nc.vector.tensor_scalar(mu1[:], vec[:, V_MU:V_MU + 6], -1.0, 1.0, ALU.mult, ALU.add))
            root(2)

            def normed_tile(k):
                chain.mark(nc.vector.scalar_tensor_tensor(h_pad[:, k, 2:T + 2], x[:, k], vec[:, V_MIX1, k:k + 1], ps[:, 6], ALU.mult, ALU.mult))
                chain.wait()

            def mixed(c, k):
                i = 8 * c + k
                if i >= 3:
                    dve.wait_ge(xs_ready, i - 2)
                chain.mark(nc.vector.tensor_scalar(h32[:, (8 * c + k) % 3], h_pad[:, k, 2:T + 2], mu1[:, c, k:k + 1], None, ALU.mult))
                chain.wait()
                nc.vector.scalar_tensor_tensor(h32[:, (8 * c + k) % 3], h_pad[:, k, 1:T + 1], vec[:, V_MU + c, k:k + 1], h32[:, (8 * c + k) % 3],
                                               ALU.mult, ALU.add).then_inc(xs32, 1)

            def mixed_lo(c, k):
                dve.wait_ge(xs_hi, 8 * c + k + 1)
                nc.vector.tensor_tensor((u_lo if c % 2 else a_lo)[:, k], h32[:, (8 * c + k) % 3], (u_hi if c % 2 else a_hi)[:, k],
                                        ALU.subtract).then_inc(xs_ready, 1)

            def mixed_all(c):
                for k in range(KT):
                    if c == 0:
                        normed_tile(k)
                    mixed(c, k)
                    if k:
                        mixed_lo(c, k - 1)
                mixed_lo(c, KT - 1)

            mixed_all(0)
            for m in range(24):
                split_lo(U_RWKV + m + AHEAD)
                mixed(m // 8 + 1, m % 8)
                mixed_lo(m // 8 + 1, m % 8)
            split_lo(U_RWKV + 24 + AHEAD)
            mixed_all(4)
            dve.wait_ge(unit_done, U_RWKV + 25)
            nc.vector.tensor_copy(lora[0:64, 0], ps[0:64, F_RWKV % 4]).then_inc(bank_free, 1)
            split_lo(U_RWKV + 25 + AHEAD)
            mixed_all(5)
            for j, (rows, slot) in enumerate(((64, 1), (P, 2), (32, 3))):
                if j:
                    split_lo(U_RWKV + 25 + j + AHEAD)
                dve.wait_ge(unit_done, U_RWKV + 26 + j)
                nc.vector.tensor_copy(lora[0:rows, slot], ps[0:rows, (F_RWKV + 1 + j) % 4]).then_inc(bank_free, 1)
            for i in range(4):
                dve.wait_ge(spill[i], 16 * 12)
            nc.vector.memset(S[:], 0.0).then_inc(state_zero, 1)

            def predicated(cell, dst, mask, src):
                nc.vector.memset(gate[:, cell:cell + 1], 0.0)
                return nc.vector.copy_predicated(dst, mask, src)

            def tt(dst, a, b, op=ALU.mult):
                return nc.vector.tensor_tensor(dst, a, b, op)

            def stt(dst, a, sc, b, op0, op1):
                return nc.vector.scalar_tensor_tensor(dst, a, sc, b, op0, op1)

            def by_head(ap):
                return ap.rearrange("p (h d) -> p h d", h=4)

            F, B = [front_t[:, i] for i in range(8)], [back_t[:, i] for i in range(5)]
            r_, k_, _, a_, v_ = (rin_f[:, c] for c in range(5))

            def prm_(j, g):
                return prm[:, j, 256 * g:256 * g + 256]

            def own_front(name, r):
                dve.wait_ge(dve_front, DVE_FRONT.value(name, r))

            def core_keys(r, b, g):
                dve.wait_ge(rin_f_in, 16 * r + 16)
                tt(F[KKR], k_, prm_(0, g)).then_inc(dve_front, 1)
                own_front("kkr", r)
                tt(F[SQ], F[KKR], F[KKR]).then_inc(dve_front, 1)
                own_front("sq", r)
                nc.vector.tensor_reduce(hst[:, b, H_SS], by_head(F[SQ]), AX.X, ALU.add).then_inc(dve_front, 1)
                own_front("ss", r)
                nc.vector.tensor_scalar(hst[:, b, H_SSM], hst[:, b, H_SS], 1e-24, None, ALU.max).then_inc(dve_front, 1)

            def core_bonus(r, b, g):
                stt(F[TA], a_, -1.0, prm_(1, g), ALU.add, ALU.mult).then_inc(dve_front, 1)
                own_front("t", r)
                stt(F[KF], F[TA], 1.0, k_, ALU.add, ALU.mult).then_inc(dve_front, 1)
                own_front("kf", r)
                tt(F[RKF], r_, F[KF]).then_inc(dve_front, 1)
                own_front("rkf", r)
                tt(F[RKF], F[RKF], prm_(2, g)).then_inc(dve_front, 1)
                own_front("rkr", r)
                nc.vector.tensor_reduce(bs[:, g], by_head(F[RKF]), AX.X, ALU.add).then_inc(dve_front, 1)

            def core_scaled(r, b):
                dve.wait_ge(pool_front, POOL_FRONT.value("rn", r))
                tt(by_head(F[KK]), by_head(F[KKR]), over(hst[:, b, H_RN], 64)).then_inc(dve_front, 1)
                own_front("kk", r)
                tt(F[BB], F[KK], a_).then_inc(dve_front, 1)
                dve.wait_ge(act_front, ACT_FRONT.value("ex_neg", r))
                if later(r, 2):
                    dve.wait_ge(pe_inv, PE_INV.value("ta", r - 2))
                stt(al_t[:, b], F[KK], -1.0, ex[:, 1], ALU.mult, ALU.mult).then_inc(dve_front, 1)

            def core_scaled_2(r, b):
                tt(F[RHO], r_, ex[:, 0]).then_inc(dve_front, 1)
                own_front("b", r)
                tt(be_ka[:, b, 0], F[BB], ex[:, 2]).then_inc(dve_front, 1)
                tt(be_ka[:, b, 1], F[KF], ex[:, 2]).then_inc(dve_front, 1)

            both = strict_incl[:].rearrange("p (o a) b -> p o a b", o=1).to_broadcast([P, 2, 2, P])

            def core_masked(r, b, m, banks, name):
                dve.wait_ge(pe_front, PE_FRONT.value(name, r))
                for e in range(2):
                    tt(m[:, b, e], ps[:, banks[e]].rearrange("p (a b c) -> p a b c", a=2, b=2), both).then_inc(dve_front, 1)

            def core_start(r, b):
                dve.wait_ge(pool_front, POOL_FRONT.value("eye", r))
                own_front("m1_1", r)
                predicated(0, TT[:, b], bcast(imask[:, 6], 4, P), m1[:, b, :, :, 0].rearrange("p e q n -> p (e q) n")).then_inc(dve_front, 1)
                own_front("tt0", r)
                nc.vector.transpose(Tm[:, b], TT[:, b]).then_inc(dve_front, 1)

            def core_level(r, b, lv):
                if lv < 5:
                    dve.wait_ge(pe_inv, PE_INV.value(f"tw{lv}", r))
                    predicated(3 + lv, Tm[:, b], bcast(imask[:, lv], 4, P), ps[:, B_TW].rearrange("p (a b) -> p a b", a=4)).then_inc(dve_inv, 1)
                dve.wait_ge(pe_inv, PE_INV.value(f"wt{lv}", r))
                if lv == 1:
                    own_front("t0", r)
                else:
                    dve.wait_ge(dve_inv, DVE_INV.value(f"tt{lv - 1}", r))
                predicated(8 + lv, TT[:, b], bcast(imask[:, 6 + lv], 4, P), ps[:, B_WT].rearrange("p (a b) -> p a b", a=4)).then_inc(dve_inv, 1)

            def core_u0(r):
                dve.wait_ge(pe_inv, PE_INV.value("u0", r))
                for e in range(2):
                    nc.vector.tensor_copy(u0[:, :, e], ps[:, B_TW, 256 * e:256 * e + 256].rearrange("p (a b) -> p a b", a=2)[:, :, 64 * e:64 * e + 64])\
                        .then_inc(dve_inv, 1)

            def own_back(name, r):
                dve.wait_ge(dve_back, DVE_BACK.value(name, r))

            def core_u(r, c):
                rows = slice(64 * c, 64 * c + 64)
                if c == 0:
                    dve.wait_ge(dve_inv, DVE_INV.value("u0_1", r))
                dve.wait_ge(pe_back, PE_BACK.value(f"y_c{c}", r))
                tt(U[rows], ps[rows, B_UY, 0:256].rearrange("p (a b) -> p a b", a=2),
                   u0[rows].rearrange("p a b c -> p a (b c)"), ALU.add).then_inc(dve_back, 1)

            def core_state(r, b, g, c):
                dve.wait_ge(pe_back, PE_BACK.value(f"s_c{c}", r))
                own_back(f"u_c{c}", r)
                tt(S[:, g], ps[:, B_S, 256 * c:256 * c + 256].rearrange("p (a b) -> p a b", a=2), S[:, g], ALU.add).then_inc(dve_back, 1)
                own_back(f"sx_c{c}", r)
                for p in range(2):
                    stt(S[:, g, p], S[:, g, p], pc[:, b, p, c:c + 1], pair_mask[:], ALU.mult, ALU.mult).then_inc(dve_back, 1)
                own_back(f"s1_c{c}", r)

            def core_y(r, b):
                dve.wait_ge(act_back, ACT_BACK.value("yh1", r))
                tt(B[YY], ps[:, B_UY, 256:512], yh[:].rearrange("p a b c -> p (a b c)"), ALU.add).then_inc(dve_back, 1)
                own_back("y", r)
                nc.vector.tensor_reduce(hst[:, b, H_SM], by_head(B[YY]), AX.X, ALU.add).then_inc(dve_back, 1)
                own_back("sm", r)
                nc.vector.tensor_scalar(hst[:, b, H_MEAN], hst[:, b, H_SM], 1.0 / 64, None, ALU.mult).then_inc(dve_back, 1)

            def core_var(r, b):
                own_back("mean", r)
                tt(by_head(B[YC]), by_head(B[YY]), over(hst[:, b, H_MEAN], 64), ALU.subtract).then_inc(dve_back, 1)
                own_back("yc", r)
                tt(B[YSQ], B[YC], B[YC]).then_inc(dve_back, 1)
                own_back("ysq", r)
                nc.vector.tensor_reduce(hst[:, b, H_VS], by_head(B[YSQ]), AX.X, ALU.add).then_inc(dve_back, 1)
                own_back("vs", r)
                nc.vector.tensor_scalar(hst[:, b, H_VE], hst[:, b, H_VS], 1.0 / 64, LNX_EPS, ALU.mult, ALU.add).then_inc(dve_back, 1)

            def core_out(r, b, g):
                dve.wait_ge(pool_back, POOL_BACK.value("ri", r))
                tt(by_head(B[YC]), by_head(B[YC]), over(hst[:, b, H_RI], 64)).then_inc(dve_back, 1)
                own_back("yn", r)
                tt(B[YC], B[YC], prm_(3, g)).then_inc(dve_back, 1)
                own_back("yw", r)
                tt(B[YC], B[YC], prm_(4, g), ALU.add).then_inc(dve_back, 1)
                tt(by_head(B[BON]), by_head(rin_b[:, 0]), over(bs[:, g], 64)).then_inc(dve_back, 1)
                own_back("bonus", r)
                tt(B[YC], B[YC], B[BON], ALU.add).then_inc(dve_back, 1)
                own_back("yv", r)
                tt(B[OUT], B[YC], rin_b[:, 1]).then_inc(dve_back, 1)

            def core_out_lo(r, t, g):
                dve.wait_ge(act_back, ACT_BACK.value("o_hi", r))
                at = (slice(None), slice(2 * g, 2 * g + 2), slice(P * t, P * t + P) if isinstance(t, int) else bass.ds(P * t, P))
                tt(a_lo[at], ps[:, B_S, 0:256].rearrange("p (a b) -> p a b", a=2), a_hi[at], ALU.subtract).then_inc(dve_back, 1)

            def core_round(t, g, front=True, inv=True, back=True):
                n, b = GROUPS * t + g, g % 2
                r, q, g2 = n + 2, 1 - b, (g + 2) % GROUPS
                if back:
                    core_u(n, 0)
                    core_state(n, b, g, 0)
                if inv:
                    core_level(n + 1, q, 1)
                if back:
                    core_u(n, 1)
                if front:
                    core_keys(r, b, g2)
                if back:
                    core_state(n, b, g, 1)
                if inv:
                    core_level(n + 1, q, 2)
                if front:
                    core_bonus(r, b, g2)
                if back:
                    core_y(n, b)
                if front:
                    core_scaled(r, b)
                if inv:
                    core_level(n + 1, q, 3)
                if front:
                    core_scaled_2(r, b)
                if back:
                    core_var(n, b)
                if inv:
                    core_level(n + 1, q, 4)
                if back:
                    core_out(n, b, g)
                if front:
                    core_masked(r, b, m1, B_M1, "m1")
                    core_masked(r, b, m2, B_M2, "m2")
                if back:
                    core_out_lo(n, t, g)
                if inv:
                    core_level(n + 1, q, 5)
                if front:
                    core_start(r, b)
                if inv:
                    core_u0(n + 1)

            dve.wait_ge(prm_in[0], 16)
            core_round(0, -2, inv=False, back=False)
            for g in range(1, GROUPS):
                dve.wait_ge(prm_in[g], 16)
            core_round(0, -1, back=False)
            with dve.Fori(0, NT - 1) as t:
                for g in range(GROUPS):
                    core_round(t, g)
            for g in range(GROUPS):
                core_round(NT - 1, g, g < 2, g < 3)
            proj(U_RWKV_O, F_RWKV_O, 3)
            norm_lo(3, 2, V_MLP1)
            mlp(U_MLP1, F_MLP1, 32, 32, 4)
            scale_x(4, V_FINAL, KT)
            norm_lo(5, 3, V_FFN1)
            ffn(U_FFN1, F_FFN1, H_FFN1, 64, 6)
            dve.wait_ge(unit_done, U_MIX)
            chain.mark(nc.vector.memset(uc[:, :, 0:2], 0.0))
            norm_lo(6, 4, V_MIXG)
            with chain.loop(2, 4 * 3) as lp:
                with dve.Fori(0, 2) as i:
                    lp.at(i)
                    for jj in range(0, 12, 6):
                        def done(q):
                            dve.wait_ge(unit_done, U_MIX + jj + q + 1 + 12 * i)

                        for e in range(2):
                            split_lo(U_MIX + jj + e + AHEAD, 12 * i)
                            done(e)
                            dve.wait_ge(u_ready, H_CONV + 2 * (jj // 6) + e - 1 + 4 * i)
                            nc.vector.tensor_copy(ep[:, 2 + e], ps[:, (F_MIX + jj + e) % 4]).then_inc(bank_free, 1)
                        for e in range(2):
                            split_lo(U_MIX + jj + 2 + e + AHEAD, 12 * i)
                            done(2 + e)
                            dve.wait_ge(bank_free, F_MIX + jj + e + 1 + 12 * i)
                            nc.vector.tensor_tensor(uc[:, e, 2:T + 2], ep[:, 2 + e], ps[:, (F_MIX + jj + 2 + e) % 4], ALU.mult)\
                                .then_inc(bank_free, 1)
                            dve.wait_ge(bank_free, F_MIX + jj + 2 + e + 1 + 12 * i)
                            tile = 2 * (jj // 6) + e
                            for w in range(3):
                                tap = vec[:, V_CONV + w, bass.ds(4 * i + tile, 1)]
                                if w == 0:
                                    chain.mark(nc.vector.tensor_scalar(uc2[:, e], uc[:, e, 0:T], tap, None, ALU.mult))
                                else:
                                    chain.wait()
                                    chain.mark(nc.vector.scalar_tensor_tensor(uc2[:, e], uc[:, e, w:T + w], tap, uc2[:, e], ALU.mult, ALU.add))
                            chain.wait()
                        for e in range(2):
                            split_lo(U_MIX + jj + 4 + e + AHEAD, 12 * i)
                            done(4 + e)
                            nc.vector.tensor_tensor(ep[:, 2 + e], uc2[:, e], ps[:, (F_MIX + jj + 4 + e) % 4], ALU.mult).then_inc(bank_free, 1)
                            tile = 2 * (jj // 6) + e
                            dve.wait_ge(u_hi_ready, H_CONV + tile + 1 + 4 * i)
                            nc.vector.tensor_tensor(u_lo[:, bass.ds(4 * i + tile, 1)].rearrange("p o t -> p (o t)"), ep[:, 2 + e],
                                                    u_hi[:, bass.ds(4 * i + tile, 1)].rearrange("p o t -> p (o t)"), ALU.subtract).then_inc(u_ready, 1)
            for g in range(6, 12):
                for q in range(4):
                    split_lo(U_MIX + 4 * g + q + AHEAD)
                if g >= 10:
                    for t in range(NT):
                        dve.wait_ge(tm_free, 4 * g + t + 1)
                        nc.vector.tensor_tensor(ep[:, t], ep[:, t], ps[:, 4 * (g % 2) + t], ALU.mult).then_inc(silu_ready, 1)
            chain.mark(nc.vector.memset(glr[:], 0.0))
            chain.wait()
            chain.mark(nc.vector.memset(glr[32:33], 1.0))
            split_lo(U_MIX + 48 + AHEAD)
            split_lo(U_MIX + 49 + AHEAD)
            dve.wait_ge(unit_done, U_MIX + 50)
            chain.wait()
            nc.vector.tensor_copy(glr[0:16], ps[0:16, (F_MIX + 24) % 4]).then_inc(bank_free, 1)
            for t in range(NT):
                dve.wait_ge(la_act, 9 + t)
                nc.vector.scalar_tensor_tensor(ep[:, t], ps[:, 4 + t], 0.0, ep[:, t], ALU.min, ALU.subtract).then_inc(la_ready, 1)
            for j in range(16):
                split_lo(U_MIX + 50 + j + AHEAD)
                dve.wait_ge(unit_done, U_MIX + 51 + j)
                nc.vector.tensor_copy((merged if j < 8 else sig_b)[:, j % 8], ps[:, (F_GATES + j) % 4]).then_inc(bank_free, 1)
            for j in range(8):
                split_lo(U_MIX + 66 + j + AHEAD)
                dve.wait_ge(unit_done, U_MIX + 67 + j)
                dve.wait_ge(gated, j + 1)
                nc.vector.tensor_tensor(merged[:, j], merged[:, j], ps[:, (F_GATES + 16 + j) % 4], ALU.mult).then_inc(bank_free, 1)
            chain.mark(nc.vector.memset(scT[:], 0.0))
            chain.wait()
            nc.vector.memset(St[:], 0.0).then_inc(st_zero, 1)
            dve.wait_ge(st_zero, 1)

            def gla_scaled(r, s, g):
                dve.wait_ge(gin_f_in[s], 8 * (r - s) + 16)
                dve.wait_ge(act_gf, ACT_GF.value("ex_neg", r))
                if later(r, 2):
                    dve.wait_ge(pe_gt, PE_GT.value("turn", r - 2))
                q_, k_ = gin_f[:, s, 0:P], gin_f[:, s, P:2 * P]
                stt(gqk[:, s, 0], q_, GLA_SCALE, gex[:, 0], ALU.mult, ALU.mult).then_inc(dve_gf, 1)
                tt(gqk[:, s, 1], k_, gex[:, 3]).then_inc(dve_gf, 1)
                stt(gqk[:, s, 2], q_, GLA_SCALE, gex[:, 1], ALU.mult, ALU.mult).then_inc(dve_gf, 1)
                tt(gks[:, g], k_, gex[:, 2]).then_inc(dve_gf, 1)

            def gla_mask(r, s):
                dve.wait_ge(pe_gt, PE_GT.value("scores", r))
                if later(r, 2):
                    dve.wait_ge(pe_gs, PE_GS.value("o1", r - 2))
                predicated(14, scT[:, s], imask[:, 13], ps[:, G_SCORE, 0:P]).then_inc(dve_gt, 1)

            def gla_state(r, g, c):
                dve.wait_ge(pe_gs, PE_GS.value(f"o{c}", r))
                if c:
                    dve.wait_ge(dve_gs, DVE_GS.value("st0", r))
                else:
                    dve.wait_ge(act_gf, ACT_GF.value("chunk", r))
                stt(St[:, g], St[:, g], gdc[:, g, c:c + 1], ps[:, G_KV + c, 0:256], ALU.mult, ALU.add).then_inc(dve_gs, 1)

            def gla_mean(r, s):
                dve.wait_ge(act_gs, ACT_GS.value("osq", r))
                nc.vector.tensor_scalar(gst[:, s, 1:2], gst[:, s, 0:1], 1.0 / 256, EPS, ALU.mult, ALU.add).then_inc(dve_gs, 1)

            def gla_out(r, s, g):
                dve.wait_ge(pool_gs, POOL_GS.value("ri", r))
                stt(on[:], ps[:, G_OUT[s], 0:256], gst[:, s, 2:3], gla_g[:, 256 * g:256 * g + 256], ALU.mult, ALU.mult).then_inc(dve_go, 1)
                dve.wait_ge(dve_go, DVE_GO.value("on", r))
                tt(gout[:], on[:], gin_b[:, s, 256:512]).then_inc(dve_go, 1)

            def gla_out_lo(r, t, g):
                dve.wait_ge(act_go, ACT_GO.value("o_hi", r))
                at = (slice(None), slice(2 * g, 2 * g + 2), slice(P * t, P * t + P) if isinstance(t, int) else bass.ds(P * t, P))
                tt(a_lo[at], ps[:, G_TURN_O, 0:256].rearrange("p (a b) -> p a b", a=2), a_hi[at], ALU.subtract).then_inc(dve_go, 1)

            def gla_round(t, g, front, turn, state):
                n, s, z = GROUPS * t + g, g % 2, 1 - g % 2
                gla_out(n, s, g)
                if front:
                    gla_scaled(n + 3, z, (g + 3) % GROUPS)
                if state:
                    gla_state(n + 1, (g + 1) % GROUPS, 0)
                gla_out_lo(n, t, g)
                if state:
                    gla_state(n + 1, (g + 1) % GROUPS, 1)
                if turn:
                    gla_mask(n + 2, s)
                if state:
                    gla_mean(n + 1, z)

            for r in range(3):
                if r == 2:
                    gla_mask(0, 0)
                gla_scaled(r, r % 2, r)
            gla_mask(1, 1)
            for c in range(2):
                gla_state(0, 0, c)
            gla_mean(0, 0)
            dve.wait_ge(gla_in, 16)
            with dve.Fori(0, NT - 1) as t:
                for g in range(GROUPS):
                    gla_round(t, g, True, True, True)
            for g in range(GROUPS):
                gla_round(NT - 1, g, g < 1, g < 2, g < 3)
            dve.wait_ge(dve_go, DVE_GO.value("o_lo", ROUNDS - 1))
            for j in range(8):
                split_lo(U_GLA_O + j + AHEAD)
                dve.wait_ge(unit_done, U_GLA_O + j + 1)
                dve.wait_ge(gated, 9 + j)
                nc.vector.tensor_tensor(sig_b[:, j], sig_b[:, j], ps[:, (F_GLA_O + j) % 4], ALU.mult).then_inc(bank_free, 1)
                dve.wait_ge(bank_free, F_GLA_O + j + 1)
                nc.vector.tensor_tensor(merged[:, j], merged[:, j], sig_b[:, j], ALU.add).then_inc(merged_ready, 1)
                dve.wait_ge(u_hi_ready, H_MERGED + j + 1)
                nc.vector.tensor_tensor(u_lo[:, j], merged[:, j], u_hi[:, j], ALU.subtract).then_inc(u_ready, 1)
            proj(U_MIX_O, F_MIX_O, 7)
            norm_lo(7, 5, V_FFN2)
            ffn(U_FFN2, F_FFN2, H_FFN2, 86, 8)
            scale_x(8, V_OUT, 2 * KT)

        @block.gpsimd
        def _(pool):
            def spill_out(slot, c, t, half):
                pool.dma_start(rk_dram[t, 2 * half:2 * half + 2, :, c].rearrange("g p n -> p g n"),
                               ep[:, slot].rearrange("p (g n) -> p g n", g=2)).then_inc(spill[slot], 16)

            rounds = rk_dram.rearrange("t g p c n -> (t g) p (c n)")

            def fetch(r, columns, dst, sem_):
                src = rounds[r] if isinstance(r, int) else rounds[bass.ds(r, 1)].rearrange("o p n -> p (o n)")
                pool.dma_start(dst.rearrange("p c n -> p (c n)"), src[:, columns]).then_inc(sem_, 16)

            def fetch_prm(g):
                cols = slice(256 * g, 256 * g + 256)
                pool.dma_start(prm[:, :, cols], io["prm"].rearrange("(o j) n -> o j n", o=1)[:, :, cols].to_broadcast([P, 5, 256]))\
                    .then_inc(prm_in[g], 16)

            FRONT_COLS, BACK_COLS = slice(0, 5 * 256), slice(4 * 256, 6 * 256)

            pool.wait_ge(unit_done, U_RWKV)
            pool.dma_start(lora2[:], io["lora2"]).then_inc(lora_in, 16)
            for g in range(6):
                for t in range(NT):
                    pool.wait_ge(tm_free, 4 * g + t + 1)
                    spill_out(t, (0, 1, 4)[g // 2], t, g % 2)
            for i in range(24):
                if i == 16:
                    pool.wait_ge(unit_done, U_RWKV_O)
                    for slot in range(4):
                        pool.wait_ge(spill[slot], 16 * (8 if slot < 2 else 7))
                    fetch(0, FRONT_COLS, rin_f[:], rin_f_in)
                    fetch(0, BACK_COLS, rin_b[:], rin_b_in)
                    fetch_prm(0)
                pool.wait_ge(lora_read, i + 1)
                spill_out(i % 4, (2, 3, 5)[i % 6 // 2], i // 6, i % 2)
            for g in range(1, GROUPS):
                fetch_prm(g)
            pool.wait_ge(bank_free, F_RWKV + 4)
            nc.gpsimd.memset(h_half[:], -0.5).then_inc(pool_step, 1)
            for s in range(4):
                pool.wait_ge(spill[s], 16 * 12)
            pool.wait_ge(pool_step, 1)
            eye = bcast(ident[:], 4, P)

            def front_part(r, b):
                if later(r, 2):
                    pool.wait_ge(pe_inv, PE_INV.value("u0", r - 2))
                nc.gpsimd.tensor_tensor(TT[:, b], eye, eye, ALU.mult).then_inc(pool_front, 1)
                pool.wait_ge(dve_front, DVE_FRONT.value("ssm", r))
                nc.gpsimd.tensor_tensor(hst[:, b, H_RN], hst[:, b, H_SSM], h_half[:], ALU.pow).then_inc(pool_front, 1)

            def back_part(r, b):
                pool.wait_ge(dve_back, DVE_BACK.value("ve", r))
                nc.gpsimd.tensor_tensor(hst[:, b, H_RI], hst[:, b, H_VE], h_half[:], ALU.pow).then_inc(pool_back, 1)

            def next_front(r):
                pool.wait_ge(pe_front, PE_FRONT.value("bv", r - 1))
                fetch(r, FRONT_COLS, rin_f[:], rin_f_in)

            def next_back(r):
                pool.wait_ge(dve_back, DVE_BACK.value("o", r - 1))
                fetch(r, BACK_COLS, rin_b[:], rin_b_in)

            front_part(0, 0)
            next_front(1)
            front_part(1, 1)
            next_front(2)
            with pool.Fori(0, NT - 1) as t:
                for s in range(GROUPS):
                    n = GROUPS * t + s
                    front_part(n + 2, s % 2)
                    back_part(n, s % 2)
                    next_back(n + 1)
                    next_front(n + 3)
            for n in range(ROUNDS - GROUPS, ROUNDS):
                if n + 2 < ROUNDS:
                    front_part(n + 2, n % 2)
                back_part(n, n % 2)
                if n + 1 < ROUNDS:
                    next_back(n + 1)
                if n + 3 < ROUNDS:
                    next_front(n + 3)
            def spill_gla(slot, t, heads, cols):
                dst = gla_dram[t, heads, :, cols].rearrange("g p n -> p g n")
                n = dst.shape[1]
                pool.dma_start(dst, ep[:, slot].rearrange("p (g n) -> p g n", g=n)).then_inc(spill[slot], 16)

            pool.wait_ge(unit_done, U_MIX)
            pool.dma_start(gate_up[:], io["gate_up"]).then_inc(gate_in, 16)
            for g in range(6, 12):
                for t in range(NT):
                    if g < 10:
                        pool.wait_ge(tm_free, 4 * g + t + 1)
                    else:
                        pool.wait_ge(silu_ready, 4 * (g - 10) + t + 1)
                    if g < 8:
                        spill_gla(t, t, slice(0, 4), slice(P * (g - 6), P * (g - 5)))
                    else:
                        half = 2 * (g % 2)
                        spill_gla(t, t, slice(half, half + 2), slice(384, 640) if g < 10 else slice(640, 896))
            for t in range(NT):
                pool.wait_ge(la_ready, t + 1)
                spill_gla(t, t, slice(0, 4), slice(256, 384))
            for t in range(NT):
                pool.wait_ge(spill[t], 16 * 19)
            rounds = gla_dram.rearrange("t h p n -> (t h) p n")

            def fetch_gla(r, s, cols, dst, sems):
                src = rounds[r] if isinstance(r, int) else rounds[bass.ds(r, 1)].rearrange("o p n -> p (o n)")
                pool.dma_start(dst[:, s, 0:cols.stop - cols.start], src[:, cols]).then_inc(sems[s], 16)

            GLA_FRONT, GLA_BACK = slice(0, 384), slice(384, 896)
            for r in range(2):
                fetch_gla(r, r, GLA_FRONT, gin_f, gin_f_in)
            for r in range(2):
                fetch_gla(r, r, GLA_BACK, gin_b, gin_b_in)
            pool.wait_ge(unit_done, U_GLA_O)
            pool.dma_start(gla_g[:], io["gla_g"].to_broadcast([P, D])).then_inc(gla_in, 16)
            nc.gpsimd.memset(g_half[:], -0.5).then_inc(pool_gla_const, 1)
            pool.wait_ge(pool_gla_const, 1)

            def gla_root(r, s):
                pool.wait_ge(dve_gs, DVE_GS.value("mean", r))
                nc.gpsimd.tensor_tensor(gst[:, s, 2:3], gst[:, s, 1:2], g_half[:], ALU.pow).then_inc(pool_gs, 1)

            def next_front_gla(r, s):
                pool.wait_ge(dve_gf, DVE_GF.value("ks", r - 2))
                fetch_gla(r, s, GLA_FRONT, gin_f, gin_f_in)

            def next_back_gla(r, s):
                pool.wait_ge(dve_go, DVE_GO.value("out", r - 2))
                fetch_gla(r, s, GLA_BACK, gin_b, gin_b_in)

            for r in range(2, 4):
                next_front_gla(r, r % 2)
            gla_root(0, 0)
            with pool.Fori(0, NT - 1) as t:
                for g in range(GROUPS):
                    n, s, z = GROUPS * t + g, g % 2, 1 - g % 2
                    next_front_gla(n + 4, s)
                    next_back_gla(n + 2, s)
                    gla_root(n + 1, z)
            for g in range(GROUPS):
                n, s, z = ROUNDS - GROUPS + g, g % 2, 1 - g % 2
                if g < 2:
                    next_back_gla(n + 2, s)
                if g < 3:
                    gla_root(n + 1, z)


def constants():
    t = np.arange(T, dtype=np.float32)
    inv = (1.0 / (np.float32(10000.0) ** (np.arange(0, 64, 2, dtype=np.float32) / np.float32(64)))).astype(np.float32)
    ang = (inv[:, None] * t[None, :]).astype(np.float32)
    cos, sin = np.cos(ang), np.sin(ang)
    j, i = np.arange(P)[:, None], np.arange(P)[None, :]
    same = j // CHUNK == i // CHUNK
    upto, before = same & (j <= i), same & (j < i)
    ref = i // CHUNK * CHUNK + CHUNK // 2 - 1
    tri = np.stack([upto * -E_HALF, before * -E_HALF,
                    (upto * 1.0 - (same & (j <= ref))) / 16, upto / 16.0, (same & (j > i)) / 16.0, 0.0 * upto], 1)
    chunk = (np.arange(P)[:, None] // CHUNK == np.arange(2)[None, :]).astype(np.float32)
    levels = [((j // s) % 2 == 1) & ((i // s) % 2 == 0) & (j // (2 * s) == i // (2 * s)) for s in LEVELS]
    imask = np.stack(levels + [m.T for m in levels] + [i > j, upto], 1)
    out = dict(
        cos=np.tile(cos, (4, 1)), sin=np.concatenate([-sin, sin, -sin, sin]), ident=np.eye(P), ones=np.ones((P, P)),
        tri=tri, strict_incl=np.stack([before, upto], 1), chunk_sum=np.stack([chunk * -E_HALF, chunk / 16], 1),
        pair_mask=same, causal=np.where(i > j, NEG, 0.0), fill=np.full((P, P), SCORE_OUT),
    )
    out = {k: np.ascontiguousarray(v, np.float32) for k, v in out.items()}
    out["imask"] = np.ascontiguousarray(imask, np.int32)
    return out


def fm(w, col, rows=range(KT)):
    u = np.zeros((P, KT, P), np.float32)
    for n, k in enumerate(rows):
        part = w[k * P:(k + 1) * P, col:col + P]
        u[:, n, :part.shape[1]] = part
    return u.reshape(P, UNIT)


def tm(w, col):
    return [np.ascontiguousarray(w[2 * q * P:(2 * q + 2) * P, col:col + T].reshape(2, P, T).transpose(1, 0, 2)).reshape(P, UNIT)
            for q in range(4)]


def stream(a):
    s = []
    w = a["dsa_w_in"][0]
    s += [fm(w, P * j) for j in range(16)] + [fm(w, 2048, range(4)), fm(w, 2048, range(4, 8))]
    s += [fm(a["dsa_w_o"][0], P * j) for j in range(8)]

    def mlp(n):
        for c in range(4):
            yield from (fm(a["mlp_w_up"][n], D * c + P * j) for j in range(8))
            yield from (fm(a["mlp_w_down"][n], P * j, range(8 * c, 8 * c + 8)) for j in range(8))

    def ffn(gu, down):
        at = 0
        for size in FFN_CHUNKS:
            for j in range(at, at + size, 2):
                yield from (fm(gu, P * j), fm(gu, P * j + P), fm(gu, 2816 + P * j), fm(gu, 2816 + P * j + P))
            yield from (fm(down, P * j, range(at, at + size)) for j in range(8))
            at += size

    s += mlp(0)
    for c in range(3):
        s += tm(a["rwkv_w_rkv"][0, c], 0) + tm(a["rwkv_w_rkv"][0, c], 512)
    s += [fm(a["rwkv_w1"][0], 0), fm(a["rwkv_a1"][0], 0), fm(a["rwkv_g1"][0], 0), fm(a["rwkv_g1"][0], P)]
    s += [fm(a["rwkv_w_o"][0], P * j) for j in range(8)]
    s += mlp(1)
    s += ffn(a["ffn1_w_gu_2"][0], a["ffn1_w_down_2"][0])
    w = a["w_in_2"][0]
    for j in range(0, 8, 2):
        s += [fm(w, D * c + P * (j + e)) for c in (1, 2, 0) for e in (0, 1)]
    for col in (3072, 3584, 4096, 4608, 5136, 5648):
        s += tm(w, col)
    s += [fm(w[:, 5120:5136], 0, range(4)), fm(w[:, 5120:5136], 0, range(4, 8))]
    s += [fm(w, 6160 + P * j) for j in range(16)]
    for name in ("w_out_conv_2", "w_out_gla_2", "w_o_2"):
        s += [fm(a[name][0], P * j) for j in range(8)]
    s += ffn(a["ffn2_w_gu_2"][0], a["ffn2_w_down_2"][0])
    assert len(s) == U_END
    return np.stack(s).reshape(U_END // 2, 2, P, UNIT).transpose(0, 2, 1, 3).reshape(U_END // 2, P, 2 * UNIT)


def arrays_of(inputs):
    a = {k: np.asarray(v) for k, v in inputs.items()}
    v = [a["mixer_norm"], a["mlp_norm"], a["final_norm"][None], a["norm_ffn1_g_2"], a["norm_mix_g_2"], a["norm_ffn2_g_2"],
         a["final_norm_g_2"][None], a["rwkv_mu"][0], a["conv_w_2"][0]]
    vectors = np.concatenate(v).reshape(N_VEC, KT, P).transpose(2, 0, 1)
    g2 = np.zeros((2 * P, D), np.float32)
    g2[:160] = a["rwkv_g2"][0]
    lora2 = np.zeros((P, 4, D), np.float32)
    lora2[:64, 0], lora2[64, 0] = a["rwkv_w2"][0], a["rwkv_w0"][0]
    lora2[:64, 1], lora2[64, 1] = a["rwkv_a2"][0], a["rwkv_a0"][0]
    lora2[:, 2], lora2[:, 3] = g2[:P], g2[P:]
    gate_up = np.zeros((P, T), np.float32)
    gate_up[:16], gate_up[32] = a["gate_w_up_2"][0], a["gate_b_2"][0]
    out = constants()
    out.update(
        x=np.ascontiguousarray(a["x"][0].T.reshape(KT, P, T).transpose(1, 0, 2)), weights=stream(a), vec=vectors,
        lora2=lora2, gate_up=gate_up,
        prm=np.stack([a["rwkv_k_k"][0], a["rwkv_k_a"][0], a["rwkv_r_k"][0].reshape(D), a["rwkv_lnx_w"][0], a["rwkv_lnx_b"][0]]),
        gla_g=a["gla_norm_g_2"][0].reshape(1, D),
    )
    return {k: np.ascontiguousarray(v) for k, v in out.items()}


def kernel(**inputs):
    import concourse.bacc as bacc
    from concourse.bass_utils import run_bass_kernel_spmd

    nc = bacc.Bacc("TRN2", target_bir_lowering=False, num_devices=1)
    arrays = arrays_of(inputs)
    io = {k: nc.dram_tensor(k + "_dram", v.shape, mybir.dt.from_np(v.dtype), kind="ExternalInput").ap() for k, v in arrays.items()}
    out = nc.dram_tensor("out_dram", (P, KT, T), F32, kind="ExternalOutput").ap()
    build(nc, io, out)
    r = run_bass_kernel_spmd(nc, [{k + "_dram": v for k, v in arrays.items()}], core_ids=[0])
    got = r.results[0]["out_dram"]
    return got.transpose(2, 1, 0).reshape(1, T, D)
```
